# Optimizing a Trainium2 kernel written in Bass

```python
import math
import jax, jax.numpy as jnp
from jax import lax
import numpy as np

D_MODEL = 1024
BATCH = 1
SEQ = 512
DEPTH = 2

HEAD_DIM = 64
N_HEADS_MOBA = 8
N_HEADS_DIL = 8
N_HEADS_EVEN = N_HEADS_MOBA + N_HEADS_DIL
EVEN_WIDTH = N_HEADS_EVEN * HEAD_DIM
MOBA_BLOCK = 256
MOBA_TOPK = 3
MOBA_Q_CHUNK = 32
DIL_PAIRS = ((128, 1), (512, 4), (2048, 16))
N_HEADS_DIFF = 8
DIFF_HEAD_DIM = 64
DIFF_WIDTH = N_HEADS_DIFF * 2 * DIFF_HEAD_DIM
DIFF_Q_BLOCK = 128
DIFF_EPS = 1e-5
D_FF = 2816
CONV_WIDTH = 3
ROPE_THETA = 10000.0
NORM_EPS = 1e-6
N_EVEN = (DEPTH + 1) // 2
N_ODD = DEPTH // 2


f32 = jnp.float32

def rms_norm(x, g, eps=NORM_EPS):
    xf = x.astype(f32)
    y = xf * lax.rsqrt(jnp.mean(xf * xf, axis=-1, keepdims=True) + eps)
    return (y * g.astype(f32)).astype(x.dtype)

def rope(t):
    S, dim = t.shape[-2], t.shape[-1]
    half = dim // 2
    inv = 1.0 / (ROPE_THETA ** (jnp.arange(half, dtype=f32) * 2.0 / dim))
    ang = jnp.arange(S, dtype=f32)[:, None] * inv[None, :]
    cos, sin = jnp.cos(ang), jnp.sin(ang)
    tf = t.astype(f32)
    t1, t2 = tf[..., :half], tf[..., half:]
    return jnp.concatenate([t1 * cos - t2 * sin, t2 * cos + t1 * sin], axis=-1).astype(t.dtype)

def moba_attention(q, k, v):
    B, H, S, hd = q.shape
    nb = -(-S // MOBA_BLOCK)
    Sp = nb * MOBA_BLOCK
    pad = ((0, 0), (0, 0), (0, Sp - S), (0, 0))
    kb = jnp.pad(k, pad).reshape(B, H, nb, MOBA_BLOCK, hd)
    vb = jnp.pad(v, pad).reshape(B, H, nb, MOBA_BLOCK, hd)
    kmean = jnp.mean(kb.astype(f32), axis=3)
    n_sel = min(MOBA_TOPK, nb - 1)
    scale = hd ** -0.5
    n_chunks = S // MOBA_Q_CHUNK

    def chunk(c):
        q0 = c * MOBA_Q_CHUNK
        qc = lax.dynamic_slice_in_dim(q, q0, MOBA_Q_CHUNK, axis=2)
        blk = q0 // MOBA_BLOCK
        qpos = q0 + jnp.arange(MOBA_Q_CHUNK)
        own_k = lax.dynamic_index_in_dim(kb, blk, axis=2, keepdims=False)
        own_v = lax.dynamic_index_in_dim(vb, blk, axis=2, keepdims=False)
        kpos = blk * MOBA_BLOCK + jnp.arange(MOBA_BLOCK)
        s_own = jnp.einsum('bhqd,bhkd->bhqk', qc, own_k).astype(f32) * scale
        s_own = jnp.where(kpos[None, :] <= qpos[:, None], s_own, -jnp.inf)
        if n_sel == 0:
            p = jax.nn.softmax(s_own, axis=-1)
            return jnp.einsum('bhqk,bhkd->bhqd', p.astype(v.dtype), own_v)
        gate = jnp.einsum('bhqd,bhnd->bhqn', qc.astype(f32), kmean)
        gate = jnp.where(jnp.arange(nb) < blk, gate, -jnp.inf)
        _, idx = lax.top_k(gate, n_sel)
        valid = jnp.arange(n_sel) < blk
        take = jax.vmap(jax.vmap(lambda tb, ib: tb[ib]))
        sel_k = take(kb, idx)
        sel_v = take(vb, idx)
        s_sel = jnp.einsum('bhqd,bhqjkd->bhqjk', qc, sel_k).astype(f32) * scale
        s_sel = jnp.where(valid[:, None], s_sel, -jnp.inf)
        s_all = jnp.concatenate(
            [s_own, s_sel.reshape(B, H, MOBA_Q_CHUNK, n_sel * MOBA_BLOCK)], axis=-1)
        p = jax.nn.softmax(s_all, axis=-1).astype(v.dtype)
        p_own = p[..., :MOBA_BLOCK]
        p_sel = p[..., MOBA_BLOCK:].reshape(B, H, MOBA_Q_CHUNK, n_sel, MOBA_BLOCK)
        return (jnp.einsum('bhqk,bhkd->bhqd', p_own, own_v)
                + jnp.einsum('bhqjk,bhqjkd->bhqd', p_sel, sel_v))

    out = lax.map(chunk, jnp.arange(n_chunks))
    return out.transpose(1, 2, 0, 3, 4).reshape(B, H, S, hd)

def dilated_window_attention(q, k, v, window, dilation):
    B, H, S, hd = q.shape
    n = window // dilation
    L = S // dilation
    nblk = -(-L // n)
    Lp = nblk * n

    def to_residue(t):
        t = t.reshape(B, H, L, dilation, hd).transpose(0, 1, 3, 2, 4)
        return jnp.pad(t, ((0, 0), (0, 0), (0, 0), (0, Lp - L), (0, 0)))

    def band(t):
        own = t.reshape(B, H, dilation, nblk, n, hd)
        prev = jnp.pad(t, ((0, 0), (0, 0), (0, 0), (n, 0), (0, 0)))[..., :Lp, :]
        prev = prev.reshape(B, H, dilation, nblk, n, hd)
        return jnp.concatenate([prev, own], axis=-2)

    qb = to_residue(q).reshape(B, H, dilation, nblk, n, hd)
    kw = band(to_residue(k))
    vw = band(to_residue(v))
    s = jnp.einsum('bhrnqd,bhrnkd->bhrnqk', qb, kw).astype(f32) * (hd ** -0.5)
    i = jnp.arange(n)[:, None]
    j = jnp.arange(2 * n)[None, :]
    blk = jnp.arange(nblk)[:, None, None]
    dist = n + i - j
    kidx = (blk - 1) * n + j
    mask = (dist >= 0) & (dist <= n) & (kidx >= 0)
    s = jnp.where(mask, s, -jnp.inf)
    m = jnp.max(s, axis=-1, keepdims=True)
    p = jnp.exp(s - m)
    den = jnp.sum(p, axis=-1, keepdims=True)
    o = jnp.einsum('bhrnqk,bhrnkd->bhrnqd', (p / den).astype(v.dtype), vw)
    lse = (m + jnp.log(den))[..., 0]
    o = o.reshape(B, H, dilation, Lp, hd)[:, :, :, :L, :]
    o = o.transpose(0, 1, 3, 2, 4).reshape(B, H, S, hd)
    lse = lse.reshape(B, H, dilation, Lp)[:, :, :, :L].transpose(0, 1, 3, 2).reshape(B, H, S)
    return o, lse

def dilated_mixture(q, k, v):
    results = [dilated_window_attention(q, k, v, w, r) for (w, r) in DIL_PAIRS]
    outs = jnp.stack([o for (o, _) in results]).astype(f32)
    lses = jnp.stack([l for (_, l) in results])
    wts = jax.nn.softmax(lses, axis=0)
    return jnp.einsum('gbhs,gbhsd->bhsd', wts, outs).astype(q.dtype)

def even_mixer(h, w_in, w_out):
    B, S, _ = h.shape
    qkv = (h @ w_in).reshape(B, S, 3, N_HEADS_EVEN, HEAD_DIM).transpose(2, 0, 3, 1, 4)
    q, k, v = rope(qkv[0]), rope(qkv[1]), qkv[2]
    na = N_HEADS_MOBA
    a = moba_attention(q[:, :na], k[:, :na], v[:, :na])
    b = dilated_mixture(q[:, na:], k[:, na:], v[:, na:])
    o = jnp.concatenate([a, b], axis=1).transpose(0, 2, 1, 3).reshape(B, S, EVEN_WIDTH)
    return o @ w_out

def diff_attention(q, k, v, lam):
    B, H, _, S, d = q.shape
    nq = S // DIFF_Q_BLOCK
    scale = d ** -0.5
    qb = q.reshape(B, H, 2, nq, DIFF_Q_BLOCK, d).transpose(3, 0, 1, 2, 4, 5)
    kpos = jnp.arange(S)

    def block(args):
        qblk, bi = args
        qpos = bi * DIFF_Q_BLOCK + jnp.arange(DIFF_Q_BLOCK)
        s = jnp.einsum('bhcqd,bhckd->bhcqk', qblk, k).astype(f32) * scale
        s = jnp.where(kpos[None, :] <= qpos[:, None], s, -jnp.inf)
        p = jax.nn.softmax(s, axis=-1)
        a = p[:, :, 0] - lam * p[:, :, 1]
        return jnp.einsum('bhqk,bhkd->bhqd', a.astype(v.dtype), v)

    out = lax.map(block, (qb, jnp.arange(nq)))
    return out.transpose(1, 2, 0, 3, 4).reshape(B, H, S, 2 * d)

def diff_mixer(h, w_qkv, lq1, lk1, lq2, lk2, subln, w_out, lambda_init):
    B, S, _ = h.shape
    H, d = N_HEADS_DIFF, DIFF_HEAD_DIM
    qkv = h @ w_qkv
    q = qkv[..., :2 * H * d].reshape(B, S, H, 2, d).transpose(0, 2, 3, 1, 4)
    k = qkv[..., 2 * H * d:4 * H * d].reshape(B, S, H, 2, d).transpose(0, 2, 3, 1, 4)
    v = qkv[..., 4 * H * d:].reshape(B, S, H, 2 * d).transpose(0, 2, 1, 3)
    q, k = rope(q), rope(k)
    lam = (jnp.exp(jnp.sum(lq1.astype(f32) * lk1.astype(f32)))
           - jnp.exp(jnp.sum(lq2.astype(f32) * lk2.astype(f32))) + lambda_init)
    o = diff_attention(q, k, v, lam)
    o = rms_norm(o, subln, DIFF_EPS) * (1.0 - lambda_init)
    return o.transpose(0, 2, 1, 3).reshape(B, S, DIFF_WIDTH) @ w_out

def causal_depthwise_conv(u, w, b):
    C = u.shape[-1]
    y = lax.conv_general_dilated(
        u, w[:, None, :].astype(u.dtype), window_strides=(1,),
        padding=((CONV_WIDTH - 1, 0),), dimension_numbers=('NWC', 'WIO', 'NWC'),
        feature_group_count=C)
    return y + b

def conv_ffn(h, w_up, conv_w, conv_b, w_down):
    u = causal_depthwise_conv(h @ w_up, conv_w, conv_b)
    gate, val = u[..., :D_FF], u[..., D_FF:]
    return (jax.nn.silu(gate) * val) @ w_down

def first_inputs(seed: int = 0) -> dict:
    key = jax.random.key(seed)
    ks = jax.random.split(key, 18)

    def nrm(kk, shape, scale):
        return jax.random.normal(kk, shape, f32) * scale

    d = DIFF_HEAD_DIM
    return {
        'x': nrm(ks[0], (BATCH, SEQ, D_MODEL), 1.0),
        'even_norm': 1.0 + nrm(ks[1], (N_EVEN, D_MODEL), 0.1),
        'even_w_in': nrm(ks[2], (N_EVEN, D_MODEL, 3 * EVEN_WIDTH), D_MODEL ** -0.5),
        'even_w_out': nrm(ks[3], (N_EVEN, EVEN_WIDTH, D_MODEL), EVEN_WIDTH ** -0.5),
        'odd_norm': 1.0 + nrm(ks[4], (N_ODD, D_MODEL), 0.1),
        'odd_w_qkv': nrm(ks[5], (N_ODD, D_MODEL, 3 * DIFF_WIDTH), D_MODEL ** -0.5),
        'odd_lambda_q1': nrm(ks[6], (N_ODD, d), 0.1),
        'odd_lambda_k1': nrm(ks[7], (N_ODD, d), 0.1),
        'odd_lambda_q2': nrm(ks[8], (N_ODD, d), 0.1),
        'odd_lambda_k2': nrm(ks[9], (N_ODD, d), 0.1),
        'odd_subln': 1.0 + nrm(ks[10], (N_ODD, 2 * d), 0.1),
        'odd_w_out': nrm(ks[11], (N_ODD, DIFF_WIDTH, D_MODEL), DIFF_WIDTH ** -0.5),
        'ffn_norm': 1.0 + nrm(ks[12], (DEPTH, D_MODEL), 0.1),
        'ffn_w_up': nrm(ks[13], (DEPTH, D_MODEL, 2 * D_FF), D_MODEL ** -0.5),
        'ffn_conv_w': nrm(ks[14], (DEPTH, CONV_WIDTH, 2 * D_FF), CONV_WIDTH ** -0.5),
        'ffn_conv_b': nrm(ks[15], (DEPTH, 2 * D_FF), 0.02),
        'ffn_w_down': nrm(ks[16], (DEPTH, D_FF, D_MODEL), D_FF ** -0.5),
        'final_norm': 1.0 + nrm(ks[17], (D_MODEL,), 0.1),
    }

def first_block(x, even_norm, even_w_in, even_w_out, odd_norm, odd_w_qkv,
              odd_lambda_q1, odd_lambda_k1, odd_lambda_q2, odd_lambda_k2, odd_subln,
              odd_w_out, ffn_norm, ffn_w_up, ffn_conv_w, ffn_conv_b, ffn_w_down,
              final_norm):
    for layer in range(DEPTH):
        i = layer // 2
        if layer % 2 == 0:
            x = x + even_mixer(rms_norm(x, even_norm[i]), even_w_in[i], even_w_out[i])
        else:
            lambda_init = 0.8 - 0.6 * math.exp(-0.3 * layer)
            x = x + diff_mixer(rms_norm(x, odd_norm[i]), odd_w_qkv[i],
                               odd_lambda_q1[i], odd_lambda_k1[i],
                               odd_lambda_q2[i], odd_lambda_k2[i],
                               odd_subln[i], odd_w_out[i], lambda_init)
        x = x + conv_ffn(rms_norm(x, ffn_norm[layer]), ffn_w_up[layer],
                         ffn_conv_w[layer], ffn_conv_b[layer], ffn_w_down[layer])
    return rms_norm(x, final_norm)


RET_HEADS = 4
RET_QK_DIM = 128
RET_V_DIM = 256
MLSTM_HEADS = 4
MLSTM_QK_DIM = 128
MLSTM_V_DIM = 256
CONV_WIDTH_2 = 4
CHUNK = 128
D_FF_2 = -(-8 * D_MODEL // (3 * 256)) * 256
ROPE_BASE = 10000.0
NORM_EPS_2 = 1e-5
DEEPNORM_ALPHA = (2 * DEPTH) ** 0.25
DEEPNORM_BETA = (8 * DEPTH) ** -0.25

RET_QK = RET_HEADS * RET_QK_DIM
RET_V = RET_HEADS * RET_V_DIM
ML_QK = MLSTM_HEADS * MLSTM_QK_DIM
ML_V = MLSTM_HEADS * MLSTM_V_DIM
IN_SIZES = (RET_QK, RET_QK, RET_V, RET_V, 2 * ML_QK, ML_V, ML_V, MLSTM_HEADS, MLSTM_HEADS, D_MODEL, D_MODEL)
IN_BETA = (1.0, 1.0, DEEPNORM_BETA, 1.0, 1.0, DEEPNORM_BETA, 1.0, 1.0, 1.0, 1.0, 1.0)
IN_OFFSETS = tuple(int(o) for o in np.cumsum(IN_SIZES)[:-1])
D_IN = int(sum(IN_SIZES))


def _layer_norm(x, g, b):
    xf = x.astype(jnp.float32)
    mu = xf.mean(-1, keepdims=True)
    var = jnp.square(xf - mu).mean(-1, keepdims=True)
    return ((xf - mu) * lax.rsqrt(var + NORM_EPS_2) * g.astype(jnp.float32) + b.astype(jnp.float32)).astype(x.dtype)

def _head_norm(h, g):
    B, S, H, d = h.shape
    mu = h.mean(-1, keepdims=True)
    var = jnp.square(h - mu).mean(-1, keepdims=True)
    hn = ((h - mu) * lax.rsqrt(var + NORM_EPS_2)).reshape(B, S, H * d)
    return hn * g.astype(jnp.float32)

def _rotary(x, pos):
    half = x.shape[-1] // 2
    inv_freq = ROPE_BASE ** (-jnp.arange(half, dtype=jnp.float32) / half)
    ang = pos.astype(jnp.float32)[:, None] * inv_freq[None, :]
    cos = jnp.cos(ang)[None, :, None, :]
    sin = jnp.sin(ang)[None, :, None, :]
    x1, x2 = x[..., :half], x[..., half:]
    return jnp.concatenate([x1 * cos - x2 * sin, x1 * sin + x2 * cos], axis=-1)

def _causal_depthwise_conv(x, w, b):
    C = x.shape[-1]
    y = lax.conv_general_dilated(
        x, w[:, None, :].astype(x.dtype), window_strides=(1,), padding=[(CONV_WIDTH_2 - 1, 0)],
        dimension_numbers=('NWC', 'WIO', 'NWC'), feature_group_count=C)
    return y + b.astype(x.dtype)

def _retention(q, k, v):
    B, S, H, dk = q.shape
    dv = v.shape[-1]
    L = CHUNK
    N = S // L
    log_gamma = jnp.log(1.0 - jnp.power(2.0, -5.0 - jnp.arange(H, dtype=jnp.float32)))
    q = q.reshape(B, N, L, H, dk)
    k = k.reshape(B, N, L, H, dk)
    v = v.reshape(B, N, L, H, dv)
    idx = jnp.arange(L, dtype=jnp.float32)
    rel = idx[:, None] - idx[None, :]
    causal = rel >= 0
    decay = jnp.where(causal[None], jnp.exp(log_gamma[:, None, None] * jnp.where(causal, rel, 0.0)[None]), 0.0)
    scores = jnp.einsum('bnihd,bnjhd->bnhij', q, k) * decay[None, None]
    o_intra = jnp.einsum('bnhij,bnjhe->bnihe', scores, v)
    k_dec = k * jnp.exp(log_gamma[None, :] * (L - 1 - idx)[:, None])[None, None, :, :, None]
    kv = jnp.einsum('bnjhd,bnjhe->nbhde', k_dec, v)
    chunk_decay = jnp.exp(log_gamma * L)[None, :, None, None]

    def step(R, kv_n):
        return R * chunk_decay + kv_n, R

    _, R_prev = lax.scan(step, jnp.zeros((B, H, dk, dv), jnp.float32), kv)
    q_dec = q * jnp.exp(log_gamma[None, :] * (idx + 1.0)[:, None])[None, None, :, :, None]
    o_inter = jnp.einsum('bnihd,nbhde->bnihe', q_dec, R_prev)
    return (o_intra + o_inter).reshape(B, S, H, dv)

def _mlstm(q, k, v, i_pre, f_pre):
    B, S, H, dk = q.shape
    dv = v.shape[-1]
    L = CHUNK
    N = S // L
    k = k * (dk ** -0.5)
    q = q.reshape(B, N, L, H, dk)
    k = k.reshape(B, N, L, H, dk)
    v = v.reshape(B, N, L, H, dv)
    log_f = jax.nn.log_sigmoid(f_pre).reshape(B, N, L, H).transpose(0, 1, 3, 2)
    log_i = i_pre.reshape(B, N, L, H).transpose(0, 1, 3, 2)
    b = jnp.cumsum(log_f, axis=-1)
    b_end = b[..., -1]
    causal = jnp.tril(jnp.ones((L, L), dtype=bool))
    log_D = jnp.where(causal, b[..., :, None] - b[..., None, :] + log_i[..., None, :], -jnp.inf)
    log_w_end = b_end[..., None] - b + log_i
    m_loc = log_w_end.max(-1)
    w_end = jnp.exp(log_w_end - m_loc[..., None])
    kv = jnp.einsum('bnhs,bnshd,bnshe->nbhde', w_end, k, v)
    ksum = jnp.einsum('bnhs,bnshd->nbhd', w_end, k)

    def step(carry, inp):
        C, n, m = carry
        kv_n, ks_n, mloc_n, bend_n = inp
        m_new = jnp.maximum(bend_n + m, mloc_n)
        a = jnp.exp(bend_n + m - m_new)
        c = jnp.exp(mloc_n - m_new)
        C_new = a[..., None, None] * C + c[..., None, None] * kv_n
        n_new = a[..., None] * n + c[..., None] * ks_n
        return (C_new, n_new, m_new), (C, n, m)

    init = (jnp.zeros((B, H, dk, dv), jnp.float32), jnp.zeros((B, H, dk), jnp.float32), jnp.zeros((B, H), jnp.float32))
    _, (C_prev, n_prev, m_prev) = lax.scan(
        step, init, (kv, ksum, m_loc.transpose(1, 0, 2), b_end.transpose(1, 0, 2)))
    log_inter = b + m_prev.transpose(1, 0, 2)[..., None]
    m_row = jnp.maximum(log_D.max(-1), log_inter)
    D = jnp.exp(log_D - m_row[..., None])
    inter = jnp.exp(log_inter - m_row)
    qk = jnp.einsum('bnthd,bnshd->bnhts', q, k) * D
    num = (jnp.einsum('bnhts,bnshe->bnthe', qk, v)
           + jnp.einsum('bnthd,nbhde->bnthe', q, C_prev) * inter.transpose(0, 1, 3, 2)[..., None])
    den = qk.sum(-1) + jnp.einsum('bnthd,nbhd->bnht', q, n_prev) * inter
    denom = jnp.maximum(jnp.abs(den), jnp.exp(-m_row)).transpose(0, 1, 3, 2)[..., None]
    return (num / denom).reshape(B, S, H, dv)

def second_inputs(seed: int = 0) -> dict:
    key = jax.random.key(seed)
    ks = jax.random.split(key, 20)
    f32 = jnp.float32

    def nrm(k, shape, scale):
        return jax.random.normal(k, shape, f32) * scale

    x = nrm(ks[0], (BATCH, SEQ, D_MODEL), 1.0)
    col_scale = jnp.concatenate([jnp.full((n,), c, f32) for n, c in zip(IN_SIZES, IN_BETA)])
    w_in = nrm(ks[1], (DEPTH, D_MODEL, D_IN), D_MODEL ** -0.5) * col_scale
    b_if = jnp.concatenate([
        nrm(ks[2], (DEPTH, MLSTM_HEADS), 0.1),
        jnp.linspace(3.0, 6.0, MLSTM_HEADS, dtype=f32)[None, :] + nrm(ks[3], (DEPTH, MLSTM_HEADS), 0.1)], axis=-1)
    b_merge = nrm(ks[4], (DEPTH, 2 * D_MODEL), 0.02)
    conv_w = nrm(ks[5], (DEPTH, CONV_WIDTH_2, 2 * ML_QK), CONV_WIDTH_2 ** -0.5)
    conv_b = nrm(ks[6], (DEPTH, 2 * ML_QK), 0.02)
    ret_norm_g = 1.0 + nrm(ks[7], (DEPTH, RET_V), 0.02)
    mlstm_norm_g = 1.0 + nrm(ks[8], (DEPTH, ML_V), 0.02)
    w_proj_ret = nrm(ks[9], (DEPTH, RET_V, D_MODEL), RET_V ** -0.5 * DEEPNORM_BETA)
    w_proj_mlstm = nrm(ks[10], (DEPTH, ML_V, D_MODEL), ML_V ** -0.5 * DEEPNORM_BETA)
    w_out = nrm(ks[11], (DEPTH, D_MODEL, D_MODEL), D_MODEL ** -0.5 * DEEPNORM_BETA)
    ln1_g = 1.0 + nrm(ks[12], (DEPTH, D_MODEL), 0.02)
    ln1_b = nrm(ks[13], (DEPTH, D_MODEL), 0.02)
    w_gate_up = nrm(ks[14], (DEPTH, D_MODEL, 2 * D_FF_2), D_MODEL ** -0.5)
    w_down = nrm(ks[15], (DEPTH, D_FF_2, D_MODEL), D_FF_2 ** -0.5 * DEEPNORM_BETA)
    ln2_g = 1.0 + nrm(ks[16], (DEPTH, D_MODEL), 0.02)
    ln2_b = nrm(ks[17], (DEPTH, D_MODEL), 0.02)
    return {"x": x, "w_in": w_in, "b_if": b_if, "b_merge": b_merge, "conv_w": conv_w, "conv_b": conv_b,
            "ret_norm_g": ret_norm_g, "mlstm_norm_g": mlstm_norm_g, "w_proj_ret": w_proj_ret,
            "w_proj_mlstm": w_proj_mlstm, "w_out": w_out, "ln1_g": ln1_g, "ln1_b": ln1_b,
            "w_gate_up": w_gate_up, "w_down": w_down, "ln2_g": ln2_g, "ln2_b": ln2_b}

def second_block(x, w_in, b_if, b_merge, conv_w, conv_b, ret_norm_g, mlstm_norm_g, w_proj_ret,
              w_proj_mlstm, w_out, ln1_g, ln1_b, w_gate_up, w_down, ln2_g, ln2_b):
    B, S, _ = x.shape
    dt = x.dtype
    f32 = jnp.float32
    pos = jnp.arange(S, dtype=jnp.int32)
    for l in range(DEPTH):
        proj = x @ w_in[l]
        (r_q, r_k, r_v, r_g, m_qk, m_v, m_o, m_i, m_f, g_a, g_b) = jnp.split(proj, IN_OFFSETS, axis=-1)

        rq = _rotary(r_q.astype(f32).reshape(B, S, RET_HEADS, RET_QK_DIM), pos)
        rk = _rotary(r_k.astype(f32).reshape(B, S, RET_HEADS, RET_QK_DIM), pos) * (RET_QK_DIM ** -0.5)
        rv = r_v.astype(f32).reshape(B, S, RET_HEADS, RET_V_DIM)
        o_ret = _head_norm(_retention(rq, rk, rv), ret_norm_g[l]) * jax.nn.silu(r_g.astype(f32))
        y_ret = o_ret.astype(dt) @ w_proj_ret[l]

        qk_c = jax.nn.silu(_causal_depthwise_conv(m_qk, conv_w[l], conv_b[l])).astype(f32)
        mq = qk_c[..., :ML_QK].reshape(B, S, MLSTM_HEADS, MLSTM_QK_DIM)
        mk = qk_c[..., ML_QK:].reshape(B, S, MLSTM_HEADS, MLSTM_QK_DIM)
        mv = m_v.astype(f32).reshape(B, S, MLSTM_HEADS, MLSTM_V_DIM)
        i_pre = m_i.astype(f32) + b_if[l, :MLSTM_HEADS].astype(f32)
        f_pre = m_f.astype(f32) + b_if[l, MLSTM_HEADS:].astype(f32)
        o_ml = _head_norm(_mlstm(mq, mk, mv, i_pre, f_pre), mlstm_norm_g[l]) * jax.nn.sigmoid(m_o.astype(f32))
        y_ml = o_ml.astype(dt) @ w_proj_mlstm[l]

        gate_a = jax.nn.sigmoid(g_a + b_merge[l, :D_MODEL])
        gate_b = jax.nn.sigmoid(g_b + b_merge[l, D_MODEL:])
        mix = (gate_a * y_ret + gate_b * y_ml) @ w_out[l]
        x = _layer_norm(DEEPNORM_ALPHA * x + mix, ln1_g[l], ln1_b[l])

        gu = x @ w_gate_up[l]
        hidden = jax.nn.silu(gu[..., :D_FF_2]) * gu[..., D_FF_2:]
        x = _layer_norm(DEEPNORM_ALPHA * x + hidden @ w_down[l], ln2_g[l], ln2_b[l])
    return x


def setup_inputs(seed=0):
    out = dict(first_inputs(seed))
    for name, value in second_inputs(seed + 1).items():
        if name != "x":
            out[name + "_2"] = value
    return out


def reference(
    x, even_norm, even_w_in, even_w_out, odd_norm, odd_w_qkv, odd_lambda_q1, odd_lambda_k1,
    odd_lambda_q2, odd_lambda_k2, odd_subln, odd_w_out, ffn_norm, ffn_w_up, ffn_conv_w,
    ffn_conv_b, ffn_w_down, final_norm, w_in_2, b_if_2, b_merge_2, conv_w_2, conv_b_2,
    ret_norm_g_2, mlstm_norm_g_2, w_proj_ret_2, w_proj_mlstm_2, w_out_2, ln1_g_2, ln1_b_2,
    w_gate_up_2, w_down_2, ln2_g_2, ln2_b_2,
):
    x = first_block(
        x, even_norm, even_w_in, even_w_out, odd_norm, odd_w_qkv, odd_lambda_q1, odd_lambda_k1,
        odd_lambda_q2, odd_lambda_k2, odd_subln, odd_w_out, ffn_norm, ffn_w_up, ffn_conv_w,
        ffn_conv_b, ffn_w_down, final_norm,
    )
    return second_block(
        x, w_in_2, b_if_2, b_merge_2, conv_w_2, conv_b_2, ret_norm_g_2, mlstm_norm_g_2,
        w_proj_ret_2, w_proj_mlstm_2, w_out_2, ln1_g_2, ln1_b_2, w_gate_up_2, w_down_2, ln2_g_2,
        ln2_b_2,
    )


_drawn_inputs = setup_inputs


def setup_inputs(seed=0):
    import zlib

    import numpy as np

    out = dict(_drawn_inputs(seed))
    spreads = {}
    factors = {'odd_lambda_q1': 3.726,
     'odd_lambda_k2': 8.0,
     'b_merge_2': 8.0,
     'conv_b_2': 8.0,
     'ret_norm_g_2': 36.179,
     'mlstm_norm_g_2': 34.876}
    for name, (base, spread) in spreads.items():
        noise = np.random.default_rng([zlib.crc32(name.encode()), seed]).standard_normal(out[name].shape)
        drawn = base * np.exp(spread * noise) if base else spread * noise
        out[name] = __import__('jax').numpy.asarray(drawn.astype(out[name].dtype))
    for name, factor in factors.items():
        out[name] = (out[name] * factor).astype(out[name].dtype)
    return out
```

```python
import math
from contextlib import ExitStack

import numpy as np

import concourse.bass as bass
from concourse import mybir
from concourse.alu_op_type import AluOpType as ALU

F32 = mybir.dt.float32
F32R = mybir.dt.float32r
BF16 = mybir.dt.bfloat16
ACT = mybir.ActivationFunctionType
AX_X = mybir.AxisListType.X

P = 128
S = 512
D = 1024
DT = D // P
TB = S // P
D_FF = 2816
FT = D_FF // P
UNIT = 1024
BIG_NEG = -1e30
HD = 64
DK, DV, NH2 = 128, 256, 4
DEPTH = 2
ALPHA = (2 * DEPTH) ** 0.25
LAMBDA_INIT = 0.8 - 0.6 * math.exp(-0.3 * 1)
TRI = [sum((TB - j) * P for j in range(b)) for b in range(TB)]
TRQ = [sum((j + 1) * P for j in range(b)) for b in range(TB)]
TRI_N = TB * (TB + 1) // 2 * P


def columns(sizes):
    at, out = 0, {}
    for name, n in sizes:
        out[name] = (at, n)
        at += n
    return out, at


PARAMS, N_PARAMS = columns(
    [("even_norm", DT), ("odd_norm", DT), ("ffn_norm0", DT), ("ffn_norm1", DT), ("final_norm", DT), ("subln", 1)]
    + [(f"{n}{l}", c) for l in range(2) for n, c in (
        ("fconv_w", 3 * 2 * FT), ("fconv_b", 2 * FT))]
    + [("lambdas", 4 * HD)]
    + [(f"{n}{l}", c) for l in range(2) for n, c in (
        ("w_if", DT * 36), ("b_i", 1), ("b_f", 1), ("b_merge", 2 * DT), ("mconv_w", 4 * DT), ("mconv_b", DT),
        ("ret_g", DT), ("ml_g", DT), ("ln1_g", DT), ("ln1_b", DT), ("ln2_g", DT), ("ln2_b", DT))]
)
TABLES, N_TABLES = columns([
    ("masks", 15 * P),
    ("ident", P), ("ones", P), ("eps", 2),
    ("rope64", 2 * S), ("rope128", 2 * S), ("decay", NH2 * S), ("select", NH2 * P),
])


def weight_units():
    out = []

    def fm(name, layer, k, c0, c1):
        for c in range(c0, c1, 256):
            for k0 in range(0, k // P, 4):
                out.append((name, layer, k0, min(4, k // P - k0), c, 256))

    def tm(name, layer, k, c0, c1):
        for c in range(c0, c1, 512):
            for k0 in range(0, k // P, 2):
                out.append((name, layer, k0, 2, c, 512))

    def ffn(layer):
        for c in range(0, D_FF, 256):
            fm("ffn_w_up", layer, D, c, c + 256)
            fm("ffn_w_up", layer, D, D_FF + c, D_FF + c + 256)
        fm("ffn_w_down", layer, D_FF, 0, D)

    fm("even_w_in", 0, D, 0, 2 * D)
    tm("even_w_in", 0, D, 2 * D, 3 * D)
    fm("even_w_out", 0, D, 0, D)
    ffn(0)
    fm("odd_w_qkv", 0, D, 0, 2 * D)
    tm("odd_w_qkv", 0, D, 2 * D, 3 * D)
    fm("odd_w_out", 0, D, 0, D)
    ffn(1)
    for l in range(2):
        rq, rv, rg, mqk, mv, mo, ga, gb = 0, 1024, 2048, 3072, 4096, 5120, 6152, 7176
        fm("w_in_2", l, D, rq, rq + 1024)
        tm("w_in_2", l, D, rv, rv + 1024)
        fm("w_in_2", l, D, mqk, mqk + 1024)
        tm("w_in_2", l, D, mv, mv + 1024)
        fm("w_in_2", l, D, rg, rg + 1024)
        for c in range(0, D, 256):
            fm("w_in_2", l, D, ga + c, ga + c + 256)
            fm("w_proj_ret_2", l, D, c, c + 256)
        fm("w_in_2", l, D, mo, mo + 1024)
        for c in range(0, D, 256):
            fm("w_in_2", l, D, gb + c, gb + c + 256)
            fm("w_proj_mlstm_2", l, D, c, c + 256)
        fm("w_out_2", l, D, 0, D)
        for c in range(0, D_FF, 256):
            fm("w_gate_up_2", l, D, c, c + 256)
            fm("w_gate_up_2", l, D, D_FF + c, D_FF + c + 256)
        fm("w_down_2", l, D_FF, 0, D)
    return out


class Queue:

    def __init__(self, sem, engine):
        self.sem, self.engine, self.count, self.passed = sem, engine, 0, {}

    def wait(self, *marks):
        for m in marks:
            if isinstance(m, list):
                self.wait(*m)
            elif m is not None and self.passed.get(m[0].name, 0) < m[1]:
                self.passed[m[0].name] = m[1]
                if self.engine is not None:
                    self.engine.wait_ge(m[0], m[1])

    def do(self, make, *marks, signal=True):
        self.wait(*marks)
        instruction = make(self.engine) if self.engine is not None else None
        if not signal:
            return None
        self.count += 1
        if instruction is not None:
            instruction.then_inc(self.sem, 1)
        return (self.sem, self.count)

    def last(self):
        return (self.sem, self.count) if self.count else None


class Loads:

    def __init__(self, queue, sem):
        self.queue, self.sem, self.count = queue, sem, 0

    def start(self, out, in_, *marks):
        self.queue.wait(*marks)
        self.count += 16
        if self.queue.engine is not None:
            self.queue.engine.dma_start(out, in_).then_inc(self.sem, 16)
        return (self.sem, self.count)


def build(nc, weights, params, tables, x_in, y_out):
    with ExitStack() as ctx:
        banks = [ctx.enter_context(nc.psum_tensor(f"bank{i}", [P, S], F32)) for i in range(8)]
        sems, tensors = {}, {}

        def sem(name):
            if name not in sems:
                sems[name] = ctx.enter_context(nc.semaphore(name))
            return sems[name]

        def at(name, shape, dt, offset):
            if name not in tensors:
                tensors[name] = nc.alloc_sbuf_tensor_at(name, shape, dt, offset=offset)
            return tensors[name]

        def walk(engine, name):
            program(nc, {name: engine}, sem, at, banks, weights, params, tables, x_in, y_out)

        for name in ("pe_done", "act_done", "dve_done"):
            sem(name)
        with nc.Block() as block:
            block.sync(lambda e: walk(e, "sp"))
            block.scalar(lambda e: walk(e, "act"))
            block.vector(lambda e: walk(e, "dve"))
            block.gpsimd(lambda e: walk(e, "pool"))
            block.tensor(lambda e: walk(e, "pe"))


def program(nc, walked, sem, at, bank, weights, params, tables, x_in, y_out):
    units = weight_units()
    pe, act, dve, sp, pool = (Queue(sem(n + "_done"), walked.get(n)) for n in ("pe", "act", "dve", "sp", "pool"))

    K = 1024
    base = -(-nc.sbuf_base // 64) * 64
    at_x = base
    at_h = at_x + 16 * K
    at_big = at_h + 32 * K
    at_scr = at_big + 88 * K
    at_ring = at_big + 96 * K
    at_misc = at_ring + 44 * K
    RAW, HL = 3, 4
    misc = [at_misc]

    def small(name, cols, dt=F32):
        t = at(name, [P, cols], dt, misc[0])
        misc[0] += -(-cols * (2 if dt == BF16 else 4) // 32) * 32
        assert misc[0] <= nc.sbuf_usable_end
        return t

    x = at("x_resid", [P, DT, S], F32, at_x)
    h_hi = at("h_hi", [P, DT, S], F32R, at_h)
    h_lo = at("h_lo", [P, DT, S], F32R, at_h + 16 * K)
    raw = [at(f"w_raw{i}", [P, UNIT], F32, at_ring + 4 * K * i) for i in range(RAW)]
    w_hi = [at(f"w_hi{i}", [P, UNIT], F32R, at_ring + 4 * K * (RAW + i)) for i in range(HL)]
    w_lo = [at(f"w_lo{i}", [P, UNIT], F32R, at_ring + 4 * K * (RAW + HL + i)) for i in range(HL)]
    scr = [at(f"scratch{i}", [P, S], F32, at_scr + 2 * K * i) for i in range(4)]
    par = small("params_sb", N_PARAMS)
    ident = small("ident", P)
    ones = small("ones", P)
    eps = small("eps", 2)
    masks = small("masks_bf16", 15 * P, BF16)
    stats = small("stats", 256)
    scr += [small(f"scratch{4 + i}", S) for i in range(2)]

    def p_(name, i=0, n=1):
        return par[:, PARAMS[name][0] + i:PARAMS[name][0] + i + n]

    bank_free = [None] * 8
    scr_free = [None] * 6

    f32 = lambda ap: ap.bitcast(F32)

    first = Loads(pool, sem("constants_in"))
    table_ap = lambda name: tables[:, TABLES[name][0]:sum(TABLES[name])]
    masks_f32 = at("masks_f32", [P, 15 * P], F32, at_big)
    x_loads = Loads(sp, sem("x_in_sem"))
    x_landed = x_loads.start(x[:, :, :], x_in)
    first.start(par[:, :], params)
    first.start(ident[:, :], table_ap("ident"))
    first.start(ones[:, :], table_ap("ones"))
    first.start(eps[:, :], table_ap("eps"))
    constants = first.start(masks_f32[:, :], table_ap("masks"))
    masks_ready = dve.do(lambda e: e.tensor_copy(masks[:, :], masks_f32[:, :]), constants)
    table_loads = Loads(pool, sem("tables_in"))
    ident_bf, causal_bf, causal_t_bf = masks[:, 0:P], masks[:, P:2 * P], masks[:, 2 * P:6 * P]
    dil_bf = lambda kind, part: masks[:, (6 + 3 * kind + part) * P:(7 + 3 * kind + part) * P]
    for q in (pe, act, dve):
        q.wait(constants)

    raw_sem = [sem(f"raw_landed{i}") for i in range(RAW)]
    raw_loads = [Loads(sp, s) for s in raw_sem]
    raw_free, split_done, unit_used = [None] * RAW, {}, {}
    loaded, split = [0], [0]
    offsets = np.cumsum([0] + [u[3] * u[5] * P for u in units]).tolist()

    def load_unit():
        u = loaded[0]
        if u < len(units):
            n = units[u][3] * units[u][5]
            src = weights[offsets[u]:offsets[u + 1]].rearrange("(p c) -> p c", p=P)
            raw_loads[u % RAW].start(raw[u % RAW][:, 0:n], src, raw_free[u % RAW])
            loaded[0] += 1

    def split_unit():
        u = split[0]
        if u < len(units):
            n, r, s = units[u][3] * units[u][5], u % RAW, u % HL
            landed = (raw_sem[r], 16 * (u // RAW + 1))
            used = unit_used.get(u - HL)
            hi = act.do(lambda e: e.activation(w_hi[s][:, 0:n], raw[r][:, 0:n], ACT.Copy), landed, used)
            lo = dve.do(lambda e: e.tensor_tensor(w_lo[s][:, 0:n], raw[r][:, 0:n], f32(w_hi[s][:, 0:n]), ALU.subtract),
                        landed, used, hi)
            raw_free[r] = [hi, lo]
            split_done[u] = [hi, lo]
            split[0] += 1
            load_unit()

    next_unit = [0]

    def take_unit():
        u = next_unit[0]
        next_unit[0] += 1
        while split[0] < min(u + HL, len(units)):
            split_unit()
        pe.wait(split_done[u])
        return u

    for _ in range(RAW):
        load_unit()

    def gemm_fm(n_tiles, k_tiles, hi, lo, ready, evacuate, tile0=0):
        for panel in range(n_tiles // 2):
            banks = [2 * (gemm_turn[0] % 2), 2 * (gemm_turn[0] % 2) + 1]
            gemm_turn[0] += 1
            kt = 0
            while kt < k_tiles:
                u = take_unit()
                nk = units[u][3]
                wh = w_hi[u % HL][:, 0:nk * 256].rearrange("p (k c) -> p k c", k=nk)
                wl = w_lo[u % HL][:, 0:nk * 256].rearrange("p (k c) -> p k c", k=nk)
                for k in range(nk):
                    pe.wait(ready[kt])
                    for step, (w, a) in enumerate(((wh, hi), (wh, lo), (wl, hi))):
                        for j, b in enumerate(banks):
                            if kt == 0 and step == 0:
                                pe.wait(bank_free[b])
                            end = k == nk - 1 and step == 2
                            mark = pe.do(
                                lambda e, b=b, w=w, a=a, k=k, kt=kt, j=j, step=step: e.matmul(
                                    bank[b][:, :], w[:, k, j * P:(j + 1) * P], a[:, kt, :],
                                    start=kt == 0 and step == 0, stop=kt == k_tiles - 1 and step == 2),
                                signal=end)
                    kt += 1
                unit_used[u] = mark
            for j, b in enumerate(banks):
                evacuate(tile0 + 2 * panel + j, b, mark)

    gemm_turn = [0]

    def gemm_tm(k_tiles, hi, lo, ready, evacuate):
        for panel in range(2):
            for kt0 in range(0, k_tiles, 2):
                u = take_unit()
                wh = w_hi[u % HL][:, :].rearrange("p (k c) -> p k c", k=2)
                wl = w_lo[u % HL][:, :].rearrange("p (k c) -> p k c", k=2)
                for k in range(2):
                    kt = kt0 + k
                    pe.wait(ready[kt])
                    for step, (a, w) in enumerate(((hi, wh), (lo, wh), (hi, wl))):
                        for t in range(TB):
                            if kt == 0 and step == 0:
                                pe.wait(bank_free[t])
                            mark = pe.do(
                                lambda e, t=t, w=w, a=a, k=k, kt=kt, step=step: e.matmul(
                                    bank[t][:, :], a[:, kt, t * P:(t + 1) * P], w[:, k, :],
                                    start=kt == 0 and step == 0, stop=kt == k_tiles - 1 and step == 2),
                                signal=step == 2)
                            if step == 2 and kt == k_tiles - 1:
                                evacuate(t, panel, mark)
                unit_used[u] = mark

    def split_tile(src, hi, lo, *ready):
        m_hi = act.do(lambda e: e.activation(hi, src, ACT.Copy), *ready)
        m_lo = dve.do(lambda e: e.tensor_tensor(lo, src, f32(hi), ALU.subtract), m_hi, *ready)
        return [m_hi, m_lo]

    SUMSQ, SUM = 4, 5

    def add_square(f, src, *ready):
        t = 4 + f % 2
        sq = act.do(lambda e: e.activation(scr[t][:, :], src, ACT.Square), scr_free[t], *ready)
        if f == 0:
            pe.wait(bank_free[SUMSQ])
        scr_free[t] = pe.do(lambda e: e.matmul(bank[SUMSQ][:, :], ones[:, :], scr[t][:, :],
                                               start=f == 0, stop=f == DT - 1), sq)
        return scr_free[t]

    def inverse_root(dst, src_bank, scale, eps_col, *ready):
        root = act.do(lambda e: e.activation(dst, src_bank, ACT.Sqrt, bias=eps[:, eps_col:eps_col + 1], scale=scale),
                      *ready)
        return root, dve.do(lambda e: e.reciprocal(dst, dst), root)

    def rms_norm(gain, sums, in_place, *h_free):
        root, inv = inverse_root(scr[0][:, :], bank[SUMSQ][:, :], 1.0 / D, 0, sums, scr_free[0])
        bank_free[SUMSQ] = root
        ready = []
        for f in range(DT):
            t = 1 + f % 3
            y = x[:, f, :] if in_place else scr[t][:, :]
            m = dve.do(lambda e: e.scalar_tensor_tensor(y, x[:, f, :], p_(gain, f), scr[0][:, :], ALU.mult, ALU.mult),
                       inv, scr_free[t])
            ready.append(split_tile(y, h_hi[:, f, :], h_lo[:, f, :], m, *h_free))
            scr_free[t] = ready[-1]
        scr_free[0] = m
        return ready

    def layer_norm(gain, shift, sums, x_ready, *h_free):
        for f in range(DT):
            m = dve.do(lambda e: e.scalar_tensor_tensor(x[:, f, :], bank[SUM][:, :], -1.0 / D, x[:, f, :],
                                                        ALU.mult, ALU.add), sums, x_ready[f])
            done = add_square(f, x[:, f, :], m)
        bank_free[SUM] = m
        root, inv = inverse_root(scr[0][:, :], bank[SUMSQ][:, :], 1.0 / D, 1, done, scr_free[0])
        bank_free[SUMSQ] = root
        ready = []
        for f in range(DT):
            t = 1 + f % 3
            m = dve.do(lambda e: e.scalar_tensor_tensor(scr[t][:, :], x[:, f, :], p_(gain, f), scr[0][:, :],
                                                        ALU.mult, ALU.mult), inv, scr_free[t])
            hi = act.do(lambda e: e.activation(h_hi[:, f, :], scr[t][:, :], ACT.Identity, bias=p_(shift, f)),
                        m, *h_free)
            xs = act.do(lambda e: e.activation(x[:, f, :], scr[t][:, :], ACT.Identity, bias=p_(shift, f)))
            lo = dve.do(lambda e: e.tensor_tensor(h_lo[:, f, :], x[:, f, :], f32(h_hi[:, f, :]), ALU.subtract),
                        hi, xs, *h_free)
            scr_free[t] = xs
            ready.append([hi, lo, xs])
        scr_free[0] = m
        return ready

    class Residual:

        def __init__(self, scale, mean):
            self.scale, self.mean, self.ready, self.sums = scale, mean, [], None

        def __call__(self, f, b, mark):
            m = dve.do(lambda e: e.scalar_tensor_tensor(x[:, f, :], x[:, f, :], self.scale, bank[b][:, :],
                                                        ALU.mult, ALU.add), mark)
            bank_free[b] = m
            self.ready.append(m)
            if self.mean:
                if f == 0:
                    pe.wait(bank_free[SUM])
                self.sums = pe.do(lambda e: e.matmul(bank[SUM][:, :], ones[:, :], x[:, f, :],
                                                     start=f == 0, stop=f == DT - 1), m)
            else:
                self.sums = add_square(f, x[:, f, :], m)

    swap_sem = [sem(f"halves_swapped{i}") for i in range(2)]
    swaps = [Loads(sp, s) for s in swap_sem]

    class Rope:

        def __init__(self, dst, half, cos, sin, scales, tables_ready, *dst_free):
            self.dst, self.half, self.cos, self.sin, self.scales = dst, half, cos, sin, scales
            self.first, self.pending, self.ready = [tables_ready, *dst_free], None, {}

        def __call__(self, f, b, mark):
            i = f % 2
            t, sw = scr[i], scr[2 + i]
            copied = act.do(lambda e: e.activation(t[:, :], bank[b][:, :], ACT.Copy, scale=self.scales(f)),
                            mark, scr_free[i])
            bank_free[b] = copied
            for p0 in range(0, P, self.half):
                p1 = p0 ^ self.half
                landed = swaps[i].start(sw[p0:p0 + self.half, :], t[p1:p1 + self.half, :], copied, scr_free[2 + i])
            self.flush()
            self.pending = (f, i, copied, landed)

        def flush(self):
            if self.pending:
                f, i, copied, landed = self.pending
                t, sw = scr[i], scr[2 + i]
                a = dve.do(lambda e: e.tensor_tensor(self.dst[:, f, :], t[:, :], self.cos, ALU.mult), copied, *self.first)
                c = dve.do(lambda e: e.tensor_tensor(sw[:, :], sw[:, :], self.sin, ALU.mult), landed)
                m = dve.do(lambda e: e.tensor_tensor(self.dst[:, f, :], self.dst[:, f, :], sw[:, :], ALU.add), a, c)
                scr_free[i], scr_free[2 + i] = [a, landed], m
                self.ready[f] = m
                self.pending = None

    def attention_stage(qkv_gain_sums, gain, differential):
        tag = "d" if differential else "e"
        h_ready = rms_norm(gain, qkv_gain_sums, False, pe.last())
        before = [pe.last(), act.last(), dve.last()]
        q = at(f"q_{tag}", [P, DT, S], F32, at_big)
        k = at(f"k_{tag}", [P, DT, S], F32, at_big + 16 * K)
        v = at(f"v_{tag}", [P, TB, D], F32, at_big + 32 * K)
        maps = 2 if differential else 1
        prob = [at(f"prob{i}_{tag}", [P, TRI_N], F32, at_big + (48 + 5 * i) * K) for i in range(2 * maps)]
        prob_t = [at(f"probt{i}_{tag}", [P, TRI_N], F32, at_big + (48 + 5 * (2 * maps + i)) * K) for i in range(2)] \
            if not differential else [at(f"probt0_{tag}", [P, TRI_N], F32, at_big + 68 * K),
                                      at(f"probt1_{tag}", [P, TRI_N], F32, at_big + 73 * K)]
        rope = at(f"rope_{tag}", [P, 2 * S], F32, at_big + 84 * K)
        rope_in = table_loads.start(rope[:, :], table_ap("rope64"), before)
        both = lambda d, s: Rope(d, HD // 2, rope[:, 0:S], rope[:, S:2 * S], s, rope_in, before)
        to_q, to_k = both(q, lambda f: HD ** -0.5), both(k, lambda f: 1.0)
        gemm_fm(DT, DT, h_hi, h_lo, h_ready, to_q)
        to_q.flush()
        gemm_fm(DT, DT, h_hi, h_lo, h_ready, to_k)
        to_k.flush()
        v_ready = []

        def keep_v(t, panel, mark):
            eng, fn = (act, lambda e: e.activation(v[:, t, panel * 512:(panel + 1) * 512], bank[t][:, :], ACT.Copy)) \
                if t % 2 else (dve, lambda e: e.tensor_copy(v[:, t, panel * 512:(panel + 1) * 512], bank[t][:, :]))
            bank_free[t] = eng.do(fn, mark, before)
            v_ready.append(bank_free[t])

        gemm_tm(DT, h_hi, h_lo, h_ready, keep_v)
        h_free = pe.last()

        turn = {"s": 0, "t": 0}
        prob_free, prob_t_free = [None] * len(prob), [None] * 2
        lam = None
        if differential:
            lv = lambda i: p_("lambdas", i * HD, HD)
            m = []
            for i in range(2):
                m.append(dve.do(lambda e: e.tensor_tensor(scr[4][:, i * HD:(i + 1) * HD], lv(2 * i), lv(2 * i + 1), ALU.mult),
                                scr_free[4]))
            m = dve.do(lambda e: e.tensor_reduce(stats[:, 200:202], scr[4][:, 0:2 * HD].rearrange("p (a b) -> p a b", a=2),
                                                 AX_X, ALU.add), m)
            m = act.do(lambda e: e.activation(stats[:, 202:204], stats[:, 200:202], ACT.Exp), m)
            m = dve.do(lambda e: e.tensor_tensor(stats[:, 204:205], stats[:, 203:204], stats[:, 202:203], ALU.subtract), m)
            lam = dve.do(lambda e: e.tensor_scalar(stats[:, 205:206], stats[:, 204:205], -LAMBDA_INIT, None, ALU.add), m)

        def head_rows(n):
            return (n // 2, (n % 2) * HD)

        heads = DT if differential else 2 * DT
        marks = {}
        col = lambda m, what, i=0, n=1: stats[:, 32 * (m % 4) + 8 * what + i:32 * (m % 4) + 8 * what + i + n]

        def scores_and_exp(n, c):
            m = n * maps + c
            tile, p0 = (n, c * HD) if differential else head_rows(n)
            slot = m % len(prob)
            dilated = not differential and n >= DT
            done = []
            for i in range(TB):
                b, w = turn["s"] % 3, (i + 1) * P
                turn["s"] += 1
                if dilated:
                    adds = [(kb, dil_bf(min(i - kb, 2), part)) for kb in range(i + 1) for part in range(3)]
                else:
                    adds = [(i, causal_bf)]
                for j, (kb, mask) in enumerate(adds):
                    pe.do(lambda e: e.matmul(bank[b][:, kb * P:(kb + 1) * P], ident_bf, mask, start=j == 0, stop=False,
                                             skip_group_check=True), bank_free[b], masks_ready, signal=False)
                s = pe.do(lambda e: e.matmul(
                    bank[b][:, 0:w], q[p0:p0 + HD, tile, i * P:(i + 1) * P], k[p0:p0 + HD, tile, 0:w],
                    start=False, stop=True, skip_group_check=True), to_q.ready[tile], to_k.ready[tile])
                mx = dve.do(lambda e, b=b, w=w, i=i: e.tensor_reduce(col(m, 0, i), bank[b][:, 0:w], AX_X, ALU.max, negate=True),
                            s, prob_free[slot])
                ex = act.do(lambda e, b=b, w=w, i=i: e.activation(
                    prob[slot][:, TRQ[i]:TRQ[i] + w], bank[b][:, 0:w], ACT.Exp, bias=col(m, 0, i), accum_out=col(m, 1, i)),
                    mx, prob_free[slot], before)
                bank_free[b] = ex
                done.append(ex)
            marks["exp", m] = done[-1]

        def normalise(n):
            out = []
            for c in range(maps):
                m = n * maps + c
                inv = dve.do(lambda e: e.reciprocal(col(m, 2, 0, TB), col(m, 1, 0, TB)), marks["exp", m])
                if c:
                    inv = dve.do(lambda e: e.tensor_scalar(col(m, 2, 0, TB), col(m, 2, 0, TB), stats[:, 205:206], None,
                                                           ALU.mult), inv, lam)
            m0 = n * maps
            s0 = m0 % len(prob)
            for i in range(TB):
                rows = slice(TRQ[i], TRQ[i] + (i + 1) * P)
                if not differential:
                    out.append(dve.do(lambda e, i=i, rows=rows: e.tensor_scalar(
                        prob[s0][:, rows], prob[s0][:, rows], col(m0, 2, i), None, ALU.mult), inv))
                else:
                    s1 = (m0 + 1) % len(prob)
                    a = dve.do(lambda e, i=i, rows=rows: e.tensor_scalar(
                        prob[s1][:, rows], prob[s1][:, rows], col(m0 + 1, 2, i), None, ALU.mult), inv)
                    out.append(dve.do(lambda e, i=i, rows=rows: e.scalar_tensor_tensor(
                        prob[s0][:, rows], prob[s0][:, rows], col(m0, 2, i), prob[s1][:, rows], ALU.mult, ALU.add), a))
                    prob_free[s1] = out[-1]
            marks["norm", n] = out

        def transpose(n):
            s0, st = (n * maps) % len(prob), n % 2
            done = []
            for kb in range(TB):
                b = 3 + turn["t"] % 3
                turn["t"] += 1
                for i in range(kb, TB):
                    src = prob[s0][:, TRQ[i] + kb * P:TRQ[i] + (kb + 1) * P]
                    t = pe.do(lambda e, b=b, i=i, kb=kb, src=src: e.transpose(
                        bank[b][:, (i - kb) * P:(i - kb + 1) * P], src, ident[:, :]),
                        marks["norm", n][i], bank_free[b], signal=i == TB - 1)
                w = (TB - kb) * P
                dst = prob_t[st][:, TRI[kb]:TRI[kb] + w]
                if kb % 2 == 0:
                    cp = act.do(lambda e, b=b, w=w, dst=dst: e.activation(dst, bank[b][:, 0:w], ACT.Copy), t,
                                prob_t_free[st], before)
                else:
                    cp = dve.do(lambda e, b=b, w=w, dst=dst: e.tensor_copy(dst, bank[b][:, 0:w]), t,
                                prob_t_free[st], before)
                bank_free[b] = cp
                done.append(cp)
            prob_free[s0] = t
            marks["pt", n] = done

        def values(n):
            st = n % 2
            if differential:
                b, rows, cols = 6 + n % 2, slice(0, P), slice(n * P, (n + 1) * P)
            else:
                b, rows, cols = 6 + (n // 2) % 2, slice((n % 2) * HD, (n % 2) * HD + HD), slice(n * HD, (n + 1) * HD)
            for kb in reversed(range(TB)):
                o = pe.do(lambda e: e.matmul(
                    bank[b][rows, kb * P:S], v[:, kb, cols], prob_t[st][:, TRI[kb]:TRI[kb] + (TB - kb) * P],
                    start=kb == TB - 1, stop=kb == 0, skip_group_check=True),
                    marks["pt", n][kb], v_ready, bank_free[b], signal=kb == 0)
            prob_t_free[st] = o
            if differential:
                m = act.do(lambda e: e.activation(q[:, n, :], bank[b][:, :], ACT.Copy), o)
                bank_free[b] = m
                marks["o", n] = m
            elif n % 2:
                f = n // 2
                hi = act.do(lambda e: e.activation(h_hi[:, f, :], bank[b][:, :], ACT.Copy), o, h_free)
                lo = dve.do(lambda e: e.tensor_tensor(h_lo[:, f, :], bank[b][:, :], f32(h_hi[:, f, :]), ALU.subtract),
                            hi, h_free)
                bank_free[b] = lo
                marks["o", f] = [hi, lo]

        for n in range(heads + 2):
            if n < heads:
                for c in range(maps):
                    scores_and_exp(n, c)
            if 1 <= n <= heads:
                normalise(n - 1)
                transpose(n - 1)
            if n >= 2:
                values(n - 2)
        if not differential:
            return [marks["o", f] for f in range(DT)]

        ready = []
        gain_m = dve.do(lambda e: e.tensor_scalar(stats[:, 206:207], p_("subln"), 1.0 - LAMBDA_INIT, None, ALU.mult))
        for f in range(DT):
            t, b = f % 2, f % 3
            sq = act.do(lambda e: e.activation(scr[t][:, :], q[:, f, :], ACT.Square), marks["o", f], scr_free[t])
            ss = pe.do(lambda e: e.matmul(bank[b][:, :], ones[:, :], scr[t][:, :], start=True, stop=True),
                       sq, bank_free[b])
            root, inv = inverse_root(scr[2 + t][:, :], bank[b][:, :], 1.0 / P, 1, ss, scr_free[2 + t])
            bank_free[b], scr_free[t] = root, ss
            y = dve.do(lambda e: e.scalar_tensor_tensor(q[:, f, :], q[:, f, :], stats[:, 206:207], scr[2 + t][:, :],
                                                        ALU.mult, ALU.mult), inv, gain_m)
            scr_free[2 + t] = y
            ready.append(split_tile(q[:, f, :], h_hi[:, f, :], h_lo[:, f, :], y, h_free))
        return ready

    def causal_conv(dst, b, weight, bias, n_taps, stride, f, *marks_):
        w = lambda tap: p_(weight, tap * stride + f)
        m = act.do(lambda e: e.activation(dst, bank[b][:, :], ACT.Identity, bias=p_(bias, f), scale=w(n_taps - 1)), *marks_)
        for back in range(1, n_taps):
            m = dve.do(lambda e, back=back: e.scalar_tensor_tensor(
                dst[:, back:S], bank[b][:, 0:S - back], w(n_taps - 1 - back), dst[:, back:S], ALU.mult, ALU.add), m)
        return m

    def ffn(h_ready, conv, residual, tag):
        before = [pe.last(), act.last(), dve.last()]
        hid_hi = at(f"hid_hi{tag}", [P, FT, S], F32R, at_big)
        hid_lo = at(f"hid_lo{tag}", [P, FT, S], F32R, at_big + 44 * K)
        gate_ready, hid_ready = {}, [None] * FT

        def gate(f, b, mark):
            t = f % 2
            if conv is None:
                m = act.do(lambda e: e.activation(scr[t][:, :], bank[b][:, :], ACT.Silu), mark, scr_free[t])
                bank_free[b] = m
            else:
                m = causal_conv(scr[t][:, :], b, f"fconv_w{conv}", f"fconv_b{conv}", 3, 2 * FT, f, mark, scr_free[t])
                bank_free[b] = m
                m = act.do(lambda e: e.activation(scr[t][:, :], scr[t][:, :], ACT.Silu), m)
            gate_ready[f] = m

        def value(f, b, mark):
            t, g = 2 + f % 2, f % 2
            if conv is None:
                m = dve.do(lambda e: e.tensor_tensor(scr[t][:, :], bank[b][:, :], scr[g][:, :], ALU.mult),
                           mark, gate_ready[f], scr_free[t])
                bank_free[b] = m
            else:
                m = causal_conv(scr[t][:, :], b, f"fconv_w{conv}", f"fconv_b{conv}", 3, 2 * FT, FT + f, mark, scr_free[t])
                bank_free[b] = m
                m = dve.do(lambda e: e.tensor_tensor(scr[t][:, :], scr[t][:, :], scr[g][:, :], ALU.mult), m, gate_ready[f])
            scr_free[g] = m
            hid_ready[f] = split_tile(scr[t][:, :], hid_hi[:, f, :], hid_lo[:, f, :], m, before)
            scr_free[t] = hid_ready[f]

        for panel in range(FT // 2):
            gemm_fm(2, DT, h_hi, h_lo, h_ready, gate, 2 * panel)
            gemm_fm(2, DT, h_hi, h_lo, h_ready, value, 2 * panel)
        gemm_fm(DT, FT, hid_hi, hid_lo, hid_ready, residual)

    for f in range(DT):
        sums = add_square(f, x[:, f, :], x_landed)
    for layer in range(DEPTH):
        o_ready = attention_stage(sums, ("even_norm", "odd_norm")[layer], layer == 1)
        res = Residual(1.0, False)
        gemm_fm(DT, DT, h_hi, h_lo, o_ready, res)
        h_ready = rms_norm(f"ffn_norm{layer}", res.sums, False, pe.last())
        res = Residual(1.0, False)
        ffn(h_ready, layer, res, f"_{layer}")
        sums = res.sums
    x_ready = rms_norm("final_norm", sums, True, pe.last())

    def recurrent_core(tag, q, k, v, v_cols, weights_t, sm, out, first_marks, q_ready, k_ready, v_ready, prepare):
        done = []
        for h in range(NH2):
            prepared = prepare(h)
            slot = h % 2
            sm_m = []
            for sb in range(TB):
                b, w = sb % 2, (TB - sb) * P
                q_h, k_h, weight = q(h), k(h), weights_t(h, sb)
                s = pe.do(lambda e, b=b, sb=sb, w=w: e.matmul(
                    bank[b][:, 0:w], k_h[:, sb * P:(sb + 1) * P], q_h[:, sb * P:S], start=True, stop=True),
                    q_ready(h), k_ready(h), bank_free[b])
                m = dve.do(lambda e, b=b, sb=sb, w=w: e.scalar_tensor_tensor(
                    sm[slot][:, TRI[sb]:TRI[sb] + w], bank[b][:, 0:w], DK ** -0.5, weight, ALU.mult, ALU.mult),
                    s, prepared, sm_free[slot], first_marks)
                bank_free[b] = m
                sm_m.append(m)
            weights_free[0] = m
            for tb in range(TB):
                b = 4 + tb
                for sb in range(tb + 1):
                    v_h = v(sb, h)
                    o = pe.do(lambda e, b=b, tb=tb, sb=sb: e.matmul(
                        bank[b][:, 0:v_cols], sm[slot][:, TRI[sb] + (tb - sb) * P:TRI[sb] + (tb - sb + 1) * P],
                        v_h, start=sb == 0, stop=sb == tb),
                        sm_m[sb], v_ready, bank_free[b], signal=sb == tb)
                c = h * TB + tb
                row_ = out[:, tb, h * DV:(h + 1) * DV]
                cp = act.do(lambda e: e.activation(row_, bank[b][:, 0:DV], ACT.Copy), o, first_marks)
                bank_free[b] = cp
                if v_cols > DV:
                    bank_free[b] = act.do(lambda e: e.activation(stats[:, 48 + c:49 + c], bank[b][:, DV:DV + 1], ACT.Copy))
                six = stats[:, 224 + 6 * (c % 4):230 + 6 * (c % 4)]
                st = dve.do(lambda e: e.bn_stats(six, row_), cp, six_free[c % 4])
                st = six_free[c % 4] = dve.do(lambda e: e.bn_aggr(stats[:, 2 * c:2 * c + 2], six), st, first_marks)
                done += [st, bank_free[b]]
            sm_free[slot] = o
        return done

    sm_free, weights_free, six_free = [None, None], [None], [None] * 4
    mean_c = lambda c: stats[:, 2 * c:2 * c + 1]
    all_var = stats[:, 0:32].rearrange("p (c two) -> p c two", two=2)[:, :, 1]

    def normalise_heads(out, var_plus, *ready):
        if var_plus is None:
            m = act.do(lambda e: e.activation(stats[:, 32:48], all_var, ACT.Sqrt, bias=eps[:, 1:2]), *ready)
        else:
            m = dve.do(lambda e: e.tensor_tensor(stats[:, 32:48], all_var, var_plus, ALU.add), *ready)
            m = act.do(lambda e: e.activation(stats[:, 32:48], stats[:, 32:48], ACT.Sqrt), m)
        m = dve.do(lambda e: e.reciprocal(stats[:, 32:48], stats[:, 32:48]), m)
        for c in range(NH2 * TB):
            h, tb = c // TB, c % TB
            y = out[:, tb, h * DV:(h + 1) * DV]
            n = dve.do(lambda e, y=y, c=c: e.tensor_scalar(y, y, mean_c(c), stats[:, 32 + c:33 + c],
                                                           ALU.subtract, ALU.mult), m)
        return n

    for layer in range(DEPTH):
        L = str(layer)
        before = [pe.last(), act.last(), dve.last()]
        tm_ret = at("ret_tm" + L, [P, TB, D], F32, at_big)
        tm_ml = at("ml_tm" + L, [P, TB, D], F32, at_big + 16 * K)
        rq = at("rq" + L, [P, NH2, S], F32, at_big + 32 * K)
        rk = at("rk" + L, [P, NH2, S], F32, at_big + 40 * K)
        rv = at("rv" + L, [P, TB, D], F32, at_big + 48 * K)
        rope = at("rope2_" + L, [P, 2 * S], F32, at_big + 28 * K)
        sm_r = [at(f"sm_ret{i}_{L}", [P, TRI_N], F32, at_big + (16 + 5 * i) * K) for i in range(2)]
        decay = at("decay" + L, [P, NH2, S], F32, at_big + 80 * K)
        rope_in = table_loads.start(rope[:, :], table_ap("rope128"), before)
        decay_in = table_loads.start(decay[:, :, :], table_ap("decay"), before)

        class Split2:
            def __init__(self):
                mk = lambda d: Rope(d, DK // 2, rope[:, 0:S], rope[:, S:2 * S], lambda f: 1.0, decay_in, before)
                self.q, self.k = mk(rq), mk(rk)

            def __call__(self, f, b, mark):
                (self.q if f < NH2 else self.k)(f % NH2, b, mark)
                if f == NH2 - 1:
                    self.q.flush()

        rot = Split2()
        gemm_fm(2 * NH2, DT, h_hi, h_lo, x_ready, rot)
        rot.k.flush()
        rv_ready = []

        def keep(dst, ready, width):
            def evacuate(t, panel, mark):
                for j in range(2):
                    d = dst[:, t, (2 * panel + j) * width:(2 * panel + j) * width + DV]
                    s_ = bank[t][:, j * DV:(j + 1) * DV]
                    if t % 2:
                        m = act.do(lambda e: e.activation(d, s_, ACT.Copy), mark, before2[0])
                    else:
                        m = dve.do(lambda e: e.tensor_copy(d, s_), mark, before2[0])
                bank_free[t] = m
                ready.append(m)
            return evacuate

        before2 = [before]
        gemm_tm(DT, h_hi, h_lo, x_ready, keep(rv, rv_ready, DV))
        ret_done = recurrent_core(
            "r", lambda h: rq[:, h, :], lambda h: rk[:, h, :], lambda sb, h: rv[:, sb, h * DV:(h + 1) * DV], DV,
            lambda h, sb: decay[:, h, 0:S - sb * P], sm_r, tm_ret, before,
            lambda h: rot.q.ready[h], lambda h: rot.k.ready[h], rv_ready, lambda h: decay_in)
        ret_normed = normalise_heads(tm_ret, None, ret_done)

        before = [pe.last(), act.last(), dve.last()]
        before2[0] = before
        mqk = at("mqk" + L, [P, DT, S], F32, at_big + 64 * K)
        mv = at("mv" + L, [P, TB, NH2 * (DV + 1)], F32, at_big + 32 * K)
        sm_m = [at(f"sm_ml{i}_{L}", [P, TRI_N], F32, at_big + 48 * K + 512 + 5 * K * i) for i in range(2)]
        gates_t = at("gates_t" + L, [P, TRI_N], F32, at_big + 58 * K + 512)
        row = [at(f"row{i}_{L}", [NH2, S], F32, at_big + (80 + 2 * i) * K) for i in range(4)]
        select = scr[5][0:NH2, :]
        select_in = table_loads.start(select, table_ap("select")[0:NH2, :], before, scr_free[5])
        mqk_ready = {}

        def to_mqk(f, b, mark):
            t = f % 2
            m = causal_conv(scr[t][:, :], b, "mconv_w" + L, "mconv_b" + L, 4, DT, f, mark, scr_free[t])
            bank_free[b] = m
            mqk_ready[f] = scr_free[t] = act.do(lambda e: e.activation(mqk[:, f, :], scr[t][:, :], ACT.Silu), m, before)

        gemm_fm(DT, DT, h_hi, h_lo, x_ready, to_mqk)
        mv_heads = mv[:, :, :].rearrange("p t (h c) -> p t h c", h=NH2)
        mv_ready = [dve.do(lambda e: e.memset(mv_heads[:, :, :, DV], 1.0), before)]
        gemm_tm(DT, h_hi, h_lo, x_ready, keep(mv, mv_ready, DV + 1))

        GB = 7
        for kt in range(DT):
            g = pe.do(lambda e, kt=kt: e.matmul(bank[GB][0:36, :], p_("w_if" + L, kt * 36, 36), x[:, kt, :],
                                                start=kt == 0, stop=kt == DT - 1), bank_free[GB], x_ready[kt],
                      signal=kt == DT - 1)
        z, lf, a_row, big_f = row
        R = slice(0, NH2)
        tmp = scr[4][R, :]
        bi, bf = (par[R, PARAMS[n + L][0]:PARAMS[n + L][0] + 1] for n in ("b_i", "b_f"))
        i_m = act.do(lambda e: e.activation(a_row[R, :], bank[GB][R, :], ACT.Identity, bias=bi), g, before)
        z_m = act.do(lambda e: e.activation(z[R, :], bank[GB][32:36, :], ACT.Identity, bias=bf), g)
        bank_free[GB] = z_m
        m = dve.do(lambda e: e.scalar_tensor_tensor(tmp, z[R, :], -1.0, z[R, :], ALU.mult, ALU.min), z_m, scr_free[4])
        m = act.do(lambda e: e.activation(tmp, tmp, ACT.Exp), m)
        m = act.do(lambda e: e.activation(tmp, tmp, ACT.Ln, bias=ones[R, 0:1]), m)
        m = dve.do(lambda e: e.scalar_tensor_tensor(lf[R, :], z[R, :], 0.0, tmp, ALU.min, ALU.subtract), m)
        zero = dve.do(lambda e: e.memset(z[R, :], 0.0), m)
        m = dve.do(lambda e: e.tensor_tensor_scan(big_f[R, :], lf[R, :], z[R, :], 0.0, ALU.add, ALU.add), m, zero)
        m = dve.do(lambda e: e.tensor_tensor(a_row[R, :], a_row[R, :], big_f[R, :], ALU.subtract), m, i_m)
        a_m = m
        m = dve.do(lambda e: e.tensor_tensor_scan(lf[R, :], a_row[R, :], a_row[R, :], 0.0, ALU.max, ALU.max), m)
        mm = m
        m = dve.do(lambda e: e.tensor_scalar(lf[R, :], lf[R, :], -1.0, None, ALU.mult), mm)
        nm_m = m
        m = dve.do(lambda e: e.tensor_tensor(z[R, :], lf[R, :], big_f[R, :], ALU.subtract), m)
        for tb in range(TB):
            t1 = pe.do(lambda e, tb=tb: e.transpose(bank[6][:, tb * 4:tb * 4 + 4], a_row[R, tb * P:(tb + 1) * P],
                                                    ident[R, R]), a_m, bank_free[6])
        for tb in range(TB):
            t1 = pe.do(lambda e, tb=tb: e.transpose(bank[6][:, 16 + tb * 4:20 + tb * 4], z[R, tb * P:(tb + 1) * P],
                                                    ident[R, R]), m)
        a_cols = dve.do(lambda e: e.tensor_copy(stats[:, 64:80], bank[6][:, 0:16]), t1)
        floor_m = act.do(lambda e: e.activation(stats[:, 80:96].rearrange("p (h t) -> p t h", h=NH2),
                                                bank[6][:, 16:32].rearrange("p (t h) -> p t h", t=TB), ACT.Exp), a_cols)
        bank_free[6] = floor_m
        scr_free[4] = m

        def prepare(h):
            out_ = []
            for b in (2, 3):
                m = pe.do(lambda e, b=b: e.matmul(bank[b][:, :], select[:, h * P:(h + 1) * P], lf[R, :],
                                                  start=True, stop=b == 2), nm_m, select_in, bank_free[b])
            m2 = pe.do(lambda e: e.matmul(bank[3][:, :], ident_bf, causal_t_bf, start=False, stop=True))
            for sb in range(TB):
                bias = stats[:, 64 + sb * NH2 + h:65 + sb * NH2 + h]
                c0, w = sb * P, (TB - sb - 1) * P
                g_ = act.do(lambda e, sb=sb, bias=bias, c0=c0: e.activation(
                    gates_t[:, TRI[sb]:TRI[sb] + P], bank[3][:, c0:c0 + P], ACT.Exp, bias=bias),
                    m2, a_cols, weights_free[0], before)
                if w:
                    g_ = act.do(lambda e, sb=sb, bias=bias, c0=c0, w=w: e.activation(
                        gates_t[:, TRI[sb] + P:TRI[sb] + P + w], bank[2][:, c0 + P:S], ACT.Exp, bias=bias))
            bank_free[2] = bank_free[3] = g_
            scr_free[5] = m2
            return g_

        ml_done = recurrent_core(
            "m", lambda h: mqk[:, h, :], lambda h: mqk[:, NH2 + h, :],
            lambda sb, h: mv[:, sb, h * (DV + 1):(h + 1) * (DV + 1)], DV + 1,
            lambda h, sb: gates_t[:, TRI[sb]:TRI[sb] + (TB - sb) * P], sm_m, tm_ml, [before, ret_normed],
            lambda h: mqk_ready[h], lambda h: mqk_ready[NH2 + h], mv_ready, prepare)
        den = stats[:, 48:64]
        m = dve.do(lambda e: e.scalar_tensor_tensor(stats[:, 96:112], den, -1.0, den, ALU.mult, ALU.max), ml_done)
        m = dve.do(lambda e: e.tensor_tensor(den, stats[:, 96:112], stats[:, 80:96], ALU.max), m, floor_m)
        m = dve.do(lambda e: e.scalar_tensor_tensor(stats[:, 96:112], den, 1e-5, den, ALU.mult, ALU.mult), m)
        ml_normed = normalise_heads(tm_ml, stats[:, 96:112], m)

        before = [pe.last(), act.last(), dve.last()]
        z_hi = at("z_hi" + L, [P, DT, S], F32R, at_big + 32 * K)
        z_lo = at("z_lo" + L, [P, DT, S], F32R, at_big + 48 * K)
        y_ret = at("y_ret" + L, [P, DT, S], F32, at_big + 64 * K)
        mix_hi = at("mix_hi" + L, [P, DT, S], F32R, at_big)
        mix_lo = at("mix_lo" + L, [P, DT, S], F32R, at_big + 16 * K)

        def gated(tm, func, gain, normed, z_free):
            ready = []

            def evacuate(f, b, mark):
                t, g_, tb_ = f % 2, 2 + f % 2, 4 + f % 2
                gm = act.do(lambda e: e.activation(scr[g_][:, :], bank[b][:, :], func), mark, scr_free[g_])
                bank_free[b] = gm
                for i in range(TB):
                    tr = pe.do(lambda e, i=i: e.transpose(bank[tb_][:, i * P:(i + 1) * P], tm[:, i, f * P:(f + 1) * P],
                                                          ident[:, :]), normed, bank_free[tb_], signal=i == TB - 1)
                m = dve.do(lambda e: e.scalar_tensor_tensor(scr[t][:, :], bank[tb_][:, :], p_(gain + L, f), scr[g_][:, :],
                                                            ALU.mult, ALU.mult), gm, tr, scr_free[t])
                bank_free[tb_] = scr_free[g_] = m
                ready.append(split_tile(scr[t][:, :], z_hi[:, f, :], z_lo[:, f, :], m, z_free))
                scr_free[t] = ready[-1]
            return ready, evacuate

        z_ready, to_z = gated(tm_ret, ACT.Silu, "ret_g", ret_normed, before)
        gemm_fm(DT, DT, h_hi, h_lo, x_ready, to_z)
        gate_m, yr_ready, mix_ready = {}, {}, []

        def merge_gate(which):
            def evacuate(f, b, mark):
                t = f % 2
                gate_m[f] = act.do(lambda e: e.activation(scr[t][:, :], bank[b][:, :], ACT.Sigmoid,
                                                          bias=p_("b_merge" + L, which * DT + f)), mark, scr_free[t])
                bank_free[b] = gate_m[f]
            return evacuate

        def gate_ret(f, b, mark):
            m = dve.do(lambda e: e.tensor_tensor(y_ret[:, f, :], bank[b][:, :], scr[f % 2][:, :], ALU.mult),
                       mark, gate_m[f], before)
            bank_free[b] = scr_free[f % 2] = yr_ready[f] = m

        def gate_ml(f, b, mark):
            t = 2 + f % 2
            m = dve.do(lambda e: e.tensor_tensor(scr[t][:, :], bank[b][:, :], scr[f % 2][:, :], ALU.mult),
                       mark, gate_m[f], scr_free[t])
            bank_free[b] = scr_free[f % 2] = m
            m = dve.do(lambda e: e.tensor_tensor(scr[t][:, :], scr[t][:, :], y_ret[:, f, :], ALU.add), m, yr_ready[f])
            mix_ready.append(split_tile(scr[t][:, :], mix_hi[:, f, :], mix_lo[:, f, :], m, tm_free))
            scr_free[t] = mix_ready[-1]

        for panel in range(DT // 2):
            gemm_fm(2, DT, h_hi, h_lo, x_ready, merge_gate(0), 2 * panel)
            gemm_fm(2, DT, z_hi, z_lo, z_ready, gate_ret, 2 * panel)
        z_ready, to_z = gated(tm_ml, ACT.Sigmoid, "ml_g", ml_normed, pe.last())
        gemm_fm(DT, DT, h_hi, h_lo, x_ready, to_z)
        tm_free = pe.last()
        for panel in range(DT // 2):
            gemm_fm(2, DT, h_hi, h_lo, x_ready, merge_gate(1), 2 * panel)
            gemm_fm(2, DT, z_hi, z_lo, z_ready, gate_ml, 2 * panel)
        res = Residual(ALPHA, True)
        gemm_fm(DT, DT, mix_hi, mix_lo, mix_ready, res)
        x_ready = layer_norm("ln1_g" + L, "ln1_b" + L, res.sums, res.ready, pe.last())
        res = Residual(ALPHA, True)
        ffn(x_ready, None, res, f"_{2 + layer}")
        x_ready = layer_norm("ln2_g" + L, "ln2_b" + L, res.sums, res.ready, pe.last())

    stores = Loads(sp, sem("y_stored"))
    for f in range(DT):
        stored = stores.start(y_out[:, f, :], x[:, f, :], x_ready[f])
    sp.wait(stored)

    assert next_unit[0] == len(units)


def shape_tables():
    t = np.zeros((P, N_TABLES), np.float32)

    def put(name, a):
        t[:, TABLES[name][0]:sum(TABLES[name])] = a

    i, j = np.arange(P)[:, None], np.arange(P)[None, :]
    eye = np.eye(P, dtype=np.float32)
    neg = np.float32(-(2.0 ** 99))
    masks = [eye, np.where(j <= i, 0, neg)] + [np.where(i <= j, 0, neg)] * TB
    top = lambda a: (a.view(np.uint32) & np.uint32(0xFFFF0000)).view(np.float32)
    for kind in range(3):
        dist = P * kind + i - j
        count = np.where(dist >= 0, (dist <= 128).astype(int) + (dist % 4 == 0) + (dist % 16 == 0), 0)
        ln = np.where(count > 0, np.log(np.maximum(count, 1)), neg).astype(np.float32)
        a = top(ln.copy())
        b = top((ln - a).astype(np.float32))
        masks += [a, b, (ln - a - b).astype(np.float32)]
    put("masks", np.concatenate(masks, 1))
    put("ident", eye)
    put("ones", 1.0)
    put("eps", np.array([[1e-6, 1e-5]]))
    pos = np.arange(S, dtype=np.float32)

    def rope(inv, half):
        ang = (pos[None, :] * inv[:, None]).astype(np.float32).astype(np.float64)
        cos, sin = np.cos(ang), np.sin(ang)
        n = P // (2 * half)
        return np.concatenate([np.tile(cos, (2 * n, 1)), np.tile(np.concatenate([-sin, sin]), (n, 1))], 1)

    put("rope64", rope((1.0 / 10000.0 ** (np.arange(32, dtype=np.float32) * 2.0 / 64)).astype(np.float32), 32))
    put("rope128", rope((10000.0 ** (-np.arange(64, dtype=np.float32) / 64)).astype(np.float32), 64))
    rel = np.arange(S)[None, :] - np.arange(P)[:, None]
    lg = np.log(1.0 - 2.0 ** (-5.0 - np.arange(NH2)))
    put("decay", np.concatenate([np.where(rel >= 0, np.exp(g * np.maximum(rel, 0)), 0) for g in lg], 1))
    sel = np.zeros((P, NH2 * P))
    for h in range(NH2):
        sel[h, h * P:(h + 1) * P] = 1
    put("select", sel)
    return t


def kernel(**inputs):
    import concourse.bacc as _bacc
    from concourse.bass_utils import run_bass_kernel_spmd as _run

    a = {k: np.asarray(v) for k, v in inputs.items()}

    pieces = []
    for name, layer, k0, nk, c, w in weight_units():
        m = a[name][layer][k0 * P:(k0 + nk) * P, c:c + w]
        pieces.append(m.reshape(nk, P, w).transpose(1, 0, 2).reshape(-1))
    weights = np.concatenate(pieces)

    params = np.zeros((P, N_PARAMS), np.float32)

    def put(name, v):
        params[:, PARAMS[name][0]:sum(PARAMS[name])] = v

    tiles = lambda v: v.reshape(-1, P).T
    put("even_norm", tiles(a["even_norm"][0]))
    put("odd_norm", tiles(a["odd_norm"][0]))
    put("final_norm", tiles(a["final_norm"]))
    put("subln", tiles(a["odd_subln"][0]))
    put("lambdas", np.concatenate([a["odd_lambda_" + n][0] for n in ("q1", "k1", "q2", "k2")])[None, :])
    for l in range(2):
        L = str(l)
        put("ffn_norm" + L, tiles(a["ffn_norm"][l]))
        put("fconv_w" + L, tiles(a["ffn_conv_w"][l].reshape(-1)))
        put("fconv_b" + L, tiles(a["ffn_conv_b"][l]))
        w_if = np.zeros((D, 36), np.float32)
        w_if[:, 0:4] = a["w_in_2"][l][:, 6144:6148]
        w_if[:, 32:36] = a["w_in_2"][l][:, 6148:6152]
        put("w_if" + L, w_if.reshape(DT, P, 36).transpose(1, 0, 2).reshape(P, -1))
        params[0:4, PARAMS["b_i" + L][0]] = a["b_if_2"][l][0:4]
        params[0:4, PARAMS["b_f" + L][0]] = a["b_if_2"][l][4:8]
        put("b_merge" + L, tiles(a["b_merge_2"][l]))
        put("mconv_w" + L, tiles(a["conv_w_2"][l].reshape(-1)))
        put("mconv_b" + L, tiles(a["conv_b_2"][l]))
        for n, src in (("ret_g", "ret_norm_g_2"), ("ml_g", "mlstm_norm_g_2"), ("ln1_g", "ln1_g_2"), ("ln1_b", "ln1_b_2"),
                       ("ln2_g", "ln2_g_2"), ("ln2_b", "ln2_b_2")):
            put(n + L, tiles(a[src][l]))

    x_fm = np.ascontiguousarray(a["x"][0].T.reshape(DT, P, S).transpose(1, 0, 2))
    arrays = {"weights": weights, "params": params, "tables": shape_tables(), "x_fm": x_fm}

    nc = _bacc.Bacc("TRN2", target_bir_lowering=False, num_devices=1)
    args = [nc.dram_tensor(n, v.shape, F32, kind="ExternalInput").ap() for n, v in arrays.items()]
    out = nc.dram_tensor("y_fm", (P, DT, S), F32, kind="ExternalOutput").ap()
    build(nc, *args, out)
    r = _run(nc, [arrays], core_ids=[0])
    y = np.asarray(r.results[0]["y_fm"])
    return np.ascontiguousarray(y.transpose(2, 1, 0).reshape(1, S, D))
```

```python
import math
from contextlib import ExitStack

import numpy as np

import concourse.bass as bass
from concourse import mybir
from concourse.alu_op_type import AluOpType as ALU

F32 = mybir.dt.float32
F32R = mybir.dt.float32r
BF16 = mybir.dt.bfloat16
ACT = mybir.ActivationFunctionType
AX_X = mybir.AxisListType.X

P = 128
S = 512
D = 1024
DT = D // P
TB = S // P
D_FF = 2816
FT = D_FF // P
UNIT = 1024
BIG_NEG = -1e30
HD = 64
DK, DV, NH2 = 128, 256, 4
DEPTH = 2
ALPHA = (2 * DEPTH) ** 0.25
LAMBDA_INIT = 0.8 - 0.6 * math.exp(-0.3 * 1)
TRI = [sum((TB - j) * P for j in range(b)) for b in range(TB)]
TRQ = [sum((j + 1) * P for j in range(b)) for b in range(TB)]
TRI_N = TB * (TB + 1) // 2 * P


def columns(sizes):
    at, out = 0, {}
    for name, n in sizes:
        out[name] = (at, n)
        at += n
    return out, at


PARAMS, N_PARAMS = columns(
    [("even_norm", DT), ("odd_norm", DT), ("ffn_norm0", DT), ("ffn_norm1", DT), ("final_norm", DT), ("subln", 1)]
    + [(f"{n}{l}", c) for l in range(2) for n, c in (
        ("fconv_w", 3 * 2 * FT), ("fconv_b", 2 * FT))]
    + [("lambdas", 4 * HD)]
    + [(f"{n}{l}", c) for l in range(2) for n, c in (
        ("w_if", DT * 36), ("b_i", 1), ("b_f", 1), ("b_merge", 2 * DT), ("mconv_w", 4 * DT), ("mconv_b", DT),
        ("ret_g", DT), ("ml_g", DT), ("ln1_g", DT), ("ln1_b", DT), ("ln2_g", DT), ("ln2_b", DT))]
)
TABLES, N_TABLES = columns([
    ("masks", 15 * P),
    ("ident", P), ("ones", P), ("eps", 2),
    ("rope64", 2 * S), ("rope128", 2 * S), ("decay", NH2 * S), ("select", NH2 * P),
])


def weight_units():
    out = []

    def fm(name, layer, k, c0, c1):
        for c in range(c0, c1, 256):
            for k0 in range(0, k // P, 4):
                out.append((name, layer, k0, min(4, k // P - k0), c, 256))

    def tm(name, layer, k, c0, c1):
        for c in range(c0, c1, 512):
            for k0 in range(0, k // P, 2):
                out.append((name, layer, k0, 2, c, 512))

    def ffn(layer):
        for c in range(0, D_FF, 256):
            fm("ffn_w_up", layer, D, c, c + 256)
            fm("ffn_w_up", layer, D, D_FF + c, D_FF + c + 256)
        fm("ffn_w_down", layer, D_FF, 0, D)

    fm("even_w_in", 0, D, 0, 2 * D)
    tm("even_w_in", 0, D, 2 * D, 3 * D)
    fm("even_w_out", 0, D, 0, D)
    ffn(0)
    fm("odd_w_qkv", 0, D, 0, 2 * D)
    tm("odd_w_qkv", 0, D, 2 * D, 3 * D)
    fm("odd_w_out", 0, D, 0, D)
    ffn(1)
    for l in range(2):
        rq, rv, rg, mqk, mv, mo, ga, gb = 0, 1024, 2048, 3072, 4096, 5120, 6152, 7176
        fm("w_in_2", l, D, rq, rq + 1024)
        tm("w_in_2", l, D, rv, rv + 1024)
        fm("w_in_2", l, D, mqk, mqk + 1024)
        tm("w_in_2", l, D, mv, mv + 1024)
        fm("w_in_2", l, D, rg, rg + 1024)
        for c in range(0, D, 256):
            fm("w_in_2", l, D, ga + c, ga + c + 256)
            fm("w_proj_ret_2", l, D, c, c + 256)
        fm("w_in_2", l, D, mo, mo + 1024)
        for c in range(0, D, 256):
            fm("w_in_2", l, D, gb + c, gb + c + 256)
            fm("w_proj_mlstm_2", l, D, c, c + 256)
        fm("w_out_2", l, D, 0, D)
        for c in range(0, D_FF, 256):
            fm("w_gate_up_2", l, D, c, c + 256)
            fm("w_gate_up_2", l, D, D_FF + c, D_FF + c + 256)
        fm("w_down_2", l, D_FF, 0, D)
    return out


class Queue:

    def __init__(self, sem, engine):
        self.sem, self.engine, self.count, self.passed = sem, engine, 0, {}

    def wait(self, *marks):
        for m in marks:
            if isinstance(m, list):
                self.wait(*m)
            elif m is not None and self.passed.get(m[0].name, 0) < m[1]:
                self.passed[m[0].name] = m[1]
                if self.engine is not None:
                    self.engine.wait_ge(m[0], m[1])

    def do(self, make, *marks, signal=True):
        self.wait(*marks)
        instruction = make(self.engine) if self.engine is not None else None
        if not signal:
            return None
        self.count += 1
        if instruction is not None:
            instruction.then_inc(self.sem, 1)
        return (self.sem, self.count)

    def last(self):
        return (self.sem, self.count) if self.count else None


class Loads:

    def __init__(self, queue, sem):
        self.queue, self.sem, self.count = queue, sem, 0

    def start(self, out, in_, *marks):
        self.queue.wait(*marks)
        self.count += 16
        if self.queue.engine is not None:
            self.queue.engine.dma_start(out, in_).then_inc(self.sem, 16)
        return (self.sem, self.count)


def build(nc, weights, params, tables, x_in, y_out):
    with ExitStack() as ctx:
        banks = [ctx.enter_context(nc.psum_tensor(f"bank{i}", [P, S], F32)) for i in range(8)]
        sems, tensors = {}, {}

        def sem(name):
            if name not in sems:
                sems[name] = ctx.enter_context(nc.semaphore(name))
            return sems[name]

        def at(name, shape, dt, offset):
            if name not in tensors:
                tensors[name] = nc.alloc_sbuf_tensor_at(name, shape, dt, offset=offset)
            return tensors[name]

        def walk(engine, name):
            program(nc, {name: engine}, sem, at, banks, weights, params, tables, x_in, y_out)

        for name in ("pe_done", "act_done", "dve_done"):
            sem(name)
        with nc.Block() as block:
            block.sync(lambda e: walk(e, "sp"))
            block.scalar(lambda e: walk(e, "act"))
            block.vector(lambda e: walk(e, "dve"))
            block.gpsimd(lambda e: walk(e, "pool"))
            block.tensor(lambda e: walk(e, "pe"))


def program(nc, walked, sem, at, bank, weights, params, tables, x_in, y_out):
    units = weight_units()
    pe, act, dve, sp, pool = (Queue(sem(n + "_done"), walked.get(n)) for n in ("pe", "act", "dve", "sp", "pool"))

    K = 1024
    base = -(-nc.sbuf_base // 64) * 64
    at_x = base
    at_h = at_x + 16 * K
    at_big = at_h + 32 * K
    at_scr = at_big + 88 * K
    at_ring = at_big + 96 * K
    at_misc = at_ring + 44 * K
    RAW, HL = 3, 4
    misc = [at_misc]

    def small(name, cols, dt=F32):
        t = at(name, [P, cols], dt, misc[0])
        misc[0] += -(-cols * (2 if dt == BF16 else 4) // 32) * 32
        assert misc[0] <= nc.sbuf_usable_end
        return t

    x = at("x_resid", [P, DT, S], F32, at_x)
    h_hi = at("h_hi", [P, DT, S], F32R, at_h)
    h_lo = at("h_lo", [P, DT, S], F32R, at_h + 16 * K)
    raw = [at(f"w_raw{i}", [P, UNIT], F32, at_ring + 4 * K * i) for i in range(RAW)]
    w_hi = [at(f"w_hi{i}", [P, UNIT], F32R, at_ring + 4 * K * (RAW + i)) for i in range(HL)]
    w_lo = [at(f"w_lo{i}", [P, UNIT], F32R, at_ring + 4 * K * (RAW + HL + i)) for i in range(HL)]
    scr = [at(f"scratch{i}", [P, S], F32, at_scr + 2 * K * i) for i in range(4)]
    par = small("params_sb", N_PARAMS)
    ident = small("ident", P)
    ones = small("ones", P)
    eps = small("eps", 2)
    masks = small("masks_bf16", 15 * P, BF16)
    stats = small("stats", 256)
    scr += [small(f"scratch{4 + i}", S) for i in range(2)]
    r_bc = small("inverse_rms", S)
    diag = small("diagonals", S)

    def p_(name, i=0, n=1):
        return par[:, PARAMS[name][0] + i:PARAMS[name][0] + i + n]

    bank_free = [None] * 8
    scr_free = [None] * 6

    f32 = lambda ap: ap.bitcast(F32)

    table_ap = lambda name: tables[:, TABLES[name][0]:sum(TABLES[name])]
    masks_f32 = at("masks_f32", [P, 15 * P], F32, at_big)
    par_loads, small_loads, mask_loads = (Loads(pool, sem(n)) for n in ("params_in", "ones_in", "masks_in"))
    params_in = par_loads.start(par[:, :], params)
    small_loads.start(ones[:, :], table_ap("ones"))
    small_loads.start(ident[:, :], table_ap("ident"))
    small_in = small_loads.start(eps[:, :], table_ap("eps"))
    masks_in = mask_loads.start(masks_f32[:, :], table_ap("masks"))
    table_loads = Loads(pool, sem("tables_in"))
    ident_bf, causal_bf, causal_t_bf = masks[:, 0:P], masks[:, P:2 * P], masks[:, 2 * P:6 * P]
    dil_bf = lambda kind, part: masks[:, (6 + 3 * kind + part) * P:(7 + 3 * kind + part) * P]

    raw_sem = [sem(f"raw_landed{i}") for i in range(RAW)]
    raw_loads = [Loads(sp, s) for s in raw_sem]
    raw_free, split_done, unit_used = [None] * RAW, {}, {}
    loaded, split = [0], [0]
    offsets = np.cumsum([0] + [u[3] * u[5] * P for u in units]).tolist()

    def load_unit():
        u = loaded[0]
        if u < len(units):
            n = units[u][3] * units[u][5]
            src = weights[offsets[u]:offsets[u + 1]].rearrange("(p c) -> p c", p=P)
            raw_loads[u % RAW].start(raw[u % RAW][:, 0:n], src, raw_free[u % RAW])
            loaded[0] += 1

    def split_unit():
        u = split[0]
        if u < len(units):
            n, r, s = units[u][3] * units[u][5], u % RAW, u % HL
            landed = (raw_sem[r], 16 * (u // RAW + 1))
            used = unit_used.get(u - HL)
            hi = act.do(lambda e: e.activation(w_hi[s][:, 0:n], raw[r][:, 0:n], ACT.Copy), landed, used)
            lo = dve.do(lambda e: e.tensor_tensor(w_lo[s][:, 0:n], raw[r][:, 0:n], f32(w_hi[s][:, 0:n]), ALU.subtract),
                        landed, used, hi)
            raw_free[r] = [hi, lo]
            split_done[u] = [hi, lo]
            split[0] += 1
            load_unit()

    next_unit = [0]

    def take_unit():
        u = next_unit[0]
        next_unit[0] += 1
        while split[0] < min(u + HL, len(units)):
            split_unit()
        pe.wait(split_done[u])
        return u

    x_loads = [Loads(act, sem(f"x_in{f}")) for f in range(DT)]
    x_landed = [x_loads[f].start(x[:, f, :], x_in[:, f, :]) for f in range(DT)]
    for _ in range(RAW):
        load_unit()
    act.wait(params_in, small_in)
    dve.wait(params_in, small_in)
    pe.wait(small_in)

    def gemm_fm(n_tiles, k_tiles, hi, lo, ready, evacuate, tile0=0):
        for panel in range(n_tiles // 2):
            banks = [2 * (gemm_turn[0] % 2), 2 * (gemm_turn[0] % 2) + 1]
            gemm_turn[0] += 1
            kt = 0
            while kt < k_tiles:
                u = take_unit()
                nk = units[u][3]
                wh = w_hi[u % HL][:, 0:nk * 256].rearrange("p (k c) -> p k c", k=nk)
                wl = w_lo[u % HL][:, 0:nk * 256].rearrange("p (k c) -> p k c", k=nk)
                for k in range(nk):
                    pe.wait(ready[kt])
                    for step, (w, a) in enumerate(((wh, hi), (wh, lo), (wl, hi))):
                        for j, b in enumerate(banks):
                            if kt == 0 and step == 0:
                                pe.wait(bank_free[b])
                            end = k == nk - 1 and step == 2
                            mark = pe.do(
                                lambda e, b=b, w=w, a=a, k=k, kt=kt, j=j, step=step: e.matmul(
                                    bank[b][:, :], w[:, k, j * P:(j + 1) * P], a[:, kt, :],
                                    start=kt == 0 and step == 0, stop=kt == k_tiles - 1 and step == 2),
                                signal=end)
                    kt += 1
                unit_used[u] = mark
            for j, b in enumerate(banks):
                evacuate(tile0 + 2 * panel + j, b, mark)

    gemm_turn = [0]

    def gemm_tm(k_tiles, hi, lo, ready, evacuate):
        for panel in range(2):
            for kt0 in range(0, k_tiles, 2):
                u = take_unit()
                wh = w_hi[u % HL][:, :].rearrange("p (k c) -> p k c", k=2)
                wl = w_lo[u % HL][:, :].rearrange("p (k c) -> p k c", k=2)
                for k in range(2):
                    kt = kt0 + k
                    pe.wait(ready[kt])
                    for step, (a, w) in enumerate(((hi, wh), (lo, wh), (hi, wl))):
                        for t in range(TB):
                            if kt == 0 and step == 0:
                                pe.wait(bank_free[t])
                            mark = pe.do(
                                lambda e, t=t, w=w, a=a, k=k, kt=kt, step=step: e.matmul(
                                    bank[t][:, :], a[:, kt, t * P:(t + 1) * P], w[:, k, :],
                                    start=kt == 0 and step == 0, stop=kt == k_tiles - 1 and step == 2),
                                signal=step == 2)
                            if step == 2 and kt == k_tiles - 1:
                                evacuate(t, panel, mark)
                unit_used[u] = mark

    def split_tile(src, hi, lo, *ready):
        m_hi = act.do(lambda e: e.activation(hi, src, ACT.Copy), *ready)
        m_lo = dve.do(lambda e: e.tensor_tensor(lo, src, f32(hi), ALU.subtract), m_hi, *ready)
        return [m_hi, m_lo]

    SUMSQ, SUM, SPREAD = 4, 5, 6

    def square(f, src, *ready):
        t = 4 + f % 2
        return act.do(lambda e: e.activation(scr[t][:, :], src, ACT.Square), scr_free[t], *ready)

    def sum_square(f, squared):
        t = 4 + f % 2
        for tb in range(TB):
            m = pe.do(lambda e: e.matmul(bank[SUMSQ][:, tb:tb + 1], scr[t][:, tb * P:(tb + 1) * P], ones[:, 0:1],
                                         start=f == 0 and tb == 0, stop=f == DT - 1, skip_group_check=True),
                      squared, bank_free[SUMSQ], signal=tb == TB - 1)
        scr_free[t] = m
        return m

    r_col = stats[:, 208:208 + TB]

    def spread_inverse_root(eps_col, sums):
        root = act.do(lambda e: e.activation(r_col, bank[SUMSQ][:, 0:TB], ACT.Sqrt, bias=eps[:, eps_col:eps_col + 1],
                                             scale=1.0 / D), sums, pe.last(), dve.last())
        bank_free[SUMSQ] = root
        inv = dve.do(lambda e: e.reciprocal(r_col, r_col), root)
        for tb in range(TB):
            m = dve.do(lambda e: e.tensor_scalar(diag[:, tb * P:(tb + 1) * P], ident[:, :], r_col[:, tb:tb + 1], None,
                                                 ALU.mult), inv)
        return pe.do(lambda e: e.matmul(bank[SPREAD][:, :], ones[:, :], diag[:, :], start=True, stop=True),
                     m, bank_free[SPREAD])

    def spread_rms(sums):
        spread = spread_inverse_root(0, sums)
        bank_free[SPREAD] = act.do(lambda e: e.activation(r_bc[:, :], bank[SPREAD][:, :], ACT.Copy), spread)
        return bank_free[SPREAD]

    def split_scaled(f, gain, *ready):
        hi = act.do(lambda e: e.activation(h_hi[:, f, :], x[:, f, :], ACT.Copy, scale=p_(gain, f)), *ready)
        lo = dve.do(lambda e: e.scalar_tensor_tensor(h_lo[:, f, :], x[:, f, :], p_(gain, f), f32(h_hi[:, f, :]),
                                                     ALU.mult, ALU.subtract), hi, *ready)
        return [hi, lo]

    def final_rms(gain, sums, *h_free):
        spread = spread_inverse_root(0, sums)
        ready, behind = [], None
        for f in range(DT + 1):
            if f < DT:
                m = dve.do(lambda e: e.scalar_tensor_tensor(x[:, f, :], x[:, f, :], p_(gain, f), bank[SPREAD][:, :],
                                                            ALU.mult, ALU.mult), spread)
                hi = act.do(lambda e: e.activation(h_hi[:, f, :], x[:, f, :], ACT.Copy), m, *h_free)
            if f:
                g = f - 1
                lo = dve.do(lambda e: e.tensor_tensor(h_lo[:, g, :], x[:, g, :], f32(h_hi[:, g, :]), ALU.subtract),
                            behind, *h_free)
                ready.append([behind, lo])
            behind = hi
        bank_free[SPREAD] = m
        return ready

    def layer_norm(gain, shift, res, *h_free):
        for f in range(DT):
            m = dve.do(lambda e: e.scalar_tensor_tensor(x[:, f, :], bank[SUM][:, :], -1.0 / D, x[:, f, :],
                                                        ALU.mult, ALU.add), res.sums, res.ready[f])
            done = sum_square(f, square(f, x[:, f, :], m))
        bank_free[SUM] = m
        spread = spread_inverse_root(1, done)
        ready, behind = [], None
        for f in range(DT + 1):
            if f < DT:
                t = f % 4
                m = dve.do(lambda e: e.scalar_tensor_tensor(scr[t][:, :], x[:, f, :], p_(gain, f), bank[SPREAD][:, :],
                                                            ALU.mult, ALU.mult), spread, scr_free[t])
                hi = act.do(lambda e: e.activation(h_hi[:, f, :], scr[t][:, :], ACT.Identity, bias=p_(shift, f)),
                            m, *h_free)
                xs = act.do(lambda e: e.activation(x[:, f, :], scr[t][:, :], ACT.Identity, bias=p_(shift, f)))
                scr_free[t] = xs
            if f:
                g = f - 1
                lo = dve.do(lambda e: e.tensor_tensor(h_lo[:, g, :], x[:, g, :], f32(h_hi[:, g, :]), ALU.subtract),
                            behind, *h_free)
                ready.append([*behind, lo])
            behind = [hi, xs]
        bank_free[SPREAD] = m
        return ready

    class Residual:

        def __init__(self, scale, mean, gain=None, h_free=None):
            self.scale, self.mean, self.gain, self.h_free = scale, mean, gain, h_free
            self.ready, self.h_ready, self.pending, self.sums = [], [], [], None

        def __call__(self, f, b, mark):
            if f % 2 == 0:
                self.flush()
            m = dve.do(lambda e: e.scalar_tensor_tensor(x[:, f, :], x[:, f, :], self.scale, bank[b][:, :],
                                                        ALU.mult, ALU.add), mark)
            bank_free[b] = m
            self.ready.append(m)
            self.take(f, m)

        def take(self, f, m):
            if self.gain:
                self.h_ready.append(split_scaled(f, self.gain, m, self.h_free))
            self.pending.append((f, m if self.mean else square(f, x[:, f, :], m)))

        def flush(self):
            for f, m in self.pending:
                if self.mean:
                    self.sums = pe.do(lambda e: e.matmul(bank[SUM][:, :], ones[:, :], x[:, f, :],
                                                         start=f == 0, stop=f == DT - 1), m, bank_free[SUM])
                else:
                    self.sums = sum_square(f, m)
            self.pending = []

    swap_sem = [sem(f"halves_swapped{i}") for i in range(2)]
    swaps = [Loads(sp, s) for s in swap_sem]

    class Rope:

        def __init__(self, dst, half, cos, sin, scale, r, tables_ready, *dst_free):
            self.dst, self.half, self.cos, self.sin, self.scale, self.r = dst, half, cos, sin, scale, r
            self.first, self.pending, self.ready = [tables_ready, *dst_free], None, {}

        def __call__(self, f, b, mark):
            i = f % 2
            t, sw = scr[i], scr[2 + i]
            if self.r is None:
                copied = act.do(lambda e: e.activation(t[:, :], bank[b][:, :], ACT.Copy), mark, scr_free[i])
            else:
                copied = dve.do(lambda e: e.scalar_tensor_tensor(t[:, :], bank[b][:, :], self.scale, r_bc[:, :],
                                                                 ALU.mult, ALU.mult), mark, scr_free[i], self.r)
            bank_free[b] = copied
            for p0 in range(0, P, self.half):
                p1 = p0 ^ self.half
                landed = swaps[i].start(sw[p0:p0 + self.half, :], t[p1:p1 + self.half, :], copied, scr_free[2 + i])
            self.flush()
            self.pending = (f, i, copied, landed)

        def flush(self):
            if self.pending:
                f, i, copied, landed = self.pending
                t, sw = scr[i], scr[2 + i]
                a = dve.do(lambda e: e.tensor_tensor(self.dst[:, f, :], t[:, :], self.cos, ALU.mult), copied, *self.first)
                c = dve.do(lambda e: e.tensor_tensor(sw[:, :], sw[:, :], self.sin, ALU.mult), landed)
                m = dve.do(lambda e: e.tensor_tensor(self.dst[:, f, :], self.dst[:, f, :], sw[:, :], ALU.add), a, c)
                scr_free[i], scr_free[2 + i] = [a, landed], m
                self.ready[f] = m
                self.pending = None

    def attention_stage(h_ready, r_ready, differential):
        tag = "d" if differential else "e"
        before = [pe.last(), act.last(), dve.last()]
        q = at(f"q_{tag}", [P, DT, S], F32, at_big)
        k = at(f"k_{tag}", [P, DT, S], F32, at_big + 16 * K)
        o_hi = at(f"o_hi_{tag}", [P, DT, S], F32R, at_big)
        o_lo = at(f"o_lo_{tag}", [P, DT, S], F32R, at_big + 16 * K)
        v = at(f"v_{tag}", [P, TB, D], F32, at_big + 32 * K)
        maps = 2 if differential else 1
        prob = [at(f"prob{i}_{tag}", [P, TRI_N], F32, at_big + (48 + 5 * i) * K) for i in range(2 * maps)]
        prob_t = [at(f"probt{i}_{tag}", [P, TRI_N], F32, at_big + (68 + 5 * i) * K) for i in range(2)]
        rope = at(f"rope_{tag}", [P, 2 * S], F32, at_big + 80 * K)
        rope_in = table_loads.start(rope[:, :], table_ap("rope64"), before)
        both = lambda d, s: Rope(d, HD // 2, rope[:, 0:S], rope[:, S:2 * S], s, r_ready, rope_in, before)
        to_q, to_k = both(q, HD ** -0.5), both(k, 1.0)
        gemm_fm(DT, DT, h_hi, h_lo, h_ready, to_q)
        to_q.flush()
        gemm_fm(DT, DT, h_hi, h_lo, h_ready, to_k)
        to_k.flush()
        v_ready = []

        def keep_v(t, panel, mark):
            dst, r = v[:, t, panel * 512:(panel + 1) * 512], r_col[:, t:t + 1]
            if t % 2:
                bank_free[t] = act.do(lambda e: e.activation(dst, bank[t][:, :], ACT.Copy, scale=r), mark, before, r_ready)
            else:
                bank_free[t] = dve.do(lambda e: e.tensor_scalar(dst, bank[t][:, :], r, None, ALU.mult), mark, before, r_ready)
            v_ready.append(bank_free[t])

        gemm_tm(DT, h_hi, h_lo, h_ready, keep_v)

        turn = {"s": 0, "t": 0}
        prob_free, prob_t_free = [None] * len(prob), [None] * 2
        lam = None
        if differential:
            lv = lambda i: p_("lambdas", i * HD, HD)
            m = []
            for i in range(2):
                m.append(dve.do(lambda e: e.tensor_tensor(scr[4][:, i * HD:(i + 1) * HD], lv(2 * i), lv(2 * i + 1), ALU.mult),
                                scr_free[4]))
            m = dve.do(lambda e: e.tensor_reduce(stats[:, 200:202], scr[4][:, 0:2 * HD].rearrange("p (a b) -> p a b", a=2),
                                                 AX_X, ALU.add), m)
            scr_free[4] = m
            m = act.do(lambda e: e.activation(stats[:, 202:204], stats[:, 200:202], ACT.Exp), m)
            m = dve.do(lambda e: e.tensor_tensor(stats[:, 204:205], stats[:, 203:204], stats[:, 202:203], ALU.subtract), m)
            lam = dve.do(lambda e: e.tensor_scalar(stats[:, 205:206], stats[:, 204:205], -LAMBDA_INIT, None, ALU.add), m)

        def head_rows(n):
            return (n // 2, (n % 2) * HD)

        heads = DT if differential else 2 * DT
        marks, col_free = {}, [None] * 4
        col = lambda m, what, i=0, n=1: stats[:, 32 * (m % 4) + 8 * what + i:32 * (m % 4) + 8 * what + i + n]

        def scores_and_exp(n, c, i):
            m = n * maps + c
            tile, p0 = (n, c * HD) if differential else head_rows(n)
            slot = m % len(prob)
            b, w = turn["s"] % 3, (i + 1) * P
            turn["s"] += 1
            if not differential and n >= DT:
                adds = [(kb, dil_bf(min(i - kb, 2), part)) for kb in range(i + 1) for part in range(3)]
            else:
                adds = [(i, causal_bf)]
            for j, (kb, mask) in enumerate(adds):
                pe.do(lambda e: e.matmul(bank[b][:, kb * P:(kb + 1) * P], ident_bf, mask, start=j == 0, stop=False,
                                         skip_group_check=True), bank_free[b], masks_ready, signal=False)
            s = pe.do(lambda e: e.matmul(
                bank[b][:, 0:w], q[p0:p0 + HD, tile, i * P:(i + 1) * P], k[p0:p0 + HD, tile, 0:w],
                start=False, stop=True, skip_group_check=True), to_q.ready[tile], to_k.ready[tile])
            mx = dve.do(lambda e: e.tensor_reduce(col(m, 0, i), bank[b][:, 0:w], AX_X, ALU.max, negate=True),
                        s, col_free[m % 4])
            ex = act.do(lambda e: e.activation(
                prob[slot][:, TRQ[i]:TRQ[i] + w], bank[b][:, 0:w], ACT.Exp, bias=col(m, 0, i), accum_out=col(m, 1, i)),
                mx, prob_free[slot], before)
            bank_free[b] = ex
            marks["exp", m, i] = ex

        def normalise(n):
            out = []
            for c in range(maps):
                m = n * maps + c
                inv = dve.do(lambda e: e.reciprocal(col(m, 2, 0, TB), col(m, 1, 0, TB)),
                             [marks["exp", m, i] for i in range(TB)])
                if c:
                    inv = dve.do(lambda e: e.tensor_scalar(col(m, 2, 0, TB), col(m, 2, 0, TB), stats[:, 205:206], None,
                                                           ALU.mult), inv, lam)
            m0 = n * maps
            s0 = m0 % len(prob)
            for i in range(TB):
                rows = slice(TRQ[i], TRQ[i] + (i + 1) * P)
                if not differential:
                    out.append(dve.do(lambda e, i=i, rows=rows: e.tensor_scalar(
                        prob[s0][:, rows], prob[s0][:, rows], col(m0, 2, i), None, ALU.mult), inv))
                else:
                    s1 = (m0 + 1) % len(prob)
                    a = dve.do(lambda e, i=i, rows=rows: e.tensor_scalar(
                        prob[s1][:, rows], prob[s1][:, rows], col(m0 + 1, 2, i), None, ALU.mult), inv)
                    out.append(dve.do(lambda e, i=i, rows=rows: e.scalar_tensor_tensor(
                        prob[s0][:, rows], prob[s0][:, rows], col(m0, 2, i), prob[s1][:, rows], ALU.mult, ALU.add), a))
                    prob_free[s1] = out[-1]
            for c in range(maps):
                col_free[(n * maps + c) % 4] = out[-1]
            marks["norm", n] = out

        def transpose(n, kb):
            s0, st = (n * maps) % len(prob), n % 2
            b = 3 + turn["t"] % 3
            turn["t"] += 1
            for i in range(kb, TB):
                src = prob[s0][:, TRQ[i] + kb * P:TRQ[i] + (kb + 1) * P]
                t = pe.do(lambda e: e.transpose(bank[b][:, (i - kb) * P:(i - kb + 1) * P], src, ident[:, :]),
                          marks["norm", n][i], bank_free[b], signal=i == TB - 1)
            w = (TB - kb) * P
            dst = prob_t[st][:, TRI[kb]:TRI[kb] + w]
            if kb % 2 == 0:
                cp = act.do(lambda e: e.activation(dst, bank[b][:, 0:w], ACT.Copy), t, prob_t_free[st], before)
            else:
                cp = dve.do(lambda e: e.tensor_copy(dst, bank[b][:, 0:w]), t, prob_t_free[st], before)
            bank_free[b] = cp
            marks["pt", n, kb] = cp
            prob_free[s0] = t

        def values(n):
            st = n % 2
            if differential:
                b, rows, cols = 6 + n % 2, slice(0, P), slice(n * P, (n + 1) * P)
            else:
                b, rows, cols = 6 + (n // 2) % 2, slice((n % 2) * HD, (n % 2) * HD + HD), slice(n * HD, (n + 1) * HD)
            for kb in reversed(range(TB)):
                o = pe.do(lambda e: e.matmul(
                    bank[b][rows, kb * P:S], v[:, kb, cols], prob_t[st][:, TRI[kb]:TRI[kb] + (TB - kb) * P],
                    start=kb == TB - 1, stop=kb == 0, skip_group_check=True),
                    marks["pt", n, kb], v_ready, bank_free[b], signal=kb == 0)
            prob_t_free[st] = o
            f = n if differential else n // 2
            if differential:
                m = act.do(lambda e: e.activation(q[:, n, :], bank[b][:, :], ACT.Copy), o)
                bank_free[b] = m
                marks["o", f] = m
                marks["o_sq", f] = square(f, q[:, n, :], m)
            elif n % 2:
                hi = act.do(lambda e: e.activation(o_hi[:, f, :], bank[b][:, :], ACT.Copy), o)
                lo = dve.do(lambda e: e.tensor_tensor(o_lo[:, f, :], bank[b][:, :], f32(o_hi[:, f, :]), ALU.subtract), hi)
                bank_free[b] = lo
                marks["o", f] = [hi, lo]

        def head_squares(n):
            t, b = 4 + n % 2, 3 + turn["t"] % 3
            turn["t"] += 1
            for tb in range(TB):
                m = pe.do(lambda e: e.matmul(bank[b][:, tb:tb + 1], scr[t][:, tb * P:(tb + 1) * P], ones[:, 0:1],
                                             start=tb == 0, stop=True, skip_group_check=True),
                          marks["o_sq", n], bank_free[b], signal=tb == TB - 1)
            scr_free[t] = m
            bank_free[b] = marks["ss", n] = dve.do(
                lambda e: e.tensor_copy(stats[:, 128 + TB * n:128 + TB * (n + 1)], bank[b][:, 0:TB]), m)

        for n in range(heads + 3):
            s_items = [(c, i) for c in range(maps) for i in reversed(range(TB))] if n < heads else []
            t_items = list(range(TB)) if 1 <= n <= heads else []
            if t_items:
                normalise(n - 1)
            for c, i in s_items[:3]:
                scores_and_exp(n, c, i)
            s_items = s_items[3:]
            while s_items or t_items:
                if t_items:
                    transpose(n - 1, t_items.pop(0))
                if s_items:
                    scores_and_exp(n, *s_items.pop(0))
            if differential and n >= 3:
                head_squares(n - 3)
            if 2 <= n < heads + 2:
                values(n - 2)
        if not differential:
            return o_hi, o_lo, [marks["o", f] for f in range(DT)]

        gain_m = dve.do(lambda e: e.tensor_scalar(stats[:, 206:207], p_("subln"), 1.0 - LAMBDA_INIT, None, ALU.mult))
        inv_head = stats[:, 128:128 + TB * DT]
        root = act.do(lambda e: e.activation(inv_head, inv_head, ACT.Sqrt, bias=eps[:, 1:2], scale=1.0 / P),
                      [marks["ss", n] for n in range(heads)])
        inv = dve.do(lambda e: e.reciprocal(inv_head, inv_head), root)
        ready, diags, diag_free = [], [diag, scr[2]], [None, scr_free[2]]
        for f in range(DT + 1):
            if f < DT:
                t, b = f % 2, f % 3
                for tb in range(TB):
                    m = dve.do(lambda e: e.tensor_scalar(diags[t][:, tb * P:(tb + 1) * P], ident[:, :],
                                                         inv_head[:, TB * f + tb:TB * f + tb + 1], None, ALU.mult),
                               inv, diag_free[t])
                spread = diag_free[t] = pe.do(lambda e: e.matmul(bank[b][:, :], ones[:, :], diags[t][:, :],
                                                                 start=True, stop=True), m, bank_free[b])
            if f:
                g, t, b = f - 1, (f - 1) % 2, (f - 1) % 3
                y = dve.do(lambda e: e.scalar_tensor_tensor(scr[t][:, :], q[:, g, :], stats[:, 206:207], bank[b][:, :],
                                                            ALU.mult, ALU.mult), behind, gain_m, scr_free[t])
                bank_free[b] = y
                ready.append(split_tile(scr[t][:, :], o_hi[:, g, :], o_lo[:, g, :], y))
                scr_free[t] = ready[-1]
            behind = spread
        scr_free[2] = diag_free[1]
        return o_hi, o_lo, ready

    def causal_conv(dst, src, weight, bias, n_taps, stride, f, *marks_):
        w = lambda tap: p_(weight, tap * stride + f)
        m = act.do(lambda e: e.activation(dst, src, ACT.Identity, bias=p_(bias, f), scale=w(n_taps - 1)), *marks_)
        for back in range(1, n_taps):
            m = dve.do(lambda e: e.scalar_tensor_tensor(dst[:, back:S], src[:, 0:S - back], w(n_taps - 1 - back),
                                                        dst[:, back:S], ALU.mult, ALU.add), m)
        return m

    def ffn(h_ready, r_ready, conv, residual, tag):
        before = [pe.last(), act.last(), dve.last()]
        hid_hi = at(f"hid_hi{tag}", [P, FT, S], F32R, at_big)
        hid_lo = at(f"hid_lo{tag}", [P, FT, S], F32R, at_big + 44 * K)
        gate_ready, hid_ready = {}, [None] * FT

        def convolve(f, channels, b, t, mark):
            u = 4 + f % 2
            m = dve.do(lambda e: e.tensor_tensor(scr[u][:, :], bank[b][:, :], r_bc[:, :], ALU.mult), mark, r_ready, scr_free[u])
            bank_free[b] = m
            scr_free[u] = causal_conv(scr[t][:, :], scr[u][:, :], f"fconv_w{conv}", f"fconv_b{conv}", 3, 2 * FT, channels,
                                      m, scr_free[t])
            return scr_free[u]

        def gate(f, b, mark):
            t = f % 2
            if conv is None:
                m = act.do(lambda e: e.activation(scr[t][:, :], bank[b][:, :], ACT.Silu), mark, scr_free[t])
                bank_free[b] = m
            else:
                m = convolve(f, f, b, t, mark)
                m = act.do(lambda e: e.activation(scr[t][:, :], scr[t][:, :], ACT.Silu), m)
            gate_ready[f] = m

        def value(f, b, mark):
            t, g = 2 + f % 2, f % 2
            if conv is None:
                m = dve.do(lambda e: e.tensor_tensor(scr[t][:, :], bank[b][:, :], scr[g][:, :], ALU.mult),
                           mark, gate_ready[f], scr_free[t])
                bank_free[b] = m
            else:
                m = convolve(f, FT + f, b, t, mark)
                m = dve.do(lambda e: e.tensor_tensor(scr[t][:, :], scr[t][:, :], scr[g][:, :], ALU.mult), m, gate_ready[f])
            scr_free[g] = m
            hid_ready[f] = split_tile(scr[t][:, :], hid_hi[:, f, :], hid_lo[:, f, :], m, before)
            scr_free[t] = hid_ready[f]

        for panel in range(FT // 2):
            gemm_fm(2, DT, h_hi, h_lo, h_ready, gate, 2 * panel)
            gemm_fm(2, DT, h_hi, h_lo, h_ready, value, 2 * panel)
        gemm_fm(DT, FT, hid_hi, hid_lo, hid_ready, residual)
        residual.flush()

    start = Residual(1.0, False, "even_norm")
    for f in range(DT):
        start.take(f, x_landed[f])
        start.flush()
    masks_ready = dve.do(lambda e: e.tensor_copy(masks[:, :], masks_f32[:, :]), masks_in)
    h_ready, sums = start.h_ready, start.sums
    for layer in range(DEPTH):
        r_ready = spread_rms(sums)
        o_hi, o_lo, o_ready = attention_stage(h_ready, r_ready, layer == 1)
        res = Residual(1.0, False, f"ffn_norm{layer}", pe.last())
        gemm_fm(DT, DT, o_hi, o_lo, o_ready, res)
        res.flush()
        r_ready = spread_rms(res.sums)
        last = Residual(1.0, False, None if layer == DEPTH - 1 else "odd_norm")
        ffn(res.h_ready, r_ready, layer, last, f"_{layer}")
        h_ready, sums = last.h_ready, last.sums
    x_ready = final_rms("final_norm", sums, pe.last())

    def recurrent_core(tag, q, k, v, v_cols, weights_t, sm, out, first_marks, q_ready, k_ready, v_ready, prepare):
        done = []
        for h in range(NH2):
            prepared = prepare(h)
            slot = h % 2
            sm_m = []
            for sb in range(TB):
                b, w = sb % 2, (TB - sb) * P
                q_h, k_h, weight = q(h), k(h), weights_t(h, sb)
                s = pe.do(lambda e, b=b, sb=sb, w=w: e.matmul(
                    bank[b][:, 0:w], k_h[:, sb * P:(sb + 1) * P], q_h[:, sb * P:S], start=True, stop=True),
                    q_ready(h), k_ready(h), bank_free[b])
                m = dve.do(lambda e, b=b, sb=sb, w=w: e.scalar_tensor_tensor(
                    sm[slot][:, TRI[sb]:TRI[sb] + w], bank[b][:, 0:w], DK ** -0.5, weight, ALU.mult, ALU.mult),
                    s, prepared, sm_free[slot], first_marks)
                bank_free[b] = m
                sm_m.append(m)
            weights_free[0] = m
            for tb in range(TB):
                b = 4 + tb
                for sb in range(tb + 1):
                    v_h = v(sb, h)
                    o = pe.do(lambda e, b=b, tb=tb, sb=sb: e.matmul(
                        bank[b][:, 0:v_cols], sm[slot][:, TRI[sb] + (tb - sb) * P:TRI[sb] + (tb - sb + 1) * P],
                        v_h, start=sb == 0, stop=sb == tb),
                        sm_m[sb], v_ready, bank_free[b], signal=sb == tb)
                c = h * TB + tb
                row_ = out[:, tb, h * DV:(h + 1) * DV]
                cp = act.do(lambda e: e.activation(row_, bank[b][:, 0:DV], ACT.Copy), o, first_marks)
                bank_free[b] = cp
                if v_cols > DV:
                    bank_free[b] = act.do(lambda e: e.activation(stats[:, 48 + c:49 + c], bank[b][:, DV:DV + 1], ACT.Copy))
                six = stats[:, 224 + 6 * (c % 4):230 + 6 * (c % 4)]
                st = dve.do(lambda e: e.bn_stats(six, row_), cp, six_free[c % 4])
                st = six_free[c % 4] = dve.do(lambda e: e.bn_aggr(stats[:, 2 * c:2 * c + 2], six), st, first_marks)
                done += [st, bank_free[b]]
            sm_free[slot] = o
        return done

    sm_free, weights_free, six_free = [None, None], [None], [None] * 4
    mean_c = lambda c: stats[:, 2 * c:2 * c + 1]
    all_var = stats[:, 0:32].rearrange("p (c two) -> p c two", two=2)[:, :, 1]

    def normalise_heads(out, var_plus, *ready):
        if var_plus is None:
            m = act.do(lambda e: e.activation(stats[:, 32:48], all_var, ACT.Sqrt, bias=eps[:, 1:2]), *ready)
        else:
            m = dve.do(lambda e: e.tensor_tensor(stats[:, 32:48], all_var, var_plus, ALU.add), *ready)
            m = act.do(lambda e: e.activation(stats[:, 32:48], stats[:, 32:48], ACT.Sqrt), m)
        m = dve.do(lambda e: e.reciprocal(stats[:, 32:48], stats[:, 32:48]), m)
        for c in range(NH2 * TB):
            h, tb = c // TB, c % TB
            y = out[:, tb, h * DV:(h + 1) * DV]
            n = dve.do(lambda e, y=y, c=c: e.tensor_scalar(y, y, mean_c(c), stats[:, 32 + c:33 + c],
                                                           ALU.subtract, ALU.mult), m)
        return n

    for layer in range(DEPTH):
        L = str(layer)
        before = [pe.last(), act.last(), dve.last()]
        tm_ret = at("ret_tm" + L, [P, TB, D], F32, at_big)
        tm_ml = at("ml_tm" + L, [P, TB, D], F32, at_big + 16 * K)
        rq = at("rq" + L, [P, NH2, S], F32, at_big + 32 * K)
        rk = at("rk" + L, [P, NH2, S], F32, at_big + 40 * K)
        rv = at("rv" + L, [P, TB, D], F32, at_big + 48 * K)
        rope = at("rope2_" + L, [P, 2 * S], F32, at_big + 28 * K)
        sm_r = [at(f"sm_ret{i}_{L}", [P, TRI_N], F32, at_big + (16 + 5 * i) * K) for i in range(2)]
        decay = at("decay" + L, [P, NH2, S], F32, at_big + 80 * K)
        rope_in = table_loads.start(rope[:, :], table_ap("rope128"), before)
        decay_in = table_loads.start(decay[:, :, :], table_ap("decay"), before)

        class Split2:
            def __init__(self):
                mk = lambda d: Rope(d, DK // 2, rope[:, 0:S], rope[:, S:2 * S], 1.0, None, decay_in, before)
                self.q, self.k = mk(rq), mk(rk)

            def __call__(self, f, b, mark):
                (self.q if f < NH2 else self.k)(f % NH2, b, mark)
                if f == NH2 - 1:
                    self.q.flush()

        rot = Split2()
        gemm_fm(2 * NH2, DT, h_hi, h_lo, x_ready, rot)
        rot.k.flush()
        rv_ready = []

        def keep(dst, ready, width):
            def evacuate(t, panel, mark):
                for j in range(2):
                    d = dst[:, t, (2 * panel + j) * width:(2 * panel + j) * width + DV]
                    s_ = bank[t][:, j * DV:(j + 1) * DV]
                    if t % 2:
                        m = act.do(lambda e: e.activation(d, s_, ACT.Copy), mark, before2[0])
                    else:
                        m = dve.do(lambda e: e.tensor_copy(d, s_), mark, before2[0])
                bank_free[t] = m
                ready.append(m)
            return evacuate

        before2 = [before]
        gemm_tm(DT, h_hi, h_lo, x_ready, keep(rv, rv_ready, DV))
        ret_done = recurrent_core(
            "r", lambda h: rq[:, h, :], lambda h: rk[:, h, :], lambda sb, h: rv[:, sb, h * DV:(h + 1) * DV], DV,
            lambda h, sb: decay[:, h, 0:S - sb * P], sm_r, tm_ret, before,
            lambda h: rot.q.ready[h], lambda h: rot.k.ready[h], rv_ready, lambda h: decay_in)
        ret_normed = normalise_heads(tm_ret, None, ret_done)

        before = [pe.last(), act.last(), dve.last()]
        before2[0] = before
        mqk = at("mqk" + L, [P, DT, S], F32, at_big + 64 * K)
        mv = at("mv" + L, [P, TB, NH2 * (DV + 1)], F32, at_big + 32 * K)
        sm_m = [at(f"sm_ml{i}_{L}", [P, TRI_N], F32, at_big + 48 * K + 512 + 5 * K * i) for i in range(2)]
        gates_t = at("gates_t" + L, [P, TRI_N], F32, at_big + 58 * K + 512)
        row = [at(f"row{i}_{L}", [NH2, S], F32, at_big + (80 + 2 * i) * K) for i in range(4)]
        select = scr[5][0:NH2, :]
        select_in = table_loads.start(select, table_ap("select")[0:NH2, :], before, scr_free[5])
        mqk_ready = {}

        def to_mqk(f, b, mark):
            t = f % 2
            m = causal_conv(scr[t][:, :], bank[b][:, :], "mconv_w" + L, "mconv_b" + L, 4, DT, f, mark, scr_free[t])
            bank_free[b] = m
            mqk_ready[f] = scr_free[t] = act.do(lambda e: e.activation(mqk[:, f, :], scr[t][:, :], ACT.Silu), m, before)

        gemm_fm(DT, DT, h_hi, h_lo, x_ready, to_mqk)
        mv_heads = mv[:, :, :].rearrange("p t (h c) -> p t h c", h=NH2)
        mv_ready = [dve.do(lambda e: e.memset(mv_heads[:, :, :, DV], 1.0), before)]
        gemm_tm(DT, h_hi, h_lo, x_ready, keep(mv, mv_ready, DV + 1))

        GB = 7
        for kt in range(DT):
            g = pe.do(lambda e, kt=kt: e.matmul(bank[GB][0:36, :], p_("w_if" + L, kt * 36, 36), x[:, kt, :],
                                                start=kt == 0, stop=kt == DT - 1), bank_free[GB], x_ready[kt],
                      signal=kt == DT - 1)
        z, lf, a_row, big_f = row
        R = slice(0, NH2)
        tmp = scr[4][R, :]
        bi, bf = (par[R, PARAMS[n + L][0]:PARAMS[n + L][0] + 1] for n in ("b_i", "b_f"))
        i_m = act.do(lambda e: e.activation(a_row[R, :], bank[GB][R, :], ACT.Identity, bias=bi), g, before)
        z_m = act.do(lambda e: e.activation(z[R, :], bank[GB][32:36, :], ACT.Identity, bias=bf), g)
        bank_free[GB] = z_m
        m = dve.do(lambda e: e.scalar_tensor_tensor(tmp, z[R, :], -1.0, z[R, :], ALU.mult, ALU.min), z_m, scr_free[4])
        m = act.do(lambda e: e.activation(tmp, tmp, ACT.Exp), m)
        m = act.do(lambda e: e.activation(tmp, tmp, ACT.Ln, bias=ones[R, 0:1]), m)
        m = dve.do(lambda e: e.scalar_tensor_tensor(lf[R, :], z[R, :], 0.0, tmp, ALU.min, ALU.subtract), m)
        zero = dve.do(lambda e: e.memset(z[R, :], 0.0), m)
        m = dve.do(lambda e: e.tensor_tensor_scan(big_f[R, :], lf[R, :], z[R, :], 0.0, ALU.add, ALU.add), m, zero)
        m = dve.do(lambda e: e.tensor_tensor(a_row[R, :], a_row[R, :], big_f[R, :], ALU.subtract), m, i_m)
        a_m = m
        m = dve.do(lambda e: e.tensor_tensor_scan(lf[R, :], a_row[R, :], a_row[R, :], 0.0, ALU.max, ALU.max), m)
        mm = m
        m = dve.do(lambda e: e.tensor_scalar(lf[R, :], lf[R, :], -1.0, None, ALU.mult), mm)
        nm_m = m
        m = dve.do(lambda e: e.tensor_tensor(z[R, :], lf[R, :], big_f[R, :], ALU.subtract), m)
        for tb in range(TB):
            t1 = pe.do(lambda e, tb=tb: e.transpose(bank[6][:, tb * 4:tb * 4 + 4], a_row[R, tb * P:(tb + 1) * P],
                                                    ident[R, R]), a_m, bank_free[6])
        for tb in range(TB):
            t1 = pe.do(lambda e, tb=tb: e.transpose(bank[6][:, 16 + tb * 4:20 + tb * 4], z[R, tb * P:(tb + 1) * P],
                                                    ident[R, R]), m)
        a_cols = dve.do(lambda e: e.tensor_copy(stats[:, 64:80], bank[6][:, 0:16]), t1)
        floor_m = act.do(lambda e: e.activation(stats[:, 80:96].rearrange("p (h t) -> p t h", h=NH2),
                                                bank[6][:, 16:32].rearrange("p (t h) -> p t h", t=TB), ACT.Exp), a_cols)
        bank_free[6] = floor_m
        scr_free[4] = m

        def prepare(h):
            out_ = []
            for b in (2, 3):
                m = pe.do(lambda e, b=b: e.matmul(bank[b][:, :], select[:, h * P:(h + 1) * P], lf[R, :],
                                                  start=True, stop=b == 2), nm_m, select_in, bank_free[b])
            m2 = pe.do(lambda e: e.matmul(bank[3][:, :], ident_bf, causal_t_bf, start=False, stop=True))
            for sb in range(TB):
                bias = stats[:, 64 + sb * NH2 + h:65 + sb * NH2 + h]
                c0, w = sb * P, (TB - sb - 1) * P
                g_ = act.do(lambda e, sb=sb, bias=bias, c0=c0: e.activation(
                    gates_t[:, TRI[sb]:TRI[sb] + P], bank[3][:, c0:c0 + P], ACT.Exp, bias=bias),
                    m2, a_cols, weights_free[0], before)
                if w:
                    g_ = act.do(lambda e, sb=sb, bias=bias, c0=c0, w=w: e.activation(
                        gates_t[:, TRI[sb] + P:TRI[sb] + P + w], bank[2][:, c0 + P:S], ACT.Exp, bias=bias))
            bank_free[2] = bank_free[3] = g_
            scr_free[5] = m2
            return g_

        ml_done = recurrent_core(
            "m", lambda h: mqk[:, h, :], lambda h: mqk[:, NH2 + h, :],
            lambda sb, h: mv[:, sb, h * (DV + 1):(h + 1) * (DV + 1)], DV + 1,
            lambda h, sb: gates_t[:, TRI[sb]:TRI[sb] + (TB - sb) * P], sm_m, tm_ml, [before, ret_normed],
            lambda h: mqk_ready[h], lambda h: mqk_ready[NH2 + h], mv_ready, prepare)
        den = stats[:, 48:64]
        m = dve.do(lambda e: e.scalar_tensor_tensor(stats[:, 96:112], den, -1.0, den, ALU.mult, ALU.max), ml_done)
        m = dve.do(lambda e: e.tensor_tensor(den, stats[:, 96:112], stats[:, 80:96], ALU.max), m, floor_m)
        m = dve.do(lambda e: e.scalar_tensor_tensor(stats[:, 96:112], den, 1e-5, den, ALU.mult, ALU.mult), m)
        ml_normed = normalise_heads(tm_ml, stats[:, 96:112], m)

        before = [pe.last(), act.last(), dve.last()]
        z_hi = at("z_hi" + L, [P, DT, S], F32R, at_big + 32 * K)
        z_lo = at("z_lo" + L, [P, DT, S], F32R, at_big + 48 * K)
        y_ret = at("y_ret" + L, [P, DT, S], F32, at_big + 64 * K)
        mix_hi = at("mix_hi" + L, [P, DT, S], F32R, at_big)
        mix_lo = at("mix_lo" + L, [P, DT, S], F32R, at_big + 16 * K)

        def gated(tm, func, gain, normed, z_free):
            ready = []

            def evacuate(f, b, mark):
                t, g_, tb_ = f % 2, 2 + f % 2, 4 + f % 2
                gm = act.do(lambda e: e.activation(scr[g_][:, :], bank[b][:, :], func), mark, scr_free[g_])
                bank_free[b] = gm
                for i in range(TB):
                    tr = pe.do(lambda e, i=i: e.transpose(bank[tb_][:, i * P:(i + 1) * P], tm[:, i, f * P:(f + 1) * P],
                                                          ident[:, :]), normed, bank_free[tb_], signal=i == TB - 1)
                m = dve.do(lambda e: e.scalar_tensor_tensor(scr[t][:, :], bank[tb_][:, :], p_(gain + L, f), scr[g_][:, :],
                                                            ALU.mult, ALU.mult), gm, tr, scr_free[t])
                bank_free[tb_] = scr_free[g_] = m
                ready.append(split_tile(scr[t][:, :], z_hi[:, f, :], z_lo[:, f, :], m, z_free))
                scr_free[t] = ready[-1]
            return ready, evacuate

        z_ready, to_z = gated(tm_ret, ACT.Silu, "ret_g", ret_normed, before)
        gemm_fm(DT, DT, h_hi, h_lo, x_ready, to_z)
        gate_m, yr_ready, mix_ready = {}, {}, []

        def merge_gate(which):
            def evacuate(f, b, mark):
                t = f % 2
                gate_m[f] = act.do(lambda e: e.activation(scr[t][:, :], bank[b][:, :], ACT.Sigmoid,
                                                          bias=p_("b_merge" + L, which * DT + f)), mark, scr_free[t])
                bank_free[b] = gate_m[f]
            return evacuate

        def gate_ret(f, b, mark):
            m = dve.do(lambda e: e.tensor_tensor(y_ret[:, f, :], bank[b][:, :], scr[f % 2][:, :], ALU.mult),
                       mark, gate_m[f], before)
            bank_free[b] = scr_free[f % 2] = yr_ready[f] = m

        def gate_ml(f, b, mark):
            t = 2 + f % 2
            m = dve.do(lambda e: e.tensor_tensor(scr[t][:, :], bank[b][:, :], scr[f % 2][:, :], ALU.mult),
                       mark, gate_m[f], scr_free[t])
            bank_free[b] = scr_free[f % 2] = m
            m = dve.do(lambda e: e.tensor_tensor(scr[t][:, :], scr[t][:, :], y_ret[:, f, :], ALU.add), m, yr_ready[f])
            mix_ready.append(split_tile(scr[t][:, :], mix_hi[:, f, :], mix_lo[:, f, :], m, tm_free))
            scr_free[t] = mix_ready[-1]

        for panel in range(DT // 2):
            gemm_fm(2, DT, h_hi, h_lo, x_ready, merge_gate(0), 2 * panel)
            gemm_fm(2, DT, z_hi, z_lo, z_ready, gate_ret, 2 * panel)
        z_ready, to_z = gated(tm_ml, ACT.Sigmoid, "ml_g", ml_normed, pe.last())
        gemm_fm(DT, DT, h_hi, h_lo, x_ready, to_z)
        tm_free = pe.last()
        for panel in range(DT // 2):
            gemm_fm(2, DT, h_hi, h_lo, x_ready, merge_gate(1), 2 * panel)
            gemm_fm(2, DT, z_hi, z_lo, z_ready, gate_ml, 2 * panel)
        res = Residual(ALPHA, True)
        gemm_fm(DT, DT, mix_hi, mix_lo, mix_ready, res)
        res.flush()
        x_ready = layer_norm("ln1_g" + L, "ln1_b" + L, res, pe.last())
        res = Residual(ALPHA, True)
        ffn(x_ready, None, None, res, f"_{2 + layer}")
        x_ready = layer_norm("ln2_g" + L, "ln2_b" + L, res, pe.last())

    stores = Loads(sp, sem("y_stored"))
    for f in range(DT):
        stored = stores.start(y_out[:, f, :], x[:, f, :], x_ready[f])
    sp.wait(stored)

    assert next_unit[0] == len(units)


def shape_tables():
    t = np.zeros((P, N_TABLES), np.float32)

    def put(name, a):
        t[:, TABLES[name][0]:sum(TABLES[name])] = a

    i, j = np.arange(P)[:, None], np.arange(P)[None, :]
    eye = np.eye(P, dtype=np.float32)
    neg = np.float32(-(2.0 ** 99))
    masks = [eye, np.where(j <= i, 0, neg)] + [np.where(i <= j, 0, neg)] * TB
    top = lambda a: (a.view(np.uint32) & np.uint32(0xFFFF0000)).view(np.float32)
    for kind in range(3):
        dist = P * kind + i - j
        count = np.where(dist >= 0, (dist <= 128).astype(int) + (dist % 4 == 0) + (dist % 16 == 0), 0)
        ln = np.where(count > 0, np.log(np.maximum(count, 1)), neg).astype(np.float32)
        a = top(ln.copy())
        b = top((ln - a).astype(np.float32))
        masks += [a, b, (ln - a - b).astype(np.float32)]
    put("masks", np.concatenate(masks, 1))
    put("ident", eye)
    put("ones", 1.0)
    put("eps", np.array([[1e-6, 1e-5]]))
    pos = np.arange(S, dtype=np.float32)

    def rope(inv, half):
        ang = (pos[None, :] * inv[:, None]).astype(np.float32).astype(np.float64)
        cos, sin = np.cos(ang), np.sin(ang)
        n = P // (2 * half)
        return np.concatenate([np.tile(cos, (2 * n, 1)), np.tile(np.concatenate([-sin, sin]), (n, 1))], 1)

    put("rope64", rope((1.0 / 10000.0 ** (np.arange(32, dtype=np.float32) * 2.0 / 64)).astype(np.float32), 32))
    put("rope128", rope((10000.0 ** (-np.arange(64, dtype=np.float32) / 64)).astype(np.float32), 64))
    rel = np.arange(S)[None, :] - np.arange(P)[:, None]
    lg = np.log(1.0 - 2.0 ** (-5.0 - np.arange(NH2)))
    put("decay", np.concatenate([np.where(rel >= 0, np.exp(g * np.maximum(rel, 0)), 0) for g in lg], 1))
    sel = np.zeros((P, NH2 * P))
    for h in range(NH2):
        sel[h, h * P:(h + 1) * P] = 1
    put("select", sel)
    return t


def kernel(**inputs):
    import concourse.bacc as _bacc
    from concourse.bass_utils import run_bass_kernel_spmd as _run

    a = {k: np.asarray(v) for k, v in inputs.items()}

    pieces = []
    for name, layer, k0, nk, c, w in weight_units():
        m = a[name][layer][k0 * P:(k0 + nk) * P, c:c + w]
        pieces.append(m.reshape(nk, P, w).transpose(1, 0, 2).reshape(-1))
    weights = np.concatenate(pieces)

    params = np.zeros((P, N_PARAMS), np.float32)

    def put(name, v):
        params[:, PARAMS[name][0]:sum(PARAMS[name])] = v

    tiles = lambda v: v.reshape(-1, P).T
    put("even_norm", tiles(a["even_norm"][0]))
    put("odd_norm", tiles(a["odd_norm"][0]))
    put("final_norm", tiles(a["final_norm"]))
    put("subln", tiles(a["odd_subln"][0]))
    put("lambdas", np.concatenate([a["odd_lambda_" + n][0] for n in ("q1", "k1", "q2", "k2")])[None, :])
    for l in range(2):
        L = str(l)
        put("ffn_norm" + L, tiles(a["ffn_norm"][l]))
        put("fconv_w" + L, tiles(a["ffn_conv_w"][l].reshape(-1)))
        put("fconv_b" + L, tiles(a["ffn_conv_b"][l]))
        w_if = np.zeros((D, 36), np.float32)
        w_if[:, 0:4] = a["w_in_2"][l][:, 6144:6148]
        w_if[:, 32:36] = a["w_in_2"][l][:, 6148:6152]
        put("w_if" + L, w_if.reshape(DT, P, 36).transpose(1, 0, 2).reshape(P, -1))
        params[0:4, PARAMS["b_i" + L][0]] = a["b_if_2"][l][0:4]
        params[0:4, PARAMS["b_f" + L][0]] = a["b_if_2"][l][4:8]
        put("b_merge" + L, tiles(a["b_merge_2"][l]))
        put("mconv_w" + L, tiles(a["conv_w_2"][l].reshape(-1)))
        put("mconv_b" + L, tiles(a["conv_b_2"][l]))
        for n, src in (("ret_g", "ret_norm_g_2"), ("ml_g", "mlstm_norm_g_2"), ("ln1_g", "ln1_g_2"), ("ln1_b", "ln1_b_2"),
                       ("ln2_g", "ln2_g_2"), ("ln2_b", "ln2_b_2")):
            put(n + L, tiles(a[src][l]))

    x_fm = np.ascontiguousarray(a["x"][0].T.reshape(DT, P, S).transpose(1, 0, 2))
    arrays = {"weights": weights, "params": params, "tables": shape_tables(), "x_fm": x_fm}

    nc = _bacc.Bacc("TRN2", target_bir_lowering=False, num_devices=1)
    args = [nc.dram_tensor(n, v.shape, F32, kind="ExternalInput").ap() for n, v in arrays.items()]
    out = nc.dram_tensor("y_fm", (P, DT, S), F32, kind="ExternalOutput").ap()
    build(nc, *args, out)
    r = _run(nc, [arrays], core_ids=[0])
    y = np.asarray(r.results[0]["y_fm"])
    return np.ascontiguousarray(y.transpose(2, 1, 0).reshape(1, S, D))
```

```python
import math
from contextlib import ExitStack

import numpy as np

import concourse.bass as bass
from concourse import mybir
from concourse.alu_op_type import AluOpType as ALU

F32 = mybir.dt.float32
F32R = mybir.dt.float32r
BF16 = mybir.dt.bfloat16
ACT = mybir.ActivationFunctionType
AX_X = mybir.AxisListType.X

P = 128
S = 512
D = 1024
DT = D // P
TB = S // P
D_FF = 2816
FT = D_FF // P
UNIT = 1024
BIG_NEG = -1e30
HD = 64
DK, DV, NH2 = 128, 256, 4
DEPTH = 2
ALPHA = (2 * DEPTH) ** 0.25
LAMBDA_INIT = 0.8 - 0.6 * math.exp(-0.3 * 1)
TRI = [sum((TB - j) * P for j in range(b)) for b in range(TB)]
TRQ = [sum((j + 1) * P for j in range(b)) for b in range(TB)]
TRI_N = TB * (TB + 1) // 2 * P


def columns(sizes):
    at, out = 0, {}
    for name, n in sizes:
        out[name] = (at, n)
        at += n
    return out, at


PARAMS, N_PARAMS = columns(
    [("even_norm", DT), ("odd_norm", DT), ("ffn_norm0", DT), ("ffn_norm1", DT), ("final_norm", DT), ("subln", 1)]
    + [(f"{n}{l}", c) for l in range(2) for n, c in (
        ("fconv_w", 3 * 2 * FT), ("fconv_b", 2 * FT))]
    + [("lambdas", 4 * HD)]
    + [(f"{n}{l}", c) for l in range(2) for n, c in (
        ("w_if", DT * 36), ("b_i", 1), ("b_f", 1), ("b_merge", 2 * DT), ("mconv_w", 4 * DT), ("mconv_b", DT),
        ("ret_g", DT), ("ml_g", DT), ("ln1_g", DT), ("ln1_b", DT), ("ln2_g", DT), ("ln2_b", DT))]
)
TABLES, N_TABLES = columns([
    ("masks", 15 * P),
    ("ident", P), ("ones", P), ("eps", 2),
    ("rope64", 2 * S), ("rope128", 2 * S), ("decay", NH2 * S), ("select", NH2 * P),
])


def weight_units():
    out = []

    def fm(name, layer, k, c0, c1):
        for c in range(c0, c1, 256):
            for k0 in range(0, k // P, 4):
                out.append((name, layer, k0, min(4, k // P - k0), c, 256))

    def tm(name, layer, k, c0, c1):
        for c in range(c0, c1, 512):
            for k0 in range(0, k // P, 2):
                out.append((name, layer, k0, 2, c, 512))

    def ffn(layer):
        for c in range(0, D_FF, 256):
            fm("ffn_w_up", layer, D, c, c + 256)
            fm("ffn_w_up", layer, D, D_FF + c, D_FF + c + 256)
        fm("ffn_w_down", layer, D_FF, 0, D)

    fm("even_w_in", 0, D, 0, 2 * D)
    tm("even_w_in", 0, D, 2 * D, 3 * D)
    fm("even_w_out", 0, D, 0, D)
    ffn(0)
    fm("odd_w_qkv", 0, D, 0, 2 * D)
    tm("odd_w_qkv", 0, D, 2 * D, 3 * D)
    fm("odd_w_out", 0, D, 0, D)
    ffn(1)
    for l in range(2):
        rq, rv, rg, mqk, mv, mo, ga, gb = 0, 1024, 2048, 3072, 4096, 5120, 6152, 7176
        fm("w_in_2", l, D, rq, rq + 1024)
        tm("w_in_2", l, D, rv, rv + 1024)
        fm("w_in_2", l, D, mqk, mqk + 1024)
        tm("w_in_2", l, D, mv, mv + 1024)
        fm("w_in_2", l, D, rg, rg + 1024)
        for c in range(0, D, 256):
            fm("w_in_2", l, D, ga + c, ga + c + 256)
            fm("w_proj_ret_2", l, D, c, c + 256)
        fm("w_in_2", l, D, mo, mo + 1024)
        for c in range(0, D, 256):
            fm("w_in_2", l, D, gb + c, gb + c + 256)
            fm("w_proj_mlstm_2", l, D, c, c + 256)
        fm("w_out_2", l, D, 0, D)
        for c in range(0, D_FF, 256):
            fm("w_gate_up_2", l, D, c, c + 256)
            fm("w_gate_up_2", l, D, D_FF + c, D_FF + c + 256)
        fm("w_down_2", l, D_FF, 0, D)
    return out


class Queue:

    def __init__(self, sem, engine):
        self.sem, self.engine, self.count, self.passed = sem, engine, 0, {}

    def wait(self, *marks):
        for m in marks:
            if isinstance(m, list):
                self.wait(*m)
            elif m is not None and self.passed.get(m[0].name, 0) < m[1]:
                self.passed[m[0].name] = m[1]
                if self.engine is not None:
                    self.engine.wait_ge(m[0], m[1])

    def do(self, make, *marks, signal=True):
        self.wait(*marks)
        instruction = make(self.engine) if self.engine is not None else None
        if not signal:
            return None
        self.count += 1
        if instruction is not None:
            instruction.then_inc(self.sem, 1)
        return (self.sem, self.count)

    def last(self):
        return (self.sem, self.count) if self.count else None


class Loads:

    def __init__(self, queue, sem):
        self.queue, self.sem, self.count = queue, sem, 0

    def start(self, out, in_, *marks):
        self.queue.wait(*marks)
        self.count += 16
        if self.queue.engine is not None:
            self.queue.engine.dma_start(out, in_).then_inc(self.sem, 16)
        return (self.sem, self.count)


def in_turn(jobs):
    jobs = [j for j in jobs if j is not None]
    while jobs:
        jobs = [j for j in jobs if next(j, "done") != "done"]


def build(nc, weights, params, tables, x_in, y_out):
    with ExitStack() as ctx:
        banks = [ctx.enter_context(nc.psum_tensor(f"bank{i}", [P, S], F32)) for i in range(8)]
        sems, tensors = {}, {}

        def sem(name):
            if name not in sems:
                sems[name] = ctx.enter_context(nc.semaphore(name))
            return sems[name]

        def at(name, shape, dt, offset):
            if name not in tensors:
                tensors[name] = nc.alloc_sbuf_tensor_at(name, shape, dt, offset=offset)
            return tensors[name]

        def walk(engine, name):
            program(nc, {name: engine}, sem, at, banks, weights, params, tables, x_in, y_out)

        for name in ("pe_done", "act_done", "dve_done"):
            sem(name)
        with nc.Block() as block:
            block.sync(lambda e: walk(e, "sp"))
            block.scalar(lambda e: walk(e, "act"))
            block.vector(lambda e: walk(e, "dve"))
            block.gpsimd(lambda e: walk(e, "pool"))
            block.tensor(lambda e: walk(e, "pe"))


def program(nc, walked, sem, at, bank, weights, params, tables, x_in, y_out):
    units = weight_units()
    pe, act, dve, sp, pool = (Queue(sem(n + "_done"), walked.get(n)) for n in ("pe", "act", "dve", "sp", "pool"))

    K = 1024
    base = -(-nc.sbuf_base // 64) * 64
    at_x = base
    at_h = at_x + 16 * K
    at_big = at_h + 32 * K
    at_scr = at_big + 88 * K
    at_ring = at_big + 96 * K
    at_misc = at_ring + 44 * K
    RAW, HL = 3, 4
    misc = [at_misc]

    def small(name, cols, dt=F32):
        t = at(name, [P, cols], dt, misc[0])
        misc[0] += -(-cols * (2 if dt == BF16 else 4) // 32) * 32
        assert misc[0] <= nc.sbuf_usable_end
        return t

    x = at("x_resid", [P, DT, S], F32, at_x)
    h_hi = at("h_hi", [P, DT, S], F32R, at_h)
    h_lo = at("h_lo", [P, DT, S], F32R, at_h + 16 * K)
    raw = [at(f"w_raw{i}", [P, UNIT], F32, at_ring + 4 * K * i) for i in range(RAW)]
    w_hi = [at(f"w_hi{i}", [P, UNIT], F32R, at_ring + 4 * K * (RAW + i)) for i in range(HL)]
    w_lo = [at(f"w_lo{i}", [P, UNIT], F32R, at_ring + 4 * K * (RAW + HL + i)) for i in range(HL)]
    scr = [at(f"scratch{i}", [P, S], F32, at_scr + 2 * K * i) for i in range(4)]
    par = small("params_sb", N_PARAMS)
    ident = small("ident", P)
    ones = small("ones", P)
    eps = small("eps", 2)
    masks = small("masks_bf16", 15 * P, BF16)
    stats = small("stats", 256)
    scr += [small(f"scratch{4 + i}", S) for i in range(2)]
    r_bc = small("inverse_rms", S)
    diag = small("diagonals", S)

    def p_(name, i=0, n=1):
        return par[:, PARAMS[name][0] + i:PARAMS[name][0] + i + n]

    bank_free = [None] * 8
    scr_free = [None] * 6

    f32 = lambda ap: ap.bitcast(F32)

    table_ap = lambda name: tables[:, TABLES[name][0]:sum(TABLES[name])]
    masks_f32 = at("masks_f32", [P, 15 * P], F32, at_big)
    par_loads, small_loads, mask_loads = (Loads(pool, sem(n)) for n in ("params_in", "ones_in", "masks_in"))
    gains = PARAMS["subln"][0]
    gains_in = Loads(pool, sem("gains_in")).start(par[:, 0:gains], params[:, 0:gains])
    params_in = par_loads.start(par[:, gains:], params[:, gains:])
    small_loads.start(ones[:, :], table_ap("ones"))
    small_loads.start(ident[:, :], table_ap("ident"))
    small_in = small_loads.start(eps[:, :], table_ap("eps"))
    table_loads = Loads(pool, sem("tables_in"))
    ident_bf, causal_bf, causal_t_bf = masks[:, 0:P], masks[:, P:2 * P], masks[:, 2 * P:6 * P]
    dil_bf = lambda kind, part: masks[:, (6 + 3 * kind + part) * P:(7 + 3 * kind + part) * P]

    raw_sem = [sem(f"raw_landed{i}") for i in range(RAW)]
    raw_loads = [Loads(sp, s) for s in raw_sem]
    raw_free, split_done, unit_used = [None] * RAW, {}, {}
    loaded, split = [0], [0]
    offsets = np.cumsum([0] + [u[3] * u[5] * P for u in units]).tolist()

    def load_unit():
        u = loaded[0]
        if u < len(units):
            n = units[u][3] * units[u][5]
            src = weights[offsets[u]:offsets[u + 1]].rearrange("(p c) -> p c", p=P)
            raw_loads[u % RAW].start(raw[u % RAW][:, 0:n], src, raw_free[u % RAW])
            loaded[0] += 1

    def split_unit():
        u = split[0]
        if u < len(units):
            n, r, s = units[u][3] * units[u][5], u % RAW, u % HL
            landed = (raw_sem[r], 16 * (u // RAW + 1))
            used = unit_used.get(u - HL)
            hi = act.do(lambda e: e.activation(w_hi[s][:, 0:n], raw[r][:, 0:n], ACT.Copy), landed, used)
            lo = dve.do(lambda e: e.tensor_tensor(w_lo[s][:, 0:n], raw[r][:, 0:n], f32(w_hi[s][:, 0:n]), ALU.subtract),
                        landed, used, hi)
            raw_free[r] = [hi, lo]
            split_done[u] = [hi, lo]
            split[0] += 1
            load_unit()

    next_unit = [0]

    def take_unit():
        u = next_unit[0]
        next_unit[0] += 1
        while split[0] < min(u + HL, len(units)):
            split_unit()
        pe.wait(split_done[u])
        return u

    x_loads = [Loads(act, sem(f"x_in{f}")) for f in range(DT)]
    x_landed = [x_loads[f].start(x[:, f, :], x_in[:, f, :]) for f in range(DT)]
    for _ in range(RAW):
        load_unit()
    masks_in = mask_loads.start(masks_f32[:, :], table_ap("masks"), x_landed)
    act.wait(gains_in)
    dve.wait(gains_in)

    def gemm_fm(n_tiles, k_tiles, hi, lo, ready, evacuate, tile0=0, beside=iter(())):
        for panel in range(n_tiles // 2):
            banks = [2 * (gemm_turn[0] % 2), 2 * (gemm_turn[0] % 2) + 1]
            gemm_turn[0] += 1
            kt = 0
            while kt < k_tiles:
                u = take_unit()
                nk = units[u][3]
                wh = w_hi[u % HL][:, 0:nk * 256].rearrange("p (k c) -> p k c", k=nk)
                wl = w_lo[u % HL][:, 0:nk * 256].rearrange("p (k c) -> p k c", k=nk)
                for k in range(nk):
                    pe.wait(ready[kt])
                    for step, (w, a) in enumerate(((wh, hi), (wh, lo), (wl, hi))):
                        for j, b in enumerate(banks):
                            if kt == 0 and step == 0:
                                pe.wait(bank_free[b])
                            end = k == nk - 1 and step == 2
                            mark = pe.do(
                                lambda e, b=b, w=w, a=a, k=k, kt=kt, j=j, step=step: e.matmul(
                                    bank[b][:, :], w[:, k, j * P:(j + 1) * P], a[:, kt, :],
                                    start=kt == 0 and step == 0, stop=kt == k_tiles - 1 and step == 2),
                                signal=end)
                    kt += 1
                unit_used[u] = mark
                in_turn([beside])
            in_turn([evacuate(tile0 + 2 * panel + j, b, mark) for j, b in enumerate(banks)])

    gemm_turn = [0]

    def gemm_tm(k_tiles, hi, lo, ready, evacuate, beside=iter(())):
        for panel in range(2):
            for kt0 in range(0, k_tiles, 2):
                u = take_unit()
                wh = w_hi[u % HL][:, :].rearrange("p (k c) -> p k c", k=2)
                wl = w_lo[u % HL][:, :].rearrange("p (k c) -> p k c", k=2)
                for k in range(2):
                    kt = kt0 + k
                    pe.wait(ready[kt])
                    for step, (a, w) in enumerate(((hi, wh), (lo, wh), (hi, wl))):
                        for t in range(TB):
                            if kt == 0 and step == 0:
                                pe.wait(bank_free[t])
                            mark = pe.do(
                                lambda e, t=t, w=w, a=a, k=k, kt=kt, step=step: e.matmul(
                                    bank[t][:, :], a[:, kt, t * P:(t + 1) * P], w[:, k, :],
                                    start=kt == 0 and step == 0, stop=kt == k_tiles - 1 and step == 2),
                                signal=step == 2)
                            if step == 2 and kt == k_tiles - 1:
                                evacuate(t, panel, mark)
                unit_used[u] = mark
                next(beside, None)
        in_turn([beside])

    def split_tile(src, hi, lo, *ready):
        m_hi = act.do(lambda e: e.activation(hi, src, ACT.Copy), *ready)
        yield
        m_lo = dve.do(lambda e: e.tensor_tensor(lo, src, f32(hi), ALU.subtract), m_hi, *ready)
        return [m_hi, m_lo]

    SUMSQ, SUM, SPREAD = 4, 5, 6
    tally = diag
    tally_free = [None]
    ON_POOL = 6

    def square(f, src, *ready):
        t = 4 + f % 2
        return act.do(lambda e: e.activation(scr[t][:, :], src, ACT.Square), scr_free[t], *ready)

    def sum_square(tile, first, last, squared):
        for tb in range(TB):
            m = pe.do(lambda e: e.matmul(bank[SUMSQ][:, tb:tb + 1], tile[:, tb * P:(tb + 1) * P], ones[:, 0:1],
                                         start=first and tb == 0, stop=last, skip_group_check=True),
                      squared, small_in, bank_free[SUMSQ], signal=tb == TB - 1)
        return m

    r_col = stats[:, 208:208 + TB]

    def diagonal_inverse_root(eps_col, sums):
        root = act.do(lambda e: e.activation(r_col, bank[SUMSQ][:, 0:TB], ACT.Sqrt, bias=eps[:, eps_col:eps_col + 1],
                                             scale=1.0 / D), sums, r_col_free[0])
        bank_free[SUMSQ] = root
        inv = dve.do(lambda e: e.reciprocal(r_col, r_col), root)
        for tb in range(TB):
            m = dve.do(lambda e: e.tensor_scalar(diag[:, tb * P:(tb + 1) * P], ident[:, :], r_col[:, tb:tb + 1], None,
                                                 ALU.mult), inv, tally_free[0])
        return m

    def spread_diagonal(made):
        tally_free[0] = pe.do(lambda e: e.matmul(bank[SPREAD][:, :], ones[:, :], diag[:, :], start=True, stop=True),
                              made, bank_free[SPREAD])
        return tally_free[0]

    r_col_free, r_bc_free = [None], [None]

    class Inverse:

        def __init__(self, residual):
            self.residual, self.made, self.mark = residual, None, None

        def make(self):
            self.residual.flush()
            self.made = diagonal_inverse_root(0, self.residual.sums)

        def beside(self):
            if not self.residual.at_once:
                self.make()
            return
            yield

        def __call__(self):
            if self.mark is None:
                if self.made is None:
                    self.make()
                spread = spread_diagonal(self.made)
                bank_free[SPREAD] = self.mark = act.do(
                    lambda e: e.activation(r_bc[:, :], bank[SPREAD][:, :], ACT.Copy), spread, r_bc_free[0])
            return self.mark

    def final_rms(gain, sums, *h_free):
        spread = spread_diagonal(diagonal_inverse_root(0, sums))
        ready, behind = [], None
        for f in range(DT + 1):
            if f < DT:
                m = dve.do(lambda e: e.scalar_tensor_tensor(x[:, f, :], x[:, f, :], p_(gain, f), bank[SPREAD][:, :],
                                                            ALU.mult, ALU.mult), spread)
                hi = act.do(lambda e: e.activation(h_hi[:, f, :], x[:, f, :], ACT.Copy), m, *h_free)
            if f:
                g = f - 1
                lo = dve.do(lambda e: e.tensor_tensor(h_lo[:, g, :], x[:, g, :], f32(h_hi[:, g, :]), ALU.subtract),
                            behind, *h_free)
                ready.append([behind, lo])
            behind = hi
        bank_free[SPREAD] = m
        return ready

    def layer_norm(gain, shift, res, *h_free):
        squares = scr + [r_bc, tally]
        free = scr_free + [r_bc_free[0], tally_free[0]]
        sq = [None] * DT
        add = lambda queue, a, b, *ready: queue.do(lambda e: e.tensor_tensor(
            squares[a][:, :], squares[a][:, :], squares[b][:, :], ALU.add), *ready)
        for f in range(DT):
            m = dve.do(lambda e: e.scalar_tensor_tensor(x[:, f, :], bank[SUM][:, :], -1.0 / D, x[:, f, :],
                                                        ALU.mult, ALU.add), res.sums, res.ready[f])
            sq[f] = act.do(lambda e: e.activation(squares[f][:, :], x[:, f, :], ACT.Square), m, free[f])
            if f in (1, 2):
                sq[0] = add(pool, 0, f, sq[0], sq[f])
        sq[4] = add(dve, 4, 5, sq[4], sq[5])
        sq[6] = add(dve, 6, 7, sq[6], sq[7])
        for n, f in enumerate((3, 0, 4, 6)):
            done = sum_square(squares[f], n == 0, n == 3, sq[f])
        scr_free[:] = [done] * len(scr)
        r_bc_free[0] = tally_free[0] = done
        bank_free[SUM] = m
        spread = spread_diagonal(diagonal_inverse_root(1, done))
        ready, behind = [], None
        for f in range(DT + 1):
            if f < DT:
                t = f % 4
                m = dve.do(lambda e: e.scalar_tensor_tensor(scr[t][:, :], x[:, f, :], p_(gain, f), bank[SPREAD][:, :],
                                                            ALU.mult, ALU.mult), spread, scr_free[t])
                hi = act.do(lambda e: e.activation(h_hi[:, f, :], scr[t][:, :], ACT.Identity, bias=p_(shift, f)),
                            m, *h_free)
                xs = act.do(lambda e: e.activation(x[:, f, :], scr[t][:, :], ACT.Identity, bias=p_(shift, f)))
            if f:
                g = f - 1
                lo = dve.do(lambda e: e.scalar_tensor_tensor(h_lo[:, g, :], scr[g % 4][:, :], p_(shift, g),
                                                             f32(h_hi[:, g, :]), ALU.add, ALU.subtract),
                            behind, *h_free)
                scr_free[g % 4] = [behind_x, lo]
                ready.append([behind, behind_x, lo])
            behind, behind_x = hi, xs
        bank_free[SPREAD] = m
        return ready

    class Residual:

        def __init__(self, scale, mean, gain=None, h_free=None, at_once=False):
            self.at_once, self.scale, self.mean, self.gain, self.h_free = at_once, scale, mean, gain, h_free
            self.ready, self.h_ready, self.pending, self.sums, self.tallied = [], [None] * DT, [], None, None

        def __call__(self, f, b, mark):
            m = dve.do(lambda e: e.scalar_tensor_tensor(x[:, f, :], x[:, f, :], self.scale, bank[b][:, :],
                                                        ALU.mult, ALU.add), mark)
            bank_free[b] = m
            self.ready.append(m)
            yield
            yield from self.scaled(f, m)
            yield from self.summed(f, m)

        def scaled(self, f, m):
            if self.gain:
                hi = act.do(lambda e: e.activation(h_hi[:, f, :], x[:, f, :], ACT.Copy, scale=p_(self.gain, f)),
                            m, self.h_free)
                yield
                lo = dve.do(lambda e: e.scalar_tensor_tensor(h_lo[:, f, :], x[:, f, :], p_(self.gain, f),
                                                             f32(h_hi[:, f, :]), ALU.mult, ALU.subtract), hi)
                self.h_ready[f] = [hi, lo]

        def summed(self, f, m):
            t = 4 + f % 2
            if self.mean:
                tile = x[:, f, :]
                if f == 1:
                    self.tallied = pool.do(lambda e: e.tensor_tensor(tally[:, :], x[:, 0, :], x[:, 1, :], ALU.add),
                                           m, self.ready[0], tally_free[0])
                elif 1 < f < ON_POOL:
                    self.tallied = pool.do(lambda e: e.tensor_tensor(tally[:, :], tally[:, :], tile, ALU.add),
                                           m, self.tallied)
                elif f >= ON_POOL:
                    self.pending.append((tile, m, None))
            elif f == 0:
                self.tallied = act.do(lambda e: e.activation(tally[:, :], x[:, f, :], ACT.Square), m, tally_free[0])
            else:
                m = square(f, x[:, f, :], m)
                yield
                if f < ON_POOL:
                    self.tallied = scr_free[t] = pool.do(
                        lambda e: e.tensor_tensor(tally[:, :], tally[:, :], scr[t][:, :], ALU.add), m, self.tallied)
                else:
                    self.pending.append((scr[t], m, t))

        def flush(self):
            terms = [(tally[:, :], self.tallied, None)] + self.pending
            for i, (tile, m, t) in enumerate(terms):
                first, last_ = i == 0, i == len(terms) - 1
                if self.mean:
                    self.sums = pe.do(lambda e: e.matmul(bank[SUM][:, :], ones[:, :], tile, start=first, stop=last_),
                                      m, bank_free[SUM])
                else:
                    self.sums = sum_square(tile, first, last_, m)
                    if t:
                        scr_free[t] = self.sums
                if first:
                    tally_free[0] = self.sums

    swap_sem = [sem(f"halves_swapped{i}") for i in range(2)]
    swaps = [Loads(sp, s) for s in swap_sem]

    class Rope:

        def __init__(self, dst, half, cos, sin, scale, r, tables_ready, *dst_free):
            self.dst, self.half, self.cos, self.sin, self.scale, self.r = dst, half, cos, sin, scale, r
            self.first, self.ready = [tables_ready, *dst_free], {}

        def __call__(self, f, b, mark):
            i = f % 2
            t, sw = scr[i], scr[2 + i]
            if self.r is None:
                copied = act.do(lambda e: e.activation(t[:, :], bank[b][:, :], ACT.Copy), mark, scr_free[i])
            else:
                r_mark = self.r()
                copied = dve.do(lambda e: e.scalar_tensor_tensor(t[:, :], bank[b][:, :], self.scale, r_bc[:, :],
                                                                 ALU.mult, ALU.mult), mark, scr_free[i], r_mark)
            bank_free[b] = copied
            yield
            if f % 2 == 0:
                add_swapped()
            for p0 in range(0, P, self.half):
                p1 = p0 ^ self.half
                landed = swaps[i].start(sw[p0:p0 + self.half, :], t[p1:p1 + self.half, :], copied, scr_free[2 + i])
            a = dve.do(lambda e: e.tensor_tensor(self.dst[:, f, :], t[:, :], self.cos, ALU.mult), copied, *self.first)
            scr_free[i] = [a, landed]
            swapped.append((self, f, i, a, landed))

    swapped = []

    def add_swapped():
        for rope_, f, i, a, landed in swapped:
            c = dve.do(lambda e: e.tensor_tensor(scr[2 + i][:, :], scr[2 + i][:, :], rope_.sin, ALU.mult), landed)
            rope_.ready[f] = scr_free[2 + i] = dve.do(
                lambda e: e.tensor_tensor(rope_.dst[:, f, :], rope_.dst[:, f, :], scr[2 + i][:, :], ALU.add), a, c)
        swapped.clear()

    def attention_stage(h_ready, r_ready, differential):
        tag = "d" if differential else "e"
        before = [pe.last(), act.last(), dve.last()]
        q = at(f"q_{tag}", [P, DT, S], F32, at_big)
        k = at(f"k_{tag}", [P, DT, S], F32, at_big + 16 * K)
        o_hi = at(f"o_hi_{tag}", [P, DT, S], F32R, at_big)
        o_lo = at(f"o_lo_{tag}", [P, DT, S], F32R, at_big + 16 * K)
        v = at(f"v_{tag}", [P, TB, D], F32, at_big + 32 * K)
        maps = 2 if differential else 1
        prob = [at(f"prob{i}_{tag}", [P, TRI_N], F32, at_big + (48 + 5 * i) * K) for i in range(2 * maps)]
        prob_t = [at(f"probt{i}_{tag}", [P, TRI_N], F32, at_big + (68 + 5 * i) * K) for i in range(2)]
        rope = at(f"rope_{tag}", [P, 2 * S], F32, at_big + 80 * K)
        rope_in = table_loads.start(rope[:, :], table_ap("rope64"), before)
        both = lambda d, s: Rope(d, HD // 2, rope[:, 0:S], rope[:, S:2 * S], s, r_ready, rope_in, before)
        to_q, to_k = both(q, HD ** -0.5), both(k, 1.0)
        gemm_fm(DT, DT, h_hi, h_lo, h_ready, to_q, beside=r_ready.beside())
        gemm_fm(DT, DT, h_hi, h_lo, h_ready, to_k)
        v_ready = []

        def keep_v(t, panel, mark):
            dst, r = v[:, t, panel * 512:(panel + 1) * 512], r_col[:, t:t + 1]
            if t % 2:
                bank_free[t] = act.do(lambda e: e.activation(dst, bank[t][:, :], ACT.Copy, scale=r), mark, before, r_ready())
            else:
                bank_free[t] = dve.do(lambda e: e.tensor_scalar(dst, bank[t][:, :], r, None, ALU.mult), mark, before, r_ready())
            v_ready.append(bank_free[t])

        turn = {"s": 0, "t": 0}
        prob_free, prob_t_free = [None] * len(prob), [None] * 2
        lam = None
        if differential:
            lv = lambda i: p_("lambdas", i * HD, HD)
            m = []
            for i in range(2):
                m.append(dve.do(lambda e: e.tensor_tensor(scr[4][:, i * HD:(i + 1) * HD], lv(2 * i), lv(2 * i + 1), ALU.mult),
                                scr_free[4]))
            m = dve.do(lambda e: e.tensor_reduce(stats[:, 200:202], scr[4][:, 0:2 * HD].rearrange("p (a b) -> p a b", a=2),
                                                 AX_X, ALU.add), m)
            scr_free[4] = m
            m = act.do(lambda e: e.activation(stats[:, 202:204], stats[:, 200:202], ACT.Exp), m)
            m = dve.do(lambda e: e.tensor_tensor(stats[:, 204:205], stats[:, 203:204], stats[:, 202:203], ALU.subtract), m)
            lam = dve.do(lambda e: e.tensor_scalar(stats[:, 205:206], stats[:, 204:205], -LAMBDA_INIT, None, ALU.add), m)

        def head_rows(n):
            return (n // 2, (n % 2) * HD)

        heads = DT if differential else 2 * DT
        batches = [(0, 3), (3, 6), (6, 8)]
        marks, col_free = {}, [None] * 4
        o_ready = [None] * DT
        col = lambda m, what, i=0, n=1: stats[:, 32 * (m % 4) + 8 * what + i:32 * (m % 4) + 8 * what + i + n]

        def scores_and_exp(n, c, i, score_banks=(0, 1, 2)):
            m = n * maps + c
            tile, p0 = (n, c * HD) if differential else head_rows(n)
            slot = m % len(prob)
            b, w = score_banks[turn["s"] % 3], (i + 1) * P
            turn["s"] += 1
            if not differential and n >= DT:
                adds = [(kb, dil_bf(min(i - kb, 2), part)) for kb in range(i + 1) for part in range(3)]
            else:
                adds = [(i, causal_bf)]
            for j, (kb, mask) in enumerate(adds):
                pe.do(lambda e: e.matmul(bank[b][:, kb * P:(kb + 1) * P], ident_bf, mask, start=j == 0, stop=False,
                                         skip_group_check=True), bank_free[b], masks_ready, signal=False)
            s = pe.do(lambda e: e.matmul(
                bank[b][:, 0:w], q[p0:p0 + HD, tile, i * P:(i + 1) * P], k[p0:p0 + HD, tile, 0:w],
                start=False, stop=True, skip_group_check=True), to_q.ready[tile], to_k.ready[tile])
            mx = dve.do(lambda e: e.tensor_reduce(col(m, 0, i), bank[b][:, 0:w], AX_X, ALU.max, negate=True),
                        s, col_free[m % 4])
            ex = act.do(lambda e: e.activation(
                prob[slot][:, TRQ[i]:TRQ[i] + w], bank[b][:, 0:w], ACT.Exp, bias=col(m, 0, i), accum_out=col(m, 1, i)),
                mx, prob_free[slot], before)
            bank_free[b] = ex
            marks["exp", m, i] = ex

        def inverse_sums(n):
            for c in range(maps):
                m = n * maps + c
                inv = dve.do(lambda e: e.reciprocal(col(m, 2, 0, TB), col(m, 1, 0, TB)),
                             [marks["exp", m, i] for i in range(TB)])
                if c:
                    inv = dve.do(lambda e: e.tensor_scalar(col(m, 2, 0, TB), col(m, 2, 0, TB), stats[:, 205:206], None,
                                                           ALU.mult), inv, lam)
            marks["inv", n] = inv

        def normalise(n, i):
            m0, inv = n * maps, marks["inv", n]
            p0 = prob[m0 % len(prob)][:, TRQ[i]:TRQ[i] + (i + 1) * P]
            if not differential:
                done = dve.do(lambda e: e.tensor_scalar(p0, p0, col(m0, 2, i), None, ALU.mult), inv)
            else:
                s1 = (m0 + 1) % len(prob)
                p1 = prob[s1][:, TRQ[i]:TRQ[i] + (i + 1) * P]
                a = dve.do(lambda e: e.tensor_scalar(p1, p1, col(m0 + 1, 2, i), None, ALU.mult), inv)
                done = prob_free[s1] = dve.do(lambda e: e.scalar_tensor_tensor(p0, p0, col(m0, 2, i), p1, ALU.mult, ALU.add), a)
            for c in range(maps):
                col_free[(m0 + c) % 4] = done
            marks["norm", n, i] = done

        def transpose(n, kb):
            s0, st = (n * maps) % len(prob), n % 2
            b = 3 + turn["t"] % 3
            turn["t"] += 1
            for i in range(kb, TB):
                src = prob[s0][:, TRQ[i] + kb * P:TRQ[i] + (kb + 1) * P]
                t = pe.do(lambda e: e.transpose(bank[b][:, (i - kb) * P:(i - kb + 1) * P], src, ident[:, :]),
                          marks["norm", n, i], bank_free[b], signal=i == TB - 1)
            w = (TB - kb) * P
            dst = prob_t[st][:, TRI[kb]:TRI[kb] + w]
            if kb % 2 == 0:
                cp = act.do(lambda e: e.activation(dst, bank[b][:, 0:w], ACT.Copy), t, prob_t_free[st], before)
            else:
                cp = dve.do(lambda e: e.tensor_copy(dst, bank[b][:, 0:w]), t, prob_t_free[st], before)
            bank_free[b] = cp
            marks["pt", n, kb] = cp
            prob_free[s0] = t

        def values(n, kb):
            st = n % 2
            if differential:
                b, rows, cols = 6 + n % 2, slice(0, P), slice(n * P, (n + 1) * P)
            else:
                b, rows, cols = 6 + (n // 2) % 2, slice((n % 2) * HD, (n % 2) * HD + HD), slice(n * HD, (n + 1) * HD)
            o = pe.do(lambda e: e.matmul(
                bank[b][rows, kb * P:S], v[:, kb, cols], prob_t[st][:, TRI[kb]:TRI[kb] + (TB - kb) * P],
                start=kb == TB - 1, stop=kb == 0, skip_group_check=True),
                marks["pt", n, kb], v_ready, bank_free[b], signal=kb == 0)
            if kb:
                return
            prob_t_free[st] = o
            f = n if differential else n // 2
            if differential:
                m = act.do(lambda e: e.activation(q[:, n, :], bank[b][:, :], ACT.Copy), o)
                bank_free[b] = m
                marks["o_sq", f] = square(f, q[:, n, :], m)
            elif n % 2:
                hi = act.do(lambda e: e.activation(o_hi[:, f, :], bank[b][:, :], ACT.Copy), o)
                lo = dve.do(lambda e: e.tensor_tensor(o_lo[:, f, :], bank[b][:, :], f32(o_hi[:, f, :]), ALU.subtract), hi)
                bank_free[b] = lo
                o_ready[f] = [hi, lo]

        def head_squares(n):
            t, b = 4 + n % 2, 3 + turn["t"] % 3
            turn["t"] += 1
            for tb in range(TB):
                m = pe.do(lambda e: e.matmul(bank[b][:, tb:tb + 1], scr[t][:, tb * P:(tb + 1) * P], ones[:, 0:1],
                                             start=tb == 0, stop=True, skip_group_check=True),
                          marks["o_sq", n], bank_free[b], signal=tb == TB - 1)
            scr_free[t] = m
            bank_free[b] = marks["ss", n] = dve.do(
                lambda e: e.tensor_copy(stats[:, 128 + TB * n:128 + TB * (n + 1)], bank[b][:, 0:TB]), m)

        def finish_heads(f0, f1):
            inv_head = stats[:, 128 + TB * f0:128 + TB * f1]
            root = act.do(lambda e: e.activation(inv_head, inv_head, ACT.Sqrt, bias=eps[:, 1:2], scale=1.0 / P),
                          [marks["ss", n] for n in range(f0, f1)])
            inv = dve.do(lambda e: e.reciprocal(inv_head, inv_head), root)

            def diagonals(f):
                for tb in range(TB):
                    m = dve.do(lambda e: e.tensor_scalar(diags[f % 2][:, tb * P:(tb + 1) * P], ident[:, :],
                                                         stats[:, 128 + TB * f + tb:129 + TB * f + tb], None, ALU.mult),
                               inv, diag_free[f % 2])
                return m

            made = diagonals(f0)
            for f in range(f0, f1):
                yield
                t, b = f % 2, 3 + turn["t"] % 3
                turn["t"] += 1
                spread = diag_free[t] = pe.do(lambda e: e.matmul(bank[b][:, :], ones[:, :], diags[t][:, :],
                                                                 start=True, stop=True), made, bank_free[b])
                if f + 1 < f1:
                    made = diagonals(f + 1)
                y = dve.do(lambda e: e.scalar_tensor_tensor(scr[t][:, :], q[:, f, :], stats[:, 206:207],
                                                            bank[b][:, :], ALU.mult, ALU.mult),
                           spread, gain_m, scr_free[t])
                bank_free[b] = y
                hi = act.do(lambda e: e.activation(o_hi[:, f, :], scr[t][:, :], ACT.Copy), y)
                lo = dve.do(lambda e: e.tensor_tensor(o_lo[:, f, :], scr[t][:, :], f32(o_hi[:, f, :]), ALU.subtract), hi)
                o_ready[f] = scr_free[t] = [hi, lo]
            tally_free[0], scr_free[2] = diag_free

        if differential:
            gain_m = dve.do(lambda e: e.tensor_scalar(stats[:, 206:207], p_("subln"), 1.0 - LAMBDA_INIT, None, ALU.mult))
            diags, diag_free = [diag, scr[2]], [tally_free[0], scr_free[2]]

        early = 1 if differential else 2
        s_steps = lambda n: [(n, c, i) for i in reversed(range(TB)) for c in range(maps)]

        def early_scores():
            add_swapped()
            yield
            for n in range(early):
                for step in s_steps(n):
                    scores_and_exp(*step, score_banks=(4, 5, 6))
                    yield

        gemm_tm(DT, h_hi, h_lo, h_ready, keep_v, early_scores())
        r_col_free[0], r_bc_free[0] = v_ready[-TB:], dve.last()

        finishing = iter(())
        for n in range(1, heads + 3):
            s_items = s_steps(n) if early <= n < heads else []
            if n <= heads:
                inverse_sums(n - 1)
            for kb in reversed(range(TB)):
                if n <= heads:
                    normalise(n - 1, kb)
                for step in s_items[:maps]:
                    scores_and_exp(*step)
                s_items = s_items[maps:]
                if 2 <= n < heads + 2:
                    values(n - 2, kb)
                if n <= heads:
                    transpose(n - 1, kb)
                next(finishing, None)
            if differential and n >= 3:
                head_squares(n - 3)
                if n - 2 == batches[0][1]:
                    in_turn([finishing])
                    finishing = finish_heads(*batches.pop(0))
        if differential:
            next(finishing)
        return o_hi, o_lo, o_ready, finishing

    def causal_conv(dst, src, weight, bias, n_taps, stride, f, *marks_):
        w = lambda tap: p_(weight, tap * stride + f)
        m = act.do(lambda e: e.activation(dst, src, ACT.Identity, bias=p_(bias, f), scale=w(n_taps - 1)), *marks_)
        yield
        for back in range(1, n_taps):
            m = dve.do(lambda e: e.scalar_tensor_tensor(dst[:, back:S], src[:, 0:S - back], w(n_taps - 1 - back),
                                                        dst[:, back:S], ALU.mult, ALU.add), m)
            yield
        return m

    def ffn(h_ready, r_ready, conv, residual, tag):
        before = [pe.last(), act.last(), dve.last()]
        hid_hi = at(f"hid_hi{tag}", [P, FT, S], F32R, at_big)
        hid_lo = at(f"hid_lo{tag}", [P, FT, S], F32R, at_big + 44 * K)
        gate_ready, hid_ready = {}, [None] * FT

        def convolve(f, channels, b, t, mark):
            u = 4 + f % 2
            r_mark = r_ready()
            m = dve.do(lambda e: e.tensor_tensor(scr[u][:, :], bank[b][:, :], r_bc[:, :], ALU.mult), mark, r_mark, scr_free[u])
            bank_free[b] = m
            yield
            scr_free[u] = yield from causal_conv(scr[t][:, :], scr[u][:, :], f"fconv_w{conv}", f"fconv_b{conv}", 3, 2 * FT, channels,
                                      m, scr_free[t])
            return scr_free[u]

        def gate(f, b, mark):
            t = f % 2
            if conv is None:
                m = act.do(lambda e: e.activation(scr[t][:, :], bank[b][:, :], ACT.Silu), mark, scr_free[t])
                bank_free[b] = m
            else:
                m = yield from convolve(f, f, b, t, mark)
                m = act.do(lambda e: e.activation(scr[t][:, :], scr[t][:, :], ACT.Silu), m)
            gate_ready[f] = m

        def value(f, b, mark):
            t, g = 2 + f % 2, f % 2
            if conv is None:
                m = dve.do(lambda e: e.tensor_tensor(scr[t][:, :], bank[b][:, :], scr[g][:, :], ALU.mult),
                           mark, gate_ready[f], scr_free[t])
                bank_free[b] = m
            else:
                m = yield from convolve(f, FT + f, b, t, mark)
                m = dve.do(lambda e: e.tensor_tensor(scr[t][:, :], scr[t][:, :], scr[g][:, :], ALU.mult), m, gate_ready[f])
            scr_free[g] = m
            yield
            hid_ready[f] = yield from split_tile(scr[t][:, :], hid_hi[:, f, :], hid_lo[:, f, :], m, before)
            scr_free[t] = hid_ready[f]

        for panel in range(FT // 2):
            gemm_fm(2, DT, h_hi, h_lo, h_ready, gate, 2 * panel,
                    beside=r_ready.beside() if r_ready and panel == 0 else iter(()))
            gemm_fm(2, DT, h_hi, h_lo, h_ready, value, 2 * panel)
        r_bc_free[0] = dve.last()
        gemm_fm(DT, FT, hid_hi, hid_lo, hid_ready, residual)

    start = Residual(1.0, False, "even_norm", at_once=True)
    for f in range(DT):
        if f in (0, 2, 4):
            split_unit()
        in_turn([start.scaled(f, x_landed[f])])
    dve.wait(params_in, small_in)
    act.wait(params_in, small_in)
    for f in range(DT):
        in_turn([start.summed(f, x_landed[f])])
    masks_ready = dve.do(lambda e: e.tensor_copy(masks[:, :], masks_f32[:, :]), masks_in)
    res = start
    for layer in range(DEPTH):
        o_hi, o_lo, o_ready, rest = attention_stage(res.h_ready, Inverse(res), layer == 1)
        res = Residual(1.0, False, f"ffn_norm{layer}", pe.last())
        gemm_fm(DT, DT, o_hi, o_lo, o_ready, res, beside=rest)
        h_ready, r_ready = res.h_ready, Inverse(res)
        res = Residual(1.0, False, None if layer == DEPTH - 1 else "odd_norm")
        ffn(h_ready, r_ready, layer, res, f"_{layer}")
    res.flush()
    x_ready = final_rms("final_norm", res.sums, pe.last())

    class RecurrentCore:

        def __init__(self, q, k, v, v_cols, weights_t, sm, out, first_marks, q_ready, k_ready, prepare):
            self.q, self.k, self.v, self.v_cols, self.weights_t, self.sm, self.out = q, k, v, v_cols, weights_t, sm, out
            self.first_marks, self.q_ready, self.k_ready, self.prepare = first_marks, q_ready, k_ready, prepare
            self.done, self.weighted, self.v_ready = [], {}, None

        def products(self, h, score_banks, prepare_banks):
            prepared = self.prepare(h, prepare_banks)
            q_h, k_h = self.q(h), self.k(h)
            for sb in range(TB):
                b, w = score_banks[sb % 2], (TB - sb) * P
                s = pe.do(lambda e: e.matmul(bank[b][:, 0:w], k_h[:, sb * P:(sb + 1) * P], q_h[:, sb * P:S],
                                             start=True, stop=True),
                          self.q_ready(h), self.k_ready(h), bank_free[b])
                bank_free[b] = self.weighted[h, sb] = dve.do(lambda e: e.scalar_tensor_tensor(
                    self.sm[h % 2][:, TRI[sb]:TRI[sb] + w], bank[b][:, 0:w], DK ** -0.5, self.weights_t(h, sb),
                    ALU.mult, ALU.mult), s, prepared, sm_free[h % 2], self.first_marks)
                if sb % 2:
                    yield
            weights_free[0] = bank_free[b]

        def outputs(self, h):
            sm = self.sm[h % 2]
            for tb in range(TB):
                b = 4 + tb
                for sb in range(tb + 1):
                    o = pe.do(lambda e: e.matmul(
                        bank[b][:, 0:self.v_cols], sm[:, TRI[sb] + (tb - sb) * P:TRI[sb] + (tb - sb + 1) * P],
                        self.v(sb, h), start=sb == 0, stop=sb == tb),
                        self.weighted[h, sb], self.v_ready, bank_free[b], signal=sb == tb)
                c = h * TB + tb
                row_ = self.out[:, tb, h * DV:(h + 1) * DV]
                cp = act.do(lambda e: e.activation(row_, bank[b][:, 0:DV], ACT.Copy), o, self.first_marks)
                bank_free[b] = cp
                if self.v_cols > DV:
                    bank_free[b] = act.do(lambda e: e.activation(stats[:, 48 + c:49 + c], bank[b][:, DV:DV + 1], ACT.Copy))
                six = stats[:, 224 + 6 * (c % 4):230 + 6 * (c % 4)]
                st = dve.do(lambda e: e.bn_stats(six, row_), cp, six_free[c % 4])
                st = six_free[c % 4] = dve.do(lambda e: e.bn_aggr(stats[:, 2 * c:2 * c + 2], six), st, self.first_marks)
                self.done += [st, bank_free[b]]
            sm_free[h % 2] = o

        def begin(self):
            add_swapped()
            yield
            for h in range(2):
                yield from self.products(h, (4, 5), (6, 7))

        def finish(self, v_ready):
            self.v_ready = v_ready
            for h in range(NH2):
                self.outputs(h)
                if h + 2 < NH2:
                    in_turn([self.products(h + 2, (0, 1), (2, 3))])
            return self.done

    sm_free, weights_free, six_free = [None, None], [None], [None] * 4
    mean_c = lambda c: stats[:, 2 * c:2 * c + 1]
    all_var = stats[:, 0:32].rearrange("p (c two) -> p c two", two=2)[:, :, 1]

    def normalise_heads(out, var_plus, *ready):
        if var_plus is None:
            m = act.do(lambda e: e.activation(stats[:, 32:48], all_var, ACT.Sqrt, bias=eps[:, 1:2]), *ready)
        else:
            m = dve.do(lambda e: e.tensor_tensor(stats[:, 32:48], all_var, var_plus, ALU.add), *ready)
            m = act.do(lambda e: e.activation(stats[:, 32:48], stats[:, 32:48], ACT.Sqrt), m)
        m = dve.do(lambda e: e.reciprocal(stats[:, 32:48], stats[:, 32:48]), m)
        for c in range(NH2 * TB):
            h, tb = c // TB, c % TB
            y = out[:, tb, h * DV:(h + 1) * DV]
            n = dve.do(lambda e, y=y, c=c: e.tensor_scalar(y, y, mean_c(c), stats[:, 32 + c:33 + c],
                                                           ALU.subtract, ALU.mult), m)
        return n

    for layer in range(DEPTH):
        L = str(layer)
        before = [pe.last(), act.last(), dve.last()]
        tm_ret = at("ret_tm" + L, [P, TB, D], F32, at_big)
        tm_ml = at("ml_tm" + L, [P, TB, D], F32, at_big + 16 * K)
        rq = at("rq" + L, [P, NH2, S], F32, at_big + 32 * K)
        rk = at("rk" + L, [P, NH2, S], F32, at_big + 40 * K)
        rv = at("rv" + L, [P, TB, D], F32, at_big + 48 * K)
        rope = at("rope2_" + L, [P, 2 * S], F32, at_big + 28 * K)
        sm_r = [at(f"sm_ret{i}_{L}", [P, TRI_N], F32, at_big + (16 + 5 * i) * K) for i in range(2)]
        decay = at("decay" + L, [P, NH2, S], F32, at_big + 80 * K)
        rope_in = table_loads.start(rope[:, :], table_ap("rope128"), before)
        decay_in = table_loads.start(decay[:, :, :], table_ap("decay"), before)

        class Split2:
            def __init__(self):
                mk = lambda d: Rope(d, DK // 2, rope[:, 0:S], rope[:, S:2 * S], 1.0, None, decay_in, before)
                self.q, self.k = mk(rq), mk(rk)

            def __call__(self, f, b, mark):
                return (self.q if f < NH2 else self.k)(f % NH2, b, mark)

        rot = Split2()
        gemm_fm(2 * NH2, DT, h_hi, h_lo, x_ready, rot)
        rv_ready = []

        def keep(dst, ready, width):
            def evacuate(t, panel, mark):
                for j in range(2):
                    d = dst[:, t, (2 * panel + j) * width:(2 * panel + j) * width + DV]
                    s_ = bank[t][:, j * DV:(j + 1) * DV]
                    if t % 2:
                        m = act.do(lambda e: e.activation(d, s_, ACT.Copy), mark, before2[0])
                    else:
                        m = dve.do(lambda e: e.tensor_copy(d, s_), mark, before2[0])
                bank_free[t] = m
                ready.append(m)
            return evacuate

        before2 = [before]
        retention = RecurrentCore(
            lambda h: rq[:, h, :], lambda h: rk[:, h, :], lambda sb, h: rv[:, sb, h * DV:(h + 1) * DV], DV,
            lambda h, sb: decay[:, h, 0:S - sb * P], sm_r, tm_ret, before,
            lambda h: rot.q.ready[h], lambda h: rot.k.ready[h], lambda h, banks: decay_in)
        gemm_tm(DT, h_hi, h_lo, x_ready, keep(rv, rv_ready, DV), retention.begin())
        ret_done = retention.finish(rv_ready)
        ret_normed = normalise_heads(tm_ret, None, ret_done)

        before = [pe.last(), act.last(), dve.last()]
        before2[0] = before
        mqk = at("mqk" + L, [P, DT, S], F32, at_big + 64 * K)
        mv = at("mv" + L, [P, TB, NH2 * (DV + 1)], F32, at_big + 32 * K)
        sm_m = [at(f"sm_ml{i}_{L}", [P, TRI_N], F32, at_big + 48 * K + 512 + 5 * K * i) for i in range(2)]
        gates_t = at("gates_t" + L, [P, TRI_N], F32, at_big + 58 * K + 512)
        row = [at(f"row{i}_{L}", [NH2, S], F32, at_big + (80 + 2 * i) * K) for i in range(4)]
        select = scr[5][0:NH2, :]
        select_in = table_loads.start(select, table_ap("select")[0:NH2, :], before, scr_free[5])
        mqk_ready = {}

        def to_mqk(f, b, mark):
            t = f % 2
            m = yield from causal_conv(scr[t][:, :], bank[b][:, :], "mconv_w" + L, "mconv_b" + L, 4, DT, f, mark, scr_free[t])
            bank_free[b] = m
            mqk_ready[f] = scr_free[t] = act.do(lambda e: e.activation(mqk[:, f, :], scr[t][:, :], ACT.Silu), m, before)

        GB = 7
        for kt in range(DT):
            g = pe.do(lambda e, kt=kt: e.matmul(bank[GB][0:36, :], p_("w_if" + L, kt * 36, 36), x[:, kt, :],
                                                start=kt == 0, stop=kt == DT - 1), bank_free[GB], x_ready[kt],
                      signal=kt == DT - 1)
        z, lf, a_row, big_f = row
        R = slice(0, NH2)
        tmp = scr[4][R, :]
        bi, bf = (par[R, PARAMS[n + L][0]:PARAMS[n + L][0] + 1] for n in ("b_i", "b_f"))
        i_m = act.do(lambda e: e.activation(a_row[R, :], bank[GB][R, :], ACT.Identity, bias=bi), g, before)
        z_m = act.do(lambda e: e.activation(z[R, :], bank[GB][32:36, :], ACT.Identity, bias=bf), g)
        bank_free[GB] = z_m
        m = dve.do(lambda e: e.scalar_tensor_tensor(tmp, z[R, :], -1.0, z[R, :], ALU.mult, ALU.min), z_m, scr_free[4])
        m = act.do(lambda e: e.activation(tmp, tmp, ACT.Exp), m)
        m = act.do(lambda e: e.activation(tmp, tmp, ACT.Ln, bias=ones[R, 0:1]), m)
        m = dve.do(lambda e: e.scalar_tensor_tensor(lf[R, :], z[R, :], 0.0, tmp, ALU.min, ALU.subtract), m)
        zero = dve.do(lambda e: e.memset(z[R, :], 0.0), m)
        m = dve.do(lambda e: e.tensor_tensor_scan(big_f[R, :], lf[R, :], z[R, :], 0.0, ALU.add, ALU.add), m, zero)
        m = dve.do(lambda e: e.tensor_tensor(a_row[R, :], a_row[R, :], big_f[R, :], ALU.subtract), m, i_m)
        a_m = m
        m = dve.do(lambda e: e.tensor_tensor_scan(lf[R, :], a_row[R, :], a_row[R, :], 0.0, ALU.max, ALU.max), m)
        mm = m
        m = dve.do(lambda e: e.tensor_scalar(lf[R, :], lf[R, :], -1.0, None, ALU.mult), mm)
        nm_m = m
        m = dve.do(lambda e: e.tensor_tensor(z[R, :], lf[R, :], big_f[R, :], ALU.subtract), m)
        gemm_fm(DT, DT, h_hi, h_lo, x_ready, to_mqk)
        for tb in range(TB):
            t1 = pe.do(lambda e, tb=tb: e.transpose(bank[6][:, tb * 4:tb * 4 + 4], a_row[R, tb * P:(tb + 1) * P],
                                                    ident[R, R]), a_m, bank_free[6])
        for tb in range(TB):
            t1 = pe.do(lambda e, tb=tb: e.transpose(bank[6][:, 16 + tb * 4:20 + tb * 4], z[R, tb * P:(tb + 1) * P],
                                                    ident[R, R]), m)
        a_cols = dve.do(lambda e: e.tensor_copy(stats[:, 64:80], bank[6][:, 0:16]), t1)
        floor_m = act.do(lambda e: e.activation(stats[:, 80:96].rearrange("p (h t) -> p t h", h=NH2),
                                                bank[6][:, 16:32].rearrange("p (t h) -> p t h", t=TB), ACT.Exp), a_cols)
        bank_free[6] = floor_m
        scr_free[4] = m

        def prepare(h, banks):
            out_ = []
            for b in banks:
                m = pe.do(lambda e, b=b: e.matmul(bank[b][:, :], select[:, h * P:(h + 1) * P], lf[R, :],
                                                  start=True, stop=b == banks[0]), nm_m, select_in, bank_free[b])
            m2 = pe.do(lambda e: e.matmul(bank[banks[1]][:, :], ident_bf, causal_t_bf, start=False, stop=True))
            for sb in range(TB):
                bias = stats[:, 64 + sb * NH2 + h:65 + sb * NH2 + h]
                c0, w = sb * P, (TB - sb - 1) * P
                g_ = act.do(lambda e, sb=sb, bias=bias, c0=c0: e.activation(
                    gates_t[:, TRI[sb]:TRI[sb] + P], bank[banks[1]][:, c0:c0 + P], ACT.Exp, bias=bias),
                    m2, a_cols, weights_free[0], before)
                if w:
                    g_ = act.do(lambda e, sb=sb, bias=bias, c0=c0, w=w: e.activation(
                        gates_t[:, TRI[sb] + P:TRI[sb] + P + w], bank[banks[0]][:, c0 + P:S], ACT.Exp, bias=bias))
            bank_free[banks[0]] = bank_free[banks[1]] = g_
            scr_free[5] = m2
            return g_

        mlstm = RecurrentCore(
            lambda h: mqk[:, h, :], lambda h: mqk[:, NH2 + h, :],
            lambda sb, h: mv[:, sb, h * (DV + 1):(h + 1) * (DV + 1)], DV + 1,
            lambda h, sb: gates_t[:, TRI[sb]:TRI[sb] + (TB - sb) * P], sm_m, tm_ml, [before, ret_normed],
            lambda h: mqk_ready[h], lambda h: mqk_ready[NH2 + h], prepare)
        mv_heads = mv[:, :, :].rearrange("p t (h c) -> p t h c", h=NH2)
        mv_ready = [dve.do(lambda e: e.memset(mv_heads[:, :, :, DV], 1.0), before)]
        gemm_tm(DT, h_hi, h_lo, x_ready, keep(mv, mv_ready, DV + 1), mlstm.begin())
        ml_done = mlstm.finish(mv_ready)
        den = stats[:, 48:64]
        m = dve.do(lambda e: e.scalar_tensor_tensor(stats[:, 96:112], den, -1.0, den, ALU.mult, ALU.max), ml_done)
        m = dve.do(lambda e: e.tensor_tensor(den, stats[:, 96:112], stats[:, 80:96], ALU.max), m, floor_m)
        m = dve.do(lambda e: e.scalar_tensor_tensor(stats[:, 96:112], den, 1e-5, den, ALU.mult, ALU.mult), m)
        ml_normed = normalise_heads(tm_ml, stats[:, 96:112], m)

        before = [pe.last(), act.last(), dve.last()]
        z_hi = at("z_hi" + L, [P, DT, S], F32R, at_big + 32 * K)
        z_lo = at("z_lo" + L, [P, DT, S], F32R, at_big + 48 * K)
        y_ret = at("y_ret" + L, [P, DT, S], F32, at_big + 64 * K)
        mix_hi = at("mix_hi" + L, [P, DT, S], F32R, at_big)
        mix_lo = at("mix_lo" + L, [P, DT, S], F32R, at_big + 16 * K)

        def gated(tm, func, gain, normed, z_free):
            ready = [None] * DT

            def evacuate(f, b, mark):
                t, g_, tb_ = f % 2, 2 + f % 2, 4 + f % 2
                gm = act.do(lambda e: e.activation(scr[g_][:, :], bank[b][:, :], func), mark, scr_free[g_])
                bank_free[b] = gm
                for i in range(TB):
                    tr = pe.do(lambda e, i=i: e.transpose(bank[tb_][:, i * P:(i + 1) * P], tm[:, i, f * P:(f + 1) * P],
                                                          ident[:, :]), normed, bank_free[tb_], signal=i == TB - 1)
                m = dve.do(lambda e: e.scalar_tensor_tensor(scr[t][:, :], bank[tb_][:, :], p_(gain + L, f), scr[g_][:, :],
                                                            ALU.mult, ALU.mult), gm, tr, scr_free[t])
                bank_free[tb_] = scr_free[g_] = m
                yield
                ready[f] = scr_free[t] = yield from split_tile(scr[t][:, :], z_hi[:, f, :], z_lo[:, f, :], m, z_free)
            return ready, evacuate

        z_ready, to_z = gated(tm_ret, ACT.Silu, "ret_g", ret_normed, before)
        gemm_fm(DT, DT, h_hi, h_lo, x_ready, to_z)
        gate_m, yr_ready, mix_ready = {}, {}, [None] * DT

        def merge_gate(which):
            def evacuate(f, b, mark):
                t = f % 2
                gate_m[f] = act.do(lambda e: e.activation(scr[t][:, :], bank[b][:, :], ACT.Sigmoid,
                                                          bias=p_("b_merge" + L, which * DT + f)), mark, scr_free[t])
                bank_free[b] = gate_m[f]
            return evacuate

        def gate_ret(f, b, mark):
            m = dve.do(lambda e: e.tensor_tensor(y_ret[:, f, :], bank[b][:, :], scr[f % 2][:, :], ALU.mult),
                       mark, gate_m[f], before)
            bank_free[b] = scr_free[f % 2] = yr_ready[f] = m

        def gate_ml(f, b, mark):
            t = 2 + f % 2
            m = dve.do(lambda e: e.tensor_tensor(scr[t][:, :], bank[b][:, :], scr[f % 2][:, :], ALU.mult),
                       mark, gate_m[f], scr_free[t])
            bank_free[b] = scr_free[f % 2] = m
            yield
            m = dve.do(lambda e: e.tensor_tensor(scr[t][:, :], scr[t][:, :], y_ret[:, f, :], ALU.add), m, yr_ready[f])
            yield
            mix_ready[f] = scr_free[t] = yield from split_tile(scr[t][:, :], mix_hi[:, f, :], mix_lo[:, f, :], m, tm_free)

        for panel in range(DT // 2):
            gemm_fm(2, DT, h_hi, h_lo, x_ready, merge_gate(0), 2 * panel)
            gemm_fm(2, DT, z_hi, z_lo, z_ready, gate_ret, 2 * panel)
        z_ready, to_z = gated(tm_ml, ACT.Sigmoid, "ml_g", ml_normed, pe.last())
        gemm_fm(DT, DT, h_hi, h_lo, x_ready, to_z)
        tm_free = pe.last()
        for panel in range(DT // 2):
            gemm_fm(2, DT, h_hi, h_lo, x_ready, merge_gate(1), 2 * panel)
            gemm_fm(2, DT, z_hi, z_lo, z_ready, gate_ml, 2 * panel)
        res = Residual(ALPHA, True)
        gemm_fm(DT, DT, mix_hi, mix_lo, mix_ready, res)
        res.flush()
        x_ready = layer_norm("ln1_g" + L, "ln1_b" + L, res, pe.last())
        res = Residual(ALPHA, True)
        ffn(x_ready, None, None, res, f"_{2 + layer}")
        res.flush()
        x_ready = layer_norm("ln2_g" + L, "ln2_b" + L, res, pe.last())

    stores = Loads(sp, sem("y_stored"))
    for f in range(DT):
        stored = stores.start(y_out[:, f, :], x[:, f, :], x_ready[f])
    sp.wait(stored)

    assert next_unit[0] == len(units)


def shape_tables():
    t = np.zeros((P, N_TABLES), np.float32)

    def put(name, a):
        t[:, TABLES[name][0]:sum(TABLES[name])] = a

    i, j = np.arange(P)[:, None], np.arange(P)[None, :]
    eye = np.eye(P, dtype=np.float32)
    neg = np.float32(-(2.0 ** 99))
    masks = [eye, np.where(j <= i, 0, neg)] + [np.where(i <= j, 0, neg)] * TB
    top = lambda a: (a.view(np.uint32) & np.uint32(0xFFFF0000)).view(np.float32)
    for kind in range(3):
        dist = P * kind + i - j
        count = np.where(dist >= 0, (dist <= 128).astype(int) + (dist % 4 == 0) + (dist % 16 == 0), 0)
        ln = np.where(count > 0, np.log(np.maximum(count, 1)), neg).astype(np.float32)
        a = top(ln.copy())
        b = top((ln - a).astype(np.float32))
        masks += [a, b, (ln - a - b).astype(np.float32)]
    put("masks", np.concatenate(masks, 1))
    put("ident", eye)
    put("ones", 1.0)
    put("eps", np.array([[1e-6, 1e-5]]))
    pos = np.arange(S, dtype=np.float32)

    def rope(inv, half):
        ang = (pos[None, :] * inv[:, None]).astype(np.float32).astype(np.float64)
        cos, sin = np.cos(ang), np.sin(ang)
        n = P // (2 * half)
        return np.concatenate([np.tile(cos, (2 * n, 1)), np.tile(np.concatenate([-sin, sin]), (n, 1))], 1)

    put("rope64", rope((1.0 / 10000.0 ** (np.arange(32, dtype=np.float32) * 2.0 / 64)).astype(np.float32), 32))
    put("rope128", rope((10000.0 ** (-np.arange(64, dtype=np.float32) / 64)).astype(np.float32), 64))
    rel = np.arange(S)[None, :] - np.arange(P)[:, None]
    lg = np.log(1.0 - 2.0 ** (-5.0 - np.arange(NH2)))
    put("decay", np.concatenate([np.where(rel >= 0, np.exp(g * np.maximum(rel, 0)), 0) for g in lg], 1))
    sel = np.zeros((P, NH2 * P))
    for h in range(NH2):
        sel[h, h * P:(h + 1) * P] = 1
    put("select", sel)
    return t


def kernel(**inputs):
    import concourse.bacc as _bacc
    from concourse.bass_utils import run_bass_kernel_spmd as _run

    a = {k: np.asarray(v) for k, v in inputs.items()}

    pieces = []
    for name, layer, k0, nk, c, w in weight_units():
        m = a[name][layer][k0 * P:(k0 + nk) * P, c:c + w]
        pieces.append(m.reshape(nk, P, w).transpose(1, 0, 2).reshape(-1))
    weights = np.concatenate(pieces)

    params = np.zeros((P, N_PARAMS), np.float32)

    def put(name, v):
        params[:, PARAMS[name][0]:sum(PARAMS[name])] = v

    tiles = lambda v: v.reshape(-1, P).T
    put("even_norm", tiles(a["even_norm"][0]))
    put("odd_norm", tiles(a["odd_norm"][0]))
    put("final_norm", tiles(a["final_norm"]))
    put("subln", tiles(a["odd_subln"][0]))
    put("lambdas", np.concatenate([a["odd_lambda_" + n][0] for n in ("q1", "k1", "q2", "k2")])[None, :])
    for l in range(2):
        L = str(l)
        put("ffn_norm" + L, tiles(a["ffn_norm"][l]))
        put("fconv_w" + L, tiles(a["ffn_conv_w"][l].reshape(-1)))
        put("fconv_b" + L, tiles(a["ffn_conv_b"][l]))
        w_if = np.zeros((D, 36), np.float32)
        w_if[:, 0:4] = a["w_in_2"][l][:, 6144:6148]
        w_if[:, 32:36] = a["w_in_2"][l][:, 6148:6152]
        put("w_if" + L, w_if.reshape(DT, P, 36).transpose(1, 0, 2).reshape(P, -1))
        params[0:4, PARAMS["b_i" + L][0]] = a["b_if_2"][l][0:4]
        params[0:4, PARAMS["b_f" + L][0]] = a["b_if_2"][l][4:8]
        put("b_merge" + L, tiles(a["b_merge_2"][l]))
        put("mconv_w" + L, tiles(a["conv_w_2"][l].reshape(-1)))
        put("mconv_b" + L, tiles(a["conv_b_2"][l]))
        for n, src in (("ret_g", "ret_norm_g_2"), ("ml_g", "mlstm_norm_g_2"), ("ln1_g", "ln1_g_2"), ("ln1_b", "ln1_b_2"),
                       ("ln2_g", "ln2_g_2"), ("ln2_b", "ln2_b_2")):
            put(n + L, tiles(a[src][l]))

    x_fm = np.ascontiguousarray(a["x"][0].T.reshape(DT, P, S).transpose(1, 0, 2))
    arrays = {"weights": weights, "params": params, "tables": shape_tables(), "x_fm": x_fm}

    nc = _bacc.Bacc("TRN2", target_bir_lowering=False, num_devices=1)
    args = [nc.dram_tensor(n, v.shape, F32, kind="ExternalInput").ap() for n, v in arrays.items()]
    out = nc.dram_tensor("y_fm", (P, DT, S), F32, kind="ExternalOutput").ap()
    build(nc, *args, out)
    r = _run(nc, [arrays], core_ids=[0])
    y = np.asarray(r.results[0]["y_fm"])
    return np.ascontiguousarray(y.transpose(2, 1, 0).reshape(1, S, D))
```
